# Optimizing a Trainium2 kernel written in Bass

```python
import jax, jax.numpy as jnp
from jax import lax
import numpy as np

D_MODEL = 1024
BATCH = 1
SEQ = 1024
DEPTH = 2
DEC_BATCH = 1
DEC_SEQ = 32
PAST_LEN = 512

CHUNK = 64
N_A_LAYERS = DEPTH // 2
N_B_LAYERS = DEPTH - N_A_LAYERS
HEAD_DIM = 128
N_HEADS_A = D_MODEL // HEAD_DIM
N_KV_A = 2
GROUP_A = N_HEADS_A // N_KV_A
D_ATT = N_HEADS_A * HEAD_DIM
N_IDX_HEADS = 8
IDX_DIM = 64
TOPK_MAX = 256
IDX_SCALE = (N_IDX_HEADS * IDX_DIM) ** -0.5
N_HEADS_B = D_MODEL // HEAD_DIM
D_ATT_B = N_HEADS_B * HEAD_DIM
D_FF = 4 * D_MODEL
BLOCK_Q = 128
ALPHA = (2.0 * DEPTH) ** 0.25
BETA = (8.0 * DEPTH) ** -0.25
LN_EPS = 1e-5
FORGET_BIAS_INIT = 2.0
A_IN = D_ATT + 2 * N_KV_A * HEAD_DIM + N_IDX_HEADS * IDX_DIM + IDX_DIM + N_IDX_HEADS
A_SPLITS = (D_ATT,
            D_ATT + N_KV_A * HEAD_DIM,
            D_ATT + 2 * N_KV_A * HEAD_DIM,
            D_ATT + 2 * N_KV_A * HEAD_DIM + N_IDX_HEADS * IDX_DIM,
            D_ATT + 2 * N_KV_A * HEAD_DIM + N_IDX_HEADS * IDX_DIM + IDX_DIM)
B_KV_IN = 2 * D_ATT_B + N_HEADS_B

kernel_name = "yoco_dsa_fox_streaming_step"

def _layernorm(x, g, b):
    xf = x.astype(jnp.float32)
    mu = jnp.mean(xf, axis=-1, keepdims=True)
    var = jnp.mean(jnp.square(xf - mu), axis=-1, keepdims=True)
    y = (xf - mu) * lax.rsqrt(var + LN_EPS) * g.astype(jnp.float32) + b.astype(jnp.float32)
    return y.astype(x.dtype)

def _sqrelu_mlp(x, w_up, w_down):
    return jnp.square(jax.nn.relu(x @ w_up)) @ w_down

def _alibi_slopes(n):
    return jnp.exp2(-8.0 * jnp.arange(1, n + 1, dtype=jnp.float32) / n)

def _split_q(a, nb):
    b, t = a.shape[0], a.shape[1]
    a = a.reshape((b, nb, t // nb) + a.shape[2:])
    return jnp.moveaxis(a, 1, 0)

def _merge_q(a):
    a = jnp.moveaxis(a, 0, 1)
    return a.reshape((a.shape[0], a.shape[1] * a.shape[2]) + a.shape[3:])

def _dsa_mixer(x, past_k, past_v, past_kidx, w_in, w_o):
    b, t, _ = x.shape
    p = past_k.shape[1]
    n_keys = p + t
    k_sel = min(TOPK_MAX, n_keys // 4)
    q, k, v, qi, ki, wi = jnp.split(x @ w_in, A_SPLITS, axis=-1)
    q = q.reshape(b, t, N_KV_A, GROUP_A, HEAD_DIM)
    k = k.reshape(b, t, N_KV_A, HEAD_DIM)
    v = v.reshape(b, t, N_KV_A, HEAD_DIM)
    qi = qi.reshape(b, t, N_IDX_HEADS, IDX_DIM)
    wi = wi.astype(jnp.float32) * IDX_SCALE
    k_all = jnp.concatenate([past_k.astype(k.dtype), k], axis=1)
    v_all = jnp.concatenate([past_v.astype(v.dtype), v], axis=1)
    ki_all = jnp.concatenate([past_kidx.astype(ki.dtype), ki], axis=1)
    slopes = _alibi_slopes(N_HEADS_A).reshape(N_KV_A, GROUP_A)
    key_pos = jnp.arange(n_keys, dtype=jnp.int32)
    q_pos = p + jnp.arange(t, dtype=jnp.int32)
    q_lim = (q_pos // CHUNK + 1) * CHUNK
    qb = CHUNK if t % CHUNK == 0 else t
    nb = t // qb

    def block(args):
        q_b, qi_b, wi_b, pos_b, lim_b = args
        rel = jax.nn.relu(jnp.einsum('bqhd,bsd->bqhs', qi_b, ki_all).astype(jnp.float32))
        score = jnp.einsum('bqh,bqhs->bqs', wi_b, rel)
        adm = key_pos[None, :] < lim_b[:, None]
        score = jnp.where(adm[None], score, -jnp.inf)
        _, sel = lax.top_k(score, k_sel)
        valid = sel < lim_b[None, :, None]
        k_g = jax.vmap(lambda kk, ii: kk[ii])(k_all, sel)
        v_g = jax.vmap(lambda vv, ii: vv[ii])(v_all, sel)
        logits = jnp.einsum('bqngd,bqknd->bqngk', q_b, k_g).astype(jnp.float32) * HEAD_DIM ** -0.5
        dist = jnp.abs(pos_b[None, :, None] - sel).astype(jnp.float32)
        logits = logits - slopes[None, None, :, :, None] * dist[:, :, None, None, :]
        logits = jnp.where(valid[:, :, None, None, :], logits, -jnp.inf)
        probs = jax.nn.softmax(logits, axis=-1).astype(v_g.dtype)
        return jnp.einsum('bqngk,bqknd->bqngd', probs, v_g)

    out = lax.map(block, (_split_q(q, nb), _split_q(qi, nb), _split_q(wi, nb),
                          q_pos.reshape(nb, qb), q_lim.reshape(nb, qb)))
    out = _merge_q(out).reshape(b, t, D_ATT)
    return out @ w_o, k, v, ki

def _fox_shared_kv(x, w_kv, b_f):
    b, t, _ = x.shape
    k, v, f = jnp.split(x @ w_kv, (D_ATT_B, 2 * D_ATT_B), axis=-1)
    log_f = jax.nn.log_sigmoid(f.astype(jnp.float32) + b_f.astype(jnp.float32))
    return (k.reshape(b, t, N_HEADS_B, HEAD_DIM), v.reshape(b, t, N_HEADS_B, HEAD_DIM), log_f)

def _fox_mixer(x, k_all, v_all, c_all, w_q, w_o):
    b, t, _ = x.shape
    n_keys = k_all.shape[1]
    p = n_keys - t
    q = (x @ w_q).reshape(b, t, N_HEADS_B, HEAD_DIM)
    c_keys = jnp.swapaxes(c_all, 1, 2)
    c_q = c_all[:, p:, :]
    key_pos = jnp.arange(n_keys, dtype=jnp.int32)
    q_pos = p + jnp.arange(t, dtype=jnp.int32)
    qb = BLOCK_Q if t % BLOCK_Q == 0 else t
    nb = t // qb

    def block(args):
        q_b, cq_b, pos_b = args
        logits = jnp.einsum('bqhd,bshd->bhqs', q_b, k_all).astype(jnp.float32) * HEAD_DIM ** -0.5
        logits = logits + jnp.swapaxes(cq_b, 1, 2)[..., None] - c_keys[:, :, None, :]
        causal = key_pos[None, :] <= pos_b[:, None]
        logits = jnp.where(causal[None, None], logits, -jnp.inf)
        probs = jax.nn.softmax(logits, axis=-1).astype(v_all.dtype)
        return jnp.einsum('bhqs,bshd->bqhd', probs, v_all)

    out = lax.map(block, (_split_q(q, nb), _split_q(c_q, nb), q_pos.reshape(nb, qb)))
    return _merge_q(out).reshape(b, t, D_ATT_B) @ w_o

def _trunk(x, past_a_k, past_a_v, past_a_kidx, past_b_k, past_b_v, past_b_logf,
           w_a_in, w_a_o, w_b_kv, b_b_f, w_b_q, w_b_o, w_up, w_down, ln_g, ln_b):
    new_a_k, new_a_v, new_a_kidx = [], [], []
    for layer in range(DEPTH):
        if layer < N_A_LAYERS:
            h, k, v, ki = _dsa_mixer(x, past_a_k[layer], past_a_v[layer], past_a_kidx[layer],
                                     w_a_in[layer], w_a_o[layer])
            new_a_k.append(k)
            new_a_v.append(v)
            new_a_kidx.append(ki)
        else:
            if layer == N_A_LAYERS:
                b_k, b_v, b_logf = _fox_shared_kv(x, w_b_kv, b_b_f)
                k_all = jnp.concatenate([past_b_k.astype(b_k.dtype), b_k], axis=1)
                v_all = jnp.concatenate([past_b_v.astype(b_v.dtype), b_v], axis=1)
                c_all = jnp.cumsum(jnp.concatenate([past_b_logf.astype(jnp.float32), b_logf], axis=1), axis=1)
            j = layer - N_A_LAYERS
            h = _fox_mixer(x, k_all, v_all, c_all, w_b_q[j], w_b_o[j])
        x = _layernorm(ALPHA * x + h, ln_g[layer, 0], ln_b[layer, 0])
        x = _layernorm(ALPHA * x + _sqrelu_mlp(x, w_up[layer], w_down[layer]), ln_g[layer, 1], ln_b[layer, 1])
    return (x, jnp.stack(new_a_k), jnp.stack(new_a_v), jnp.stack(new_a_kidx), b_k, b_v, b_logf)

def setup_inputs(seed: int = 0) -> dict:
    key = jax.random.key(seed)
    ks = jax.random.split(key, 20)

    def nrm(k, shape, s):
        return jax.random.normal(k, shape, jnp.float32) * s

    v0, v1 = A_SPLITS[1], A_SPLITS[2]
    a_col_scale = jnp.ones((A_IN,), jnp.float32).at[v0:v1].set(BETA)
    b_col_scale = jnp.concatenate([jnp.ones((D_ATT_B,), jnp.float32),
                                   jnp.full((D_ATT_B,), BETA, jnp.float32),
                                   jnp.full((N_HEADS_B,), 0.5, jnp.float32)])
    inputs = {}
    inputs['x_prompt'] = nrm(ks[0], (BATCH, SEQ, D_MODEL), 1.0)
    inputs['x_sample'] = nrm(ks[1], (DEC_BATCH, DEC_SEQ, D_MODEL), 1.0)
    inputs['cache_a_k'] = nrm(ks[2], (N_A_LAYERS, DEC_BATCH, PAST_LEN, N_KV_A, HEAD_DIM), 1.0)
    inputs['cache_a_v'] = nrm(ks[3], (N_A_LAYERS, DEC_BATCH, PAST_LEN, N_KV_A, HEAD_DIM), BETA)
    inputs['cache_a_kidx'] = nrm(ks[4], (N_A_LAYERS, DEC_BATCH, PAST_LEN, IDX_DIM), 1.0)
    inputs['cache_b_k'] = nrm(ks[5], (DEC_BATCH, PAST_LEN, N_HEADS_B, HEAD_DIM), 1.0)
    inputs['cache_b_v'] = nrm(ks[6], (DEC_BATCH, PAST_LEN, N_HEADS_B, HEAD_DIM), BETA)
    inputs['cache_b_logf'] = jax.nn.log_sigmoid(FORGET_BIAS_INIT + nrm(ks[7], (DEC_BATCH, PAST_LEN, N_HEADS_B), 0.5))
    inputs['w_a_in'] = nrm(ks[8], (N_A_LAYERS, D_MODEL, A_IN), D_MODEL ** -0.5) * a_col_scale
    inputs['w_a_o'] = nrm(ks[9], (N_A_LAYERS, D_ATT, D_MODEL), BETA * D_ATT ** -0.5)
    inputs['w_b_kv'] = nrm(ks[10], (D_MODEL, B_KV_IN), D_MODEL ** -0.5) * b_col_scale
    inputs['b_b_f'] = FORGET_BIAS_INIT + nrm(ks[11], (N_HEADS_B,), 0.5)
    inputs['w_b_q'] = nrm(ks[12], (N_B_LAYERS, D_MODEL, D_ATT_B), D_MODEL ** -0.5)
    inputs['w_b_o'] = nrm(ks[13], (N_B_LAYERS, D_ATT_B, D_MODEL), BETA * D_ATT_B ** -0.5)
    inputs['w_up'] = nrm(ks[14], (DEPTH, D_MODEL, D_FF), D_MODEL ** -0.5)
    inputs['w_down'] = nrm(ks[15], (DEPTH, D_FF, D_MODEL), BETA * D_FF ** -0.5)
    inputs['ln_g'] = 1.0 + nrm(ks[16], (DEPTH, 2, D_MODEL), 0.02)
    inputs['ln_b'] = nrm(ks[17], (DEPTH, 2, D_MODEL), 0.02)
    return inputs

def reference(x_prompt, x_sample, cache_a_k, cache_a_v, cache_a_kidx, cache_b_k, cache_b_v, cache_b_logf,
              w_a_in, w_a_o, w_b_kv, b_b_f, w_b_q, w_b_o, w_up, w_down, ln_g, ln_b):
    bp, dt = x_prompt.shape[0], x_prompt.dtype
    empty_a_k = jnp.zeros((N_A_LAYERS, bp, 0, N_KV_A, HEAD_DIM), dt)
    empty_a_kidx = jnp.zeros((N_A_LAYERS, bp, 0, IDX_DIM), dt)
    empty_b_k = jnp.zeros((bp, 0, N_HEADS_B, HEAD_DIM), dt)
    empty_b_logf = jnp.zeros((bp, 0, N_HEADS_B), jnp.float32)
    (y_prompt, pa_k, pa_v, pa_kidx, pb_k, pb_v, pb_logf) = _trunk(
        x_prompt, empty_a_k, empty_a_k, empty_a_kidx, empty_b_k, empty_b_k, empty_b_logf,
        w_a_in, w_a_o, w_b_kv, b_b_f, w_b_q, w_b_o, w_up, w_down, ln_g, ln_b)
    (y_sample, sa_k, sa_v, sa_kidx, sb_k, sb_v, sb_logf) = _trunk(
        x_sample, cache_a_k, cache_a_v, cache_a_kidx, cache_b_k, cache_b_v, cache_b_logf,
        w_a_in, w_a_o, w_b_kv, b_b_f, w_b_q, w_b_o, w_up, w_down, ln_g, ln_b)
    return (y_prompt, y_sample, pa_k, pa_v, pa_kidx, pb_k, pb_v, pb_logf,
            sa_k, sa_v, sa_kidx, sb_k, sb_v, sb_logf)


_drawn_inputs = setup_inputs


def setup_inputs(seed=0):
    import zlib

    import numpy as np

    out = dict(_drawn_inputs(seed))
    spreads = {}
    factors = {'cache_a_k': 2.667, 'cache_b_k': 3.385, 'cache_b_logf': 8.0}
    for name, (base, spread) in spreads.items():
        noise = np.random.default_rng([zlib.crc32(name.encode()), seed]).standard_normal(out[name].shape)
        drawn = base * np.exp(spread * noise) if base else spread * noise
        out[name] = __import__('jax').numpy.asarray(drawn.astype(out[name].dtype))
    for name, factor in factors.items():
        out[name] = (out[name] * factor).astype(out[name].dtype)
    return out
```

```python
from contextlib import ExitStack

import numpy as np

import concourse.bass as bass
from concourse import mybir

F32 = mybir.dt.float32
F32R = mybir.dt.float32r
ALU = mybir.AluOpType
ACT = mybir.ActivationFunctionType
AX_X = mybir.AxisListType.X

P = 128
D = 1024
KT = D // P
SEQ, NEW, PAST = 1024, 32, 512
TOK = SEQ + NEW
NG = 3
G = TOK // NG
TT = SEQ // P + 1
ST = TT - 1
HEADS, HD = 8, 128
N_KV = 2
IDX_H, IDX_D = 8, 64
CHUNK = 64
D_FF = 4 * D
KEYS = SEQ + PAST + NEW
S0 = SEQ
SN = SEQ + PAST
TOPK = 256
TOPK_STREAM = min(TOPK, (PAST + NEW) // 4)
IDX_SCALE = (IDX_H * IDX_D) ** -0.5
SCALE = HD ** -0.5
ALPHA = 4.0 ** 0.25
LN_EPS = 1e-5
BIG = 1e30
TAKEN = -3.0e38
BARRED = -3.2e38
A_Q, A_K, A_V, A_QI, A_KI = 0, 8, 10, 12, 16


def rows_of(t):
    return NEW if t == ST else P


def width_of(t):
    return PAST + NEW if t == ST else P * (t + 1)


def key0_of(t):
    return S0 if t == ST else 0


def wait_apart(engine, sem, value, passed):
    engine.wait_ge(sem, value)
    engine.sem_inc(passed, 1)


class Counted:

    def __init__(self, sem):
        self.sem, self.n = sem, 0

    def up(self, instruction):
        self.n += 1
        instruction.then_inc(self.sem, 1)
        return self.n


def in_pairs(engine, first, count, step):
    if count >= 4:
        with engine.Fori(first // 2, (first + count) // 2) as pair:
            for s in range(2):
                step(pair * 2 + s, s)
    elif count >= 2:
        for n in range(first, first + count // 2 * 2):
            step(n, n % 2)
    if count % 2:
        step(first + count - 1, 0)


class Phase:

    raised = []

    def __init__(self, nc, name):
        self.nc, self.name, self.ctx = nc, name, ExitStack()

    def __enter__(self):
        return self

    def __exit__(self, *e):
        return self.ctx.__exit__(*e)

    def sb(self, name, shape, dt=F32):
        return self.ctx.enter_context(self.nc.sbuf_tensor(f"{self.name}_{name}", shape, dt))

    def ps(self, name, shape):
        return self.ctx.enter_context(self.nc.psum_tensor(f"{self.name}_{name}", shape, F32))

    def sem(self, name):
        handle = self.nc.alloc_semaphore(f"{self.name}_{name}")
        self.raised.append(handle)
        return handle

    def block(self):
        return self.ctx.enter_context(self.nc.Block())


def clear_semaphores(nc):
    nc.clear_and_free_semaphores(list(Phase.raised))
    Phase.raised.clear()
    nc.all_engine_barrier()


def make_identity(nc, ident):
    with Phase(nc, "ident") as ph:
        zeroed = ph.sem("zeroed")
        block = ph.block()

        @block.gpsimd
        def _(pool):
            nc.gpsimd.memset(ident[:], 0.0).then_inc(zeroed, 1)
            pool.wait_ge(zeroed, 1)
            nc.gpsimd.affine_select(out=ident[:], in_=ident[:], compare_op=ALU.not_equal, fill=1.0, base=0,
                                    pattern=[[-1, P]], channel_multiplier=1).then_inc(zeroed, 1)
            pool.wait_ge(zeroed, 2)


def refill(nc, name, ident, xh, xl, source, residual=None, y=None, gain=None, shift=None, keep=None, last=False):
    with Phase(nc, name) as ph:
        rin = [ph.sem(f"rows_in{s}") for s in range(2)]
        kept = [ph.sem(f"rows_kept{s}") for s in range(2)]
        turned, high, low = ph.sem("turned"), ph.sem("high"), ph.sem("low")
        back = ph.ps("back", [P, 2, 2, 512])
        norm = source == "norm"
        if source != "sbuf":
            rows = ph.sb("rows", [P, 2, D])
        if norm:
            fed, centred, scaled, shifted = (ph.sem(n) for n in ("fed", "centred", "scaled", "shifted"))
            params, vec, root = ph.sem("params"), ph.sem("vec"), ph.sem("root")
            up = ph.ps("up", [P, 2, 2, 512])
            summed = ph.sb("summed", [P, 2, D])
            cent = ph.sb("cent", [P, 2, D])
            done = ph.sb("done", [P, 2, D])
            gains = ph.sb("gains", [P, D])
            shifts = ph.sb("shifts", [P, D])
            stats = ph.sb("stats", [P, 2, 2, 6])
            mv = ph.sb("mv", [P, 2, 2])
            small = ph.sb("small", [P, 2, 3])
        src = {"rows": lambda t: rows[:, t % 2], "sbuf": lambda t: y[:, t, :], "norm": lambda t: done[:, t % 2]}[source]
        block = ph.block()

        @block.sync
        def _(sp):
            if norm:
                sp.dma_start(gains[:], gain.partition_broadcast(P)).then_inc(params, 16)
                sp.dma_start(shifts[:], shift.partition_broadcast(P)).then_inc(params, 16)
            if source != "sbuf":
                for t in range(TT):
                    if t >= 2:
                        sp.wait_ge(vec if norm else turned, 1 + 6 * (t - 2) if norm else t - 1)
                    sp.dma_start(rows[:rows_of(t), t % 2], residual(t)).then_inc(rin[t % 2], 16)

        if norm:
            @block.gpsimd
            def _(pool):
                pool.wait_ge(params, 32)
                for t in range(TT):
                    r = rows_of(t)
                    pool.wait_ge(scaled, t + 1)
                    if t >= 2:
                        pool.wait_ge(kept[t % 2], 16 * (t // 2))
                        if not last:
                            pool.wait_ge(turned, t - 1)
                    nc.gpsimd.tensor_tensor(done[:r, t % 2], summed[:r, t % 2], shifts[:r], ALU.add).then_inc(shifted, 1)
                    pool.wait_ge(shifted, t + 1)
                    pool.dma_start(keep(t), done[:r, t % 2]).then_inc(kept[t % 2], 16)
                for s in range(2):
                    pool.wait_ge(kept[s], 16 * ((TT + 1 - s) // 2))

        @block.tensor
        def _(pe):
            def feed(t):
                r = rows_of(t)
                if t >= 2:
                    pe.wait_ge(vec, 1 + 6 * (t - 2))
                for j in range(KT):
                    mm = nc.tensor.transpose(up[:r, t % 2, j // 4, j % 4 * P:(j % 4 + 1) * P],
                                             y[:, j, t * P:t * P + r], ident[:])
                mm.then_inc(fed, 1)

            def turn(t):
                r = rows_of(t)
                if norm:
                    pe.wait_ge(shifted, t + 1)
                elif source == "rows":
                    pe.wait_ge(rin[t % 2], 16 * (t // 2 + 1))
                if t >= 2:
                    pe.wait_ge(low, t - 1)
                for j in range(KT):
                    mm = nc.tensor.transpose(back[:, t % 2, j // 4, j % 4 * P:j % 4 * P + r],
                                             src(t)[:r, j * P:(j + 1) * P], ident[:r, :r])
                mm.then_inc(turned, 1)

            for t in range(TT + 1):
                if norm and t < TT:
                    feed(t)
                if not last and t >= 1:
                    turn(t - 1)

        def fm(x, t):
            r = rows_of(t)
            return x[:, :, t * P:t * P + r].rearrange("p (a b) n -> p a b n", a=2)

        def bank(t):
            r = rows_of(t)
            return back[:, t % 2].rearrange("p a (b n) -> p a b n", n=P)[:, :, :, :r]

        @block.scalar
        def _(act):
            for t in range(TT + 1):
                if norm and t < TT:
                    r, s = rows_of(t), t % 2
                    act.wait_ge(centred, 2 * t + 1)
                    nc.scalar.activation(small[:r, s, 1:2], small[:r, s, 0:1], ACT.Sqrt).then_inc(root, 1)
                    act.wait_ge(centred, 2 * t + 2)
                    nc.scalar.mul(summed[:r, s], cent[:r, s], small[:r, s, 2:3]).then_inc(scaled, 1)
                if not last and t >= 1:
                    act.wait_ge(turned, t)
                    nc.scalar.copy(fm(xh, t - 1), bank(t - 1)).then_inc(high, 1)

        @block.vector
        def _(dve):
            for t in range(TT + 1):
                if norm and t < TT:
                    r, s = rows_of(t), t % 2
                    dve.wait_ge(fed, t + 1)
                    dve.wait_ge(rin[s], 16 * (t // 2 + 1))
                    if t >= 2:
                        dve.wait_ge(shifted, t - 1)
                    nc.vector.scalar_tensor_tensor(out=summed[:r, s], in0=rows[:r, s], scalar=ALPHA,
                                                   in1=up[:r, s].rearrange("p a b -> p (a b)"), op0=ALU.mult,
                                                   op1=ALU.add).then_inc(vec, 1)
                    dve.wait_ge(vec, 6 * t + 1)
                    for c in range(2):
                        nc.vector.bn_stats(stats[:r, s, c], summed[:r, s, c * 512:(c + 1) * 512]).then_inc(vec, 1)
                    dve.wait_ge(vec, 6 * t + 3)
                    nc.vector.bn_aggr(mv[:r, s], stats[:r, s].rearrange("p a b -> p (a b)")).then_inc(vec, 1)
                    dve.wait_ge(vec, 6 * t + 4)
                    nc.vector.tensor_scalar_add(small[:r, s, 0:1], mv[:r, s, 1:2], LN_EPS).then_inc(centred, 1)
                    if t == 0:
                        dve.wait_ge(params, 32)
                    if t >= 2:
                        dve.wait_ge(scaled, t - 1)
                    nc.vector.scalar_tensor_tensor(out=cent[:r, s], in0=summed[:r, s], scalar=mv[:r, s, 0:1],
                                                   in1=gains[:r], op0=ALU.subtract, op1=ALU.mult).then_inc(vec, 1)
                    dve.wait_ge(root, t + 1)
                    nc.vector.reciprocal(small[:r, s, 2:3], small[:r, s, 1:2]).then_inc(vec, 1)
                    dve.wait_ge(vec, 6 * t + 6)
                    dve.sem_inc(centred, 1)
                if not last and t >= 1:
                    dve.wait_ge(high, t)
                    nc.vector.tensor_tensor(fm(xl, t - 1), bank(t - 1), fm(xh, t - 1).bitcast(F32),
                                            ALU.subtract).then_inc(low, 1)


def weight_slots(ph):
    raw = ph.sb("raw", [P, 2, D])
    wh = ph.sb("wh", [P, 2, D], F32R)
    wl = ph.sb("wl", [P, 2, D], F32R)
    return raw, wh, wl, [ph.sem(f"weights_in{s}") for s in range(2)], ph.sem("weights_high"), ph.sem("weights_low")


def project(nc, name, xh, xl, weights, ident=None, blocks=KT, last_cols=P, y=None, fm=None, turns=None):
    wv = weights.rearrange("(k p) n -> p k n", p=P)
    with Phase(nc, name) as ph:
        raw, wh, wl, win, high, low = weight_slots(ph)
        multiplied, taken = ph.sem("multiplied"), ph.sem("taken")
        acc = ph.ps("acc", [P, 2, NG, 512])
        if y is None:
            stage = ph.sb("stage", [P, 2, TOK])
            stored = [ph.sem(f"stored{s}") for s in range(2)]
            group, staged = ph.sem("group"), ph.sem("staged")
            turned, rowed, passed = ph.sem("turned"), ph.sem("rowed"), ph.sem("passed")
            tstage = ph.sb("tstage", [P, 2, TT, P])
            tstored = [ph.sem(f"tstored{s}") for s in range(2)]
            tb = ph.ps("tb", [P, 2, 512])
        segments, at, so_far = [], 0, 0
        for first, count, stores in turns or []:
            if first > at:
                segments.append((at, first - at, None, 0))
            segments.append((first, count, stores, so_far - first))
            at, so_far = first + count, so_far + count
        if at < blocks:
            segments.append((at, blocks - at, None, 0))

        block = ph.block()

        def load(sp, n, s):
            sp.wait_ge(low, n + 1)
            if isinstance(n, int) and n == blocks - 1 and last_cols < P:
                sp.dma_start(raw[:, s].rearrange("p (k n) -> p k n", k=KT)[:, :, 0:last_cols],
                             wv[:, :, n * P:n * P + last_cols]).then_inc(win[s], 16)
            else:
                sp.dma_start(raw[:, s].rearrange("p (k n) -> p k n", k=KT),
                             wv[:, :, bass.ds(n * P, P)]).then_inc(win[s], 16)

        @block.sync
        def _(sp):
            if y is not None:
                in_pairs(sp, 0, blocks, lambda n, s: load(sp, n, s))
                return
            load(sp, 0, 0)
            load(sp, 1, 1)
            whole = blocks - (last_cols < P)
            row_stores = [0, 0]
            for first, count, stores, m_less_n in segments:
                def step(n, s):
                    sp.wait_ge(taken, n + 3)
                    sp.dma_start(fm[bass.ds(n * P, P), 0:SEQ], stage[:, s, 0:SEQ]).then_inc(stored[s], 16)
                    sp.dma_start(fm[bass.ds(n * P, P), SN:KEYS], stage[:, s, SEQ:TOK]).then_inc(stored[s], 16)
                    if not isinstance(n, int) or n + 2 < blocks:
                        load(sp, n + 2, s)
                    if stores:
                        m = n + m_less_n
                        ms = m % 2 if isinstance(m, int) else s
                        wait_apart(sp, rowed, m * 3 + 4, passed)
                        for out, part in stores(n):
                            row_stores[ms] += 16
                            sp.dma_start(out, part(tstage[:, ms])).then_inc(tstored[ms], 16)

                regular = min(count, max(0, whole - 2 - first)) // 2 * 2
                before = list(row_stores)
                in_pairs(sp, first, regular, step)
                if regular >= 4:
                    row_stores[:] = [b + (r - b) * (regular // 2) for b, r in zip(before, row_stores)]
                for n in range(first + regular, first + count):
                    step(n, n % 2)
            for s in range(2):
                sp.wait_ge(stored[s], 32 + 32 * ((blocks + 1 - s) // 2))
                if row_stores[s]:
                    sp.wait_ge(tstored[s], 32 + row_stores[s])

        @block.scalar
        def _(act):
            def split_high(n, s):
                act.wait_ge(win[s], n // 2 * 16 + 16 if isinstance(n, int) else (n - s) * 8 + 16)
                act.wait_ge(multiplied, n + 1)
                nc.scalar.copy(wh[:, s], raw[:, s]).then_inc(high, 1)

            in_pairs(act, 0, blocks, split_high)

        @block.gpsimd
        def _(pool):
            pool.sem_inc(low, 2)

            def split_low(n, s):
                pool.wait_ge(high, n + 1)
                nc.gpsimd.tensor_tensor(wl[:, s], raw[:, s], wh[:, s].bitcast(F32), ALU.subtract).then_inc(low, 1)

            in_pairs(pool, 0, blocks, split_low)

        @block.tensor
        def _(pe):
            pe.sem_inc(multiplied, 2)

            def multiply(n, s):
                pe.wait_ge(low, n + 3)
                pe.wait_ge(taken, n + 1)
                for g in range(NG):
                    for k in range(KT):
                        for part, (w, x) in enumerate(((wh, xh), (wh, xl), (wl, xh))):
                            mm = nc.tensor.matmul(acc[:, s, g, 0:G], w[:, s, k * P:(k + 1) * P],
                                                  x[:, k, g * G:(g + 1) * G], start=k == 0 and part == 0,
                                                  stop=k == KT - 1 and part == 2)
                    if g < NG - 1 and y is None:
                        mm.then_inc(group, 1)
                mm.then_inc(multiplied, 1)

            def turn(n, s, m):
                for t in range(TT):
                    if t == 0:
                        pe.wait_ge(staged, n * 2 + 2)
                        pe.wait_ge(rowed, m * 3 + 1)
                    if t == 5:
                        pe.wait_ge(taken, n + 3)
                    if t == ST:
                        pe.wait_ge(rowed, m * 3 + 2)
                    r = rows_of(t)
                    mm = nc.tensor.transpose(tb[:r, t // 4 % 2, t % 4 * P:(t % 4 + 1) * P],
                                             stage[:, s, t * P:t * P + r], ident[:])
                    if t in (3, 7, 8):
                        mm.then_inc(turned, 1)

            for first, count, stores, m_less_n in segments:
                def step(n, s):
                    multiply(n, s)
                    if stores:
                        turn(n, s, n + m_less_n)
                in_pairs(pe, first, count, step)

        @block.vector
        def _(dve):
            dve.sem_inc(taken, 2)
            if y is not None:
                def take(n, s):
                    dve.wait_ge(multiplied, n + 3)
                    nc.vector.tensor_copy(y[:, bass.ds(n, 1), :].rearrange("p a (g n) -> p (a g) n", g=NG),
                                          acc[:, s, :, 0:G]).then_inc(taken, 1)
                in_pairs(dve, 0, blocks, take)
                return
            dve.sem_inc(rowed, 1)
            for s in range(2):
                dve.sem_inc(stored[s], 32)
                dve.sem_inc(tstored[s], 32)

            for first, count, stores, m_less_n in segments:
                def step(n, s):
                    m = n + m_less_n
                    dve.wait_ge(stored[s], n // 2 * 32 + 32 if isinstance(n, int) else (n - s) * 16 + 32)
                    for g in range(NG):
                        if g < NG - 1:
                            dve.wait_ge(group, n * 2 + g + 1)
                        else:
                            dve.wait_ge(multiplied, n + 3)
                        nc.vector.tensor_copy(stage[:, s, g * G:(g + 1) * G], acc[:, s, g, 0:G]
                                              ).then_inc(staged if g < NG - 1 else taken, 1)
                    if stores:
                        ms = m % 2 if isinstance(m, int) else s
                        dve.wait_ge(tstored[ms], m // 2 * 32 + 32 if isinstance(m, int) else (m - ms) * 16 + 32)
                        for i, (a, b) in enumerate(((0, 4), (4, 8), (8, 9))):
                            dve.wait_ge(turned, m * 3 + i + 1)
                            r = rows_of(a)
                            nc.vector.tensor_copy(tstage[:r, ms, a:b, :],
                                                  tb[:r, i % 2, 0:(b - a) * P].rearrange("p (a n) -> p a n", n=P)
                                                  ).then_inc(rowed, 1)
                in_pairs(dve, first, count, step)


def turn_caches(nc, ident, jobs):
    with Phase(nc, "caches") as ph:
        cin, stored = ph.sem("rows_in"), [ph.sem(f"stored{s}") for s in range(2)]
        turned, copied = ph.sem("turned"), ph.sem("copied")
        tiles = [ph.sb(f"rows{j}", [P, PAST // P, rows.shape[1] * rows.shape[2]]) for j, (rows, _, _) in enumerate(jobs)]
        stage = ph.sb("stage", [P, 2, PAST])
        bank = ph.ps("bank", [P, 2, 512])
        heads = [(j, h, rows.shape[2], fm, row0 + h * rows.shape[2])
                 for j, (rows, fm, row0) in enumerate(jobs) for h in range(rows.shape[1])]
        block = ph.block()

        @block.sync
        def _(sp):
            for j, (rows, _, _) in enumerate(jobs):
                sp.dma_start(tiles[j][:], rows.rearrange("(t p) h d -> p t (h d)", p=P)).then_inc(cin, 16)
            for n, (j, h, w, fm, row) in enumerate(heads):
                sp.wait_ge(copied, n + 1)
                sp.dma_start(fm[row:row + w, S0:SN], stage[:w, n % 2]).then_inc(stored[n % 2], 16)
            for s in range(2):
                sp.wait_ge(stored[s], 16 * ((len(heads) + 1 - s) // 2))

        @block.tensor
        def _(pe):
            pe.wait_ge(cin, 16 * len(jobs))
            for n, (j, h, w, _, _) in enumerate(heads):
                if n >= 2:
                    pe.wait_ge(copied, n - 1)
                for t in range(PAST // P):
                    mm = nc.tensor.transpose(bank[:w, n % 2, t * P:(t + 1) * P], tiles[j][:, t, h * w:(h + 1) * w],
                                             ident[:])
                mm.then_inc(turned, 1)

        @block.scalar
        def _(act):
            for n, (j, h, w, _, _) in enumerate(heads):
                act.wait_ge(turned, n + 1)
                if n >= 2:
                    act.wait_ge(stored[n % 2], n // 2 * 16)
                nc.scalar.copy(stage[:w, n % 2], bank[:w, n % 2]).then_inc(copied, 1)


def select_keys(nc, fm, wtok, bias):
    with Phase(nc, "select") as ph:
        tiles = [2, ST, 3, 4, 5, 6, 7]
        Q0 = 2 * P
        QN = SEQ - Q0
        QC = QN + P
        qraw = ph.sb("qraw", [P, IDX_H, QN + NEW])
        qtmp = ph.sb("qtmp", [P, IDX_H, QN + NEW])
        qhl = ph.sb("qhl", [P, IDX_H, QC], F32R)
        kraw = ph.sb("kraw", [P, KEYS])
        khh = ph.sb("khh", [P, KEYS], F32R)
        kll = ph.sb("kll", [P, KEYS], F32R)
        wraw = ph.sb("wraw", [P, TT, IDX_H])
        w = ph.sb("w", [P, TT, IDX_H])
        rel = ph.sb("rel", [P, 2, SEQ])
        wrel = ph.sb("wrel", [P, 2, SEQ])
        score = ph.sb("score", [P, 2, SEQ])
        left = ph.sb("left", [P, SEQ])
        best = ph.sb("best", [P, 8])
        offset = ph.sb("offset", [P, SEQ], mybir.dt.int32)
        minus = ph.sb("minus", [P, SEQ])
        dots = ph.ps("dots", [P, 2, 2, 512])
        q_in, k_in, w_in = ph.sem("q_in"), ph.sem("k_in"), ph.sem("w_in")
        cleared, qcopied, khigh, wscaled = (ph.sem(n) for n in ("cleared", "qcopied", "khigh", "wscaled"))
        qready, kready, numbered, measured = (ph.sem(n) for n in ("qready", "kready", "numbered", "measured"))
        multiplied, rectified, weighted, added = (ph.sem(n) for n in ("multiplied", "rectified", "weighted", "added"))
        chosen, step, passed = ph.sem("chosen"), ph.sem("step"), ph.sem("passed")
        back = (ST - 1) * P

        def q_of(t):
            return QN if t == ST else t * P - Q0

        def distance(t):
            at = back - (PAST if t == ST else t * P)
            return minus[:, at:at + width_of(t)]

        units = [(i, t, h) for i, t in enumerate(tiles) for h in range(IDX_H)]
        block = ph.block()

        @block.sync
        def _(sp):
            qrows = fm[A_QI * P:(A_QI + 4) * P].rearrange("(h d) c -> d h c", d=IDX_D)
            krows = fm[A_KI * P:A_KI * P + IDX_D]
            for half in range(2):
                at = slice(half * 64, half * 64 + 64)
                sp.dma_start(kraw[at], krows).then_inc(k_in, 16)
                sp.dma_start(qraw[at, :, 0:QN], qrows[:, :, Q0:SEQ]).then_inc(q_in, 16)
                sp.dma_start(qraw[at, :, QN:QN + NEW], qrows[:, :, SN:KEYS]).then_inc(q_in, 16)
            sp.wait_ge(cleared, 2)
            sp.dma_start(wraw[:, 0:ST], wtok[0:SEQ].rearrange("(t p) h -> p t h", p=P)).then_inc(w_in, 16)
            sp.dma_start(wraw[:NEW, ST], wtok[SEQ:TOK]).then_inc(w_in, 16)

        @block.gpsimd
        def _(pool):
            nc.gpsimd.memset(wraw[:, ST], 0.0).then_inc(cleared, 1)
            nc.gpsimd.memset(qhl[:, :, QN + NEW:QC].bitcast(F32), 0.0).then_inc(cleared, 1)
            nc.gpsimd.iota(offset[:], pattern=[[-1, SEQ]], base=back, channel_multiplier=1).then_inc(numbered, 1)
            pool.wait_ge(khigh, 1)
            nc.gpsimd.tensor_tensor(kll[:], kraw[:], khh[:].bitcast(F32), ALU.subtract).then_inc(kready, 1)
            for n, (i, t, h) in enumerate(units):
                wd = width_of(t)
                pool.wait_ge(weighted, n + 1)
                if h == 0:
                    if i >= 2:
                        pool.wait_ge(chosen, i - 1)
                    nc.gpsimd.tensor_copy(score[:, i % 2, 0:wd], wrel[:, n % 2, 0:wd]).then_inc(added, 1)
                else:
                    pool.wait_ge(added, n)
                    nc.gpsimd.tensor_tensor(score[:, i % 2, 0:wd], score[:, i % 2, 0:wd], wrel[:, n % 2, 0:wd],
                                            ALU.add).then_inc(added, 1)

        @block.tensor
        def _(pe):
            pe.wait_ge(kready, 1)
            pe.wait_ge(cleared, 2)
            for n, (i, t, h) in enumerate(units):
                if i == 0:
                    pe.wait_ge(qready, h + 1)
                if n >= 2:
                    pe.wait_ge(rectified, n - 1)
                wd, k0 = width_of(t), key0_of(t)
                for a in range(0, wd, 512):
                    b = min(a + 512, wd)
                    for part, k in enumerate((khh, kll)):
                        mm = nc.tensor.matmul(dots[:, n % 2, a // 512, 0:b - a], qhl[:, h, q_of(t):q_of(t) + P],
                                              k[:, k0 + a:k0 + b], start=part == 0, stop=part == 1)
                mm.then_inc(multiplied, 1)

        @block.scalar
        def _(act):
            act.wait_ge(k_in, 32)
            nc.scalar.copy(khh[:], kraw[:]).then_inc(khigh, 1)
            act.wait_ge(q_in, 64)
            for h in range(IDX_H):
                nc.scalar.copy(qhl[0:64, h, 0:QN + NEW], qraw[0:64, h]).then_inc(qcopied, 1)
                nc.scalar.copy(qtmp[64:128, h].bitcast(F32R), qraw[64:128, h]).then_inc(qcopied, 1)
            act.wait_ge(w_in, 32)
            nc.scalar.mul(w[:].rearrange("p a b -> p (a b)"), wraw[:].rearrange("p a b -> p (a b)"), IDX_SCALE
                          ).then_inc(wscaled, 1)
            act.wait_ge(wscaled, 1)
            for n, (i, t, h) in enumerate(units):
                wd = width_of(t)
                act.wait_ge(multiplied, n + 1)
                if n >= 2:
                    act.wait_ge(added, n - 1)
                nc.scalar.activation(rel[:, n % 2, 0:wd], dots[:, n % 2].rearrange("p a b -> p (a b)")[:, 0:wd],
                                     ACT.Relu).then_inc(rectified, 1)
                act.wait_ge(rectified, n + 1)
                nc.scalar.mul(wrel[:, n % 2, 0:wd], rel[:, n % 2, 0:wd], w[:, t, h:h + 1]).then_inc(weighted, 1)

        @block.vector
        def _(dve):
            steps = Counted(step)
            for h in range(IDX_H):
                dve.wait_ge(qcopied, 2 * h + 2)
                nc.vector.tensor_tensor(qhl[64:128, h, 0:QN + NEW], qraw[64:128, h], qtmp[64:128, h], ALU.subtract
                                        ).then_inc(qready, 1)
            dve.wait_ge(numbered, 1)
            nc.vector.tensor_copy(minus[:], offset[:]).then_inc(measured, 1)
            dve.wait_ge(measured, 1)
            nc.vector.tensor_scalar(left[:], minus[:], -1.0, None, ALU.mult).then_inc(measured, 1)
            dve.wait_ge(measured, 2)
            nc.vector.tensor_tensor(minus[:], minus[:], left[:], ALU.min).then_inc(measured, 1)
            dve.wait_ge(measured, 3)
            for t in (0, 1):
                steps.up(nc.vector.tensor_copy(bias[t], distance(t)))
                dve.wait_ge(step, steps.n)
                steps.up(nc.vector.memset(bias[t][0:CHUNK, width_of(t) - CHUNK:width_of(t)], -BIG))
            for i, t in enumerate(tiles):
                wd = width_of(t)
                scores, rest = score[:, i % 2, 0:wd], left[:, 0:wd]
                dve.wait_ge(added, IDX_H * (i + 1))
                if t != ST:
                    steps.up(nc.vector.memset(score[0:CHUNK, i % 2, wd - CHUNK:wd], BARRED))
                    dve.wait_ge(step, steps.n)
                steps.up(nc.vector.max(best[:], scores))
                dve.wait_ge(step, steps.n)
                steps.up(nc.vector.match_replace(rest, best[:], scores, TAKEN))
                rounds = (TOPK_STREAM if t == ST else TOPK) // 8 - 1
                n0 = steps.n
                with dve.Fori(0, rounds) as r:
                    wait_apart(dve, step, r * 2 + n0, passed)
                    nc.vector.max(best[:], rest).then_inc(step, 1)
                    wait_apart(dve, step, r * 2 + n0 + 1, passed)
                    nc.vector.match_replace(rest, best[:], rest, TAKEN).then_inc(step, 1)
                steps.n += 2 * rounds
                dve.wait_ge(step, steps.n)
                steps.up(nc.vector.tensor_tensor(rest, rest, scores, ALU.not_equal))
                dve.wait_ge(step, steps.n)
                steps.up(nc.vector.tensor_scalar(rest, rest, BIG, -BIG, ALU.mult, ALU.add))
                dve.wait_ge(step, steps.n)
                nc.vector.tensor_tensor(bias[t], rest, distance(t), ALU.add).then_inc(chosen, 1)
                dve.wait_ge(chosen, i + 1)


def forget_gates(nc, ident, fm, b_f, cache_logf, out_prompt, out_sample, minus_c, ctok):
    with Phase(nc, "forget") as ph:
        f = ph.sb("f", [HEADS, TOK])
        bf = ph.sb("bf", [HEADS, 1])
        z, e, u, d, lnu, r, logf = (ph.sb(n, [HEADS, TOK]) for n in ("z", "e", "u", "d", "lnu", "r", "logf"))
        stream = ph.sb("stream", [HEADS, PAST + NEW])
        ones = ph.sb("ones", [HEADS, SEQ])
        c = ph.sb("c", [HEADS, KEYS])
        mc = ph.sb("mc", [HEADS, KEYS])
        ltok = ph.sb("ltok", [P, TT, HEADS])
        bank = ph.ps("bank", [P, 2, 512])
        fin, step, turned, copied, stored = (ph.sem(n) for n in ("f_in", "step", "turned", "copied", "stored"))
        acts = ph.sem("acts")
        block = ph.block()

        @block.sync
        def _(sp):
            sp.dma_start(f[:, 0:SEQ], fm[0:HEADS, 0:SEQ]).then_inc(fin, 16)
            sp.dma_start(f[:, SEQ:TOK], fm[0:HEADS, SN:KEYS]).then_inc(fin, 16)
            sp.dma_start(bf[:], b_f).then_inc(fin, 16)
            with nc.allow_non_contiguous_dma("512 by 8 values"):
                sp.dma_start(stream[:, 0:PAST], cache_logf.rearrange("s h -> h s")).then_inc(fin, 16)
            sp.wait_ge(copied, 3)
            sp.dma_start(minus_c, mc[:]).then_inc(stored, 16)
            sp.dma_start(out_prompt.rearrange("(t p) h -> p t h", p=P), ltok[:, 0:ST]).then_inc(stored, 16)
            sp.dma_start(out_sample, ltok[:NEW, ST]).then_inc(stored, 16)
            sp.wait_ge(stored, 48)

        @block.scalar
        def _(act):
            act.wait_ge(step, 4)
            nc.scalar.activation(e[:], e[:], ACT.Exp, scale=-1.0).then_inc(acts, 1)
            act.wait_ge(step, 6)
            nc.scalar.activation(lnu[:], u[:], ACT.Ln).then_inc(acts, 1)

        @block.vector
        def _(dve):
            s = Counted(step)

            def then(instruction):
                s.up(instruction)
                dve.wait_ge(step, s.n)

            then(nc.vector.memset(ones[:], 1.0))
            nc.vector.memset(ctok[:, ST], 0.0)
            dve.wait_ge(fin, 64)
            then(nc.vector.tensor_scalar(z[:], f[:], bf[:], None, ALU.add))
            then(nc.vector.tensor_scalar(e[:], z[:], -1.0, None, ALU.mult))
            then(nc.vector.tensor_tensor(e[:], e[:], z[:], ALU.max))
            dve.wait_ge(acts, 1)
            then(nc.vector.tensor_scalar_min(z[:], z[:], 0.0))
            then(nc.vector.tensor_scalar_add(u[:], e[:], 1.0))
            then(nc.vector.tensor_scalar(d[:], u[:], -1.0, 1e-30, ALU.add, ALU.max))
            then(nc.vector.reciprocal(r[:], d[:]))
            then(nc.vector.tensor_tensor(r[:], r[:], e[:], ALU.mult))
            dve.wait_ge(acts, 2)
            then(nc.vector.tensor_scalar(d[:], u[:], 1.0, None, ALU.is_equal))
            then(nc.vector.tensor_tensor(d[:], d[:], e[:], ALU.mult))
            then(nc.vector.tensor_scalar(u[:], u[:], 1.0, None, ALU.is_gt))
            then(nc.vector.tensor_tensor(u[:], u[:], r[:], ALU.mult))
            then(nc.vector.tensor_tensor(u[:], u[:], lnu[:], ALU.mult))
            then(nc.vector.tensor_tensor(u[:], u[:], d[:], ALU.add))
            then(nc.vector.tensor_tensor(logf[:], z[:], u[:], ALU.subtract))
            then(nc.vector.tensor_copy(stream[:, PAST:], logf[:, SEQ:TOK]))
            then(nc.vector.tensor_tensor_scan(c[:, 0:SEQ], ones[:], logf[:, 0:SEQ], 0.0, ALU.mult, ALU.add))
            then(nc.vector.tensor_tensor_scan(c[:, S0:KEYS], ones[:, 0:PAST + NEW], stream[:], 0.0, ALU.mult, ALU.add))
            dve.sem_inc(turned, 1)
            nc.vector.tensor_scalar(mc[:], c[:], -1.0, None, ALU.mult).then_inc(copied, 1)
            dve.wait_ge(turned, 2)
            for n, to in enumerate((ltok, ctok)):
                nc.vector.tensor_copy(to[:, 0:ST], bank[:, n, 0:ST * HEADS].rearrange("p (t h) -> p t h", h=HEADS)
                                      ).then_inc(step, 1)
                nc.vector.tensor_copy(to[:NEW, ST], bank[:NEW, n, ST * HEADS:TT * HEADS]).then_inc(copied, 1)
            dve.wait_ge(copied, 3)

        @block.tensor
        def _(pe):
            pe.wait_ge(turned, 1)
            for n in range(2):
                for t in range(TT):
                    r_ = rows_of(t)
                    src = (logf[:, t * P:t * P + r_] if n == 0 else
                           c[:, SN:KEYS] if t == ST else c[:, t * P:(t + 1) * P])
                    mm = nc.tensor.transpose(bank[:r_, n, t * HEADS:(t + 1) * HEADS], src, ident[:HEADS, :HEADS])
            mm.then_inc(turned, 1)


def attend(nc, name, ident, o, fmq, q0, fmk, kv_of, v_prompt, v_past, v_new, bias=None, minus_c=None, ctok=None):
    sparse = bias is not None
    QW = SEQ + P
    VT = KEYS // P + 1
    order = [7, ST, 6, 5, 4, 3, 2, 1, 0]
    NU = 2 * TT
    with Phase(nc, name) as ph:
        qraw, kraw, vraw = ph.sb("qraw", [P, TOK]), ph.sb("kraw", [P, KEYS]), ph.sb("vraw", [P, VT, HD])
        qh, ql = (ph.sb(n, [P, 2, QW], F32R) for n in ("qh", "ql"))
        kh, kl = (ph.sb(n, [P, 2, KEYS], F32R) for n in ("kh", "kl"))
        vh, vl = (ph.sb(n, [P, 2, VT, HD], F32R) for n in ("vh", "vl"))
        qscale, slope = ph.sb("qscale", [P, HEADS]), ph.sb("slope", [P, HEADS])
        prob = ph.sb("prob", [P, 2, SEQ])
        pth, ptl = (ph.sb(n, [P, 2, KT, P], F32R) for n in ("pth", "ptl"))
        top, shift = ph.sb("top", [P, 2]), ph.sb("shift", [P, 2])
        total, inverse = ph.sb("total", [P, 4]), ph.sb("inverse", [P, 4])
        if not sparse:
            minus = ph.sb("minus", [P, 2, KEYS])
            row_c = ph.sb("row_c", [P, 2])
            later = ph.sb("later", [P, P], F32R)
            one = ph.sb("one", [P, P], F32R)
        logits, trans, outs = ph.ps("logits", [P, 2, 2, 512]), ph.ps("trans", [P, 2, 512]), ph.ps("outs", [P, 2, 512])
        q_in, k_in, v_in = (ph.sem(n) for n in ("q_in", "k_in", "v_in"))
        c_in = [ph.sem(f"c_in{s}") for s in range(2)]
        constants, qscaled, highs, lows = (ph.sem(n) for n in ("constants", "qscaled", "highs", "lows"))
        multiplied, biased, shifted, raised = (ph.sem(n) for n in ("multiplied", "biased", "shifted", "raised"))
        turned, thigh, tlow, summed, scaled = (ph.sem(n) for n in ("turned", "thigh", "tlow", "summed", "scaled"))
        small, passed = ph.sem("small"), ph.sem("passed")
        unit = lambda n: (n // TT, order[n % TT])

        def pairs(engine, body):
            with engine.Fori(0, HEADS // 2 - 1) as pair:
                body(pair * NU, pair, False)
            body((HEADS // 2 - 1) * NU, HEADS // 2 - 1, True)

        block = ph.block()

        @block.sync
        def _(sp):
            def load(head, kv):
                wait_apart(sp, lows, head * 3 + 1, passed)
                sp.dma_start(qraw[:, 0:SEQ], fmq[bass.ds(q0 + head * P, P), 0:SEQ]).then_inc(q_in, 16)
                sp.dma_start(qraw[:, SEQ:TOK], fmq[bass.ds(q0 + head * P, P), SN:KEYS]).then_inc(q_in, 16)
                wait_apart(sp, lows, head * 3 + 2, passed)
                sp.dma_start(kraw[:], fmk[bass.ds(kv * P, P)]).then_inc(k_in, 16)
                wait_apart(sp, lows, head * 3 + 3, passed)
                sp.dma_start(vraw[:, 0:8], v_prompt[:, bass.ds(kv * P, P)].rearrange("(t p) d -> p t d", p=P)
                             ).then_inc(v_in, 16)
                sp.dma_start(vraw[:, 8:12], v_past[:, bass.ds(kv * P, P)].rearrange("(t p) d -> p t d", p=P)
                             ).then_inc(v_in, 16)
                sp.dma_start(vraw[:NEW, 12], v_new[:, bass.ds(kv * P, P)]).then_inc(v_in, 16)

            sp.wait_ge(constants, 1)
            load(0, 0)

            def body(u0, pair, last):
                for s in range(2):
                    if not sparse:
                        sp.wait_ge(biased, u0 + s * TT + 1)
                        sp.dma_start(minus[:, s], minus_c[bass.ds(pair * 2 + s, 1)].rearrange("a k -> (a k)")
                                     .partition_broadcast(P)).then_inc(c_in[s], 16)
                    if not (last and s == 1):
                        load(pair * 2 + s + 1, kv_of(pair, s))
            pairs(sp, body)

        @block.gpsimd
        def _(pool):
            nc.gpsimd.memset(vraw[:, 12], 0.0).then_inc(constants, 1)
            nc.gpsimd.memset(qh[:, :, TOK:QW].bitcast(F32), 0.0).then_inc(constants, 1)
            nc.gpsimd.memset(ql[:, :, TOK:QW].bitcast(F32), 0.0).then_inc(constants, 1)
            for h in range(HEADS):
                power = 2.0 ** (h + 1) if sparse else 1.0
                nc.gpsimd.memset(qscale[:, h:h + 1], SCALE * power).then_inc(constants, 1)
                nc.gpsimd.memset(slope[:, h:h + 1], 1.0 / power).then_inc(constants, 1)
            if not sparse:
                nc.gpsimd.memset(prob[:, 0, 0:P], 0.0).then_inc(constants, 1)
                pool.wait_ge(constants, 20)
                nc.gpsimd.affine_select(out=later[:], in_=prob[:, 0, 0:P], compare_op=ALU.is_ge, fill=-BIG, base=0,
                                        pattern=[[-1, P]], channel_multiplier=1).then_inc(constants, 1)
                nc.gpsimd.tensor_copy(one[:], ident[:]).then_inc(constants, 1)
            pool.sem_inc(lows, 3)

            def low(head, s):
                pool.wait_ge(highs, head * 3 + 1)
                nc.gpsimd.tensor_tensor(ql[:, s, 0:TOK], qraw[:], qh[:, s, 0:TOK].bitcast(F32), ALU.subtract
                                        ).then_inc(lows, 1)
                pool.wait_ge(highs, head * 3 + 2)
                nc.gpsimd.tensor_tensor(kl[:, s], kraw[:], kh[:, s].bitcast(F32), ALU.subtract).then_inc(lows, 1)
                pool.wait_ge(highs, head * 3 + 3)
                nc.gpsimd.tensor_tensor(vl[:, s], vraw[:], vh[:, s].bitcast(F32), ALU.subtract).then_inc(lows, 1)

            low(0, 0)

            def body(u0, pair, last):
                for s in range(2):
                    if not (last and s == 1):
                        low(pair * 2 + s + 1, 1 - s)
            pairs(pool, body)

        @block.tensor
        def _(pe):
            pe.sem_inc(turned, 2)
            pe.sem_inc(summed, 2)
            pe.wait_ge(constants, 19 if sparse else 22)

            def scores(n, u0, pair):
                s, t = unit(n)
                if n % TT == 0:
                    pe.wait_ge(lows, (pair * 2 + s) * 3 + 5)
                pe.wait_ge(biased, u0 + n + TT)
                wd, k0, q = width_of(t), key0_of(t), slice(t * P, (t + 1) * P)
                for a in range(0, wd, 512):
                    b = min(a + 512, wd)
                    to = logits[:, n % 2, a // 512, 0:b - a]
                    parts = ((qh, kh), (ql, kh), (qh, kl))
                    masked = not sparse and b == wd
                    for part, (x, y) in enumerate(parts):
                        mm = nc.tensor.matmul(to, x[:, s, q], y[:, s, k0 + a:k0 + b], start=part == 0,
                                              stop=part == 2 and not masked)
                    if masked:
                        m = rows_of(t)
                        mm = nc.tensor.matmul(logits[:, n % 2, a // 512, b - a - m:b - a], one[:], later[:, 0:m],
                                              start=False, stop=True)
                mm.then_inc(multiplied, 1)

            def turn(n, u0):
                s, t = unit(n)
                wd = width_of(t)
                pe.wait_ge(raised, u0 + n + 1)
                pe.wait_ge(tlow, u0 + n + 1)
                for j, a in enumerate(range(0, wd, P)):
                    b = min(a + P, wd)
                    mm = nc.tensor.transpose(trans[:b - a, j // 4, j % 4 * P:(j % 4 + 1) * P],
                                             prob[:, n % 2, a:b], ident[:])
                mm.then_inc(turned, 1)

            def weigh(n, u0, pair):
                s, t = unit(n)
                wd, v0 = width_of(t), key0_of(t) // P
                if n % TT == 0:
                    pe.wait_ge(lows, (pair * 2 + s) * 3 + 6)
                pe.wait_ge(tlow, u0 + n + 2)
                pe.wait_ge(scaled, u0 + n + 1)
                tiles = [(j, min(P, wd - j * P)) for j in range((wd + P - 1) // P)]
                for j, m in tiles:
                    for part, (x, y) in enumerate(((pth, vh), (ptl, vh), (pth, vl))):
                        mm = nc.tensor.matmul(outs[:, n % 2, 0:HD], x[:m, n % 2, j], y[:m, s, v0 + j],
                                              start=j == 0 and part == 0, stop=j == len(tiles) - 1 and part == 2)
                mm.then_inc(summed, 1)

            def body(u0, pair, last):
                for n in range(NU + 2):
                    if n < NU:
                        scores(n, u0, pair)
                    if 1 <= n <= NU:
                        turn(n - 1, u0)
                    if n >= 2:
                        weigh(n - 2, u0, pair)
            pairs(pe, body)

        @block.scalar
        def _(act):
            def high(head, s, what):
                if what == 0:
                    act.wait_ge(q_in, head * 32 + 32)
                    nc.scalar.mul(qraw[:], qraw[:], qscale[:, bass.ds(head, 1)]).then_inc(qscaled, 1)
                    act.wait_ge(qscaled, head + 1)
                    nc.scalar.copy(qh[:, s, 0:TOK], qraw[:]).then_inc(highs, 1)
                elif what == 1:
                    act.wait_ge(k_in, head * 16 + 16)
                    nc.scalar.copy(kh[:, s], kraw[:]).then_inc(highs, 1)
                else:
                    act.wait_ge(v_in, head * 48 + 48)
                    nc.scalar.copy(vh[:, s], vraw[:]).then_inc(highs, 1)

            def raise_(n, u0, pair):
                s, t = unit(n)
                wd = width_of(t)
                wait_apart(act, shifted, u0 + n + 1, passed)
                scale = slope[:, bass.ds(pair * 2 + s, 1)] if sparse else 1.0
                nc.scalar.activation(prob[:, n % 2, 0:wd], prob[:, n % 2, 0:wd], ACT.Exp, scale=scale,
                                     bias=shift[:, n % 2:n % 2 + 1], accum_out=total[:, n % 4:n % 4 + 1]
                                     ).then_inc(raised, 1)

            def turned_high(n, u0):
                s, t = unit(n)
                wd = width_of(t)
                act.wait_ge(turned, u0 + n + 3)
                act.wait_ge(summed, u0 + n + 1)
                full, rest = wd // P, wd % P
                for i, a in enumerate(range(0, full, 4)):
                    b = min(a + 4, full)
                    last = nc.scalar.copy(pth[:, n % 2, a:b].rearrange("p a n -> p (a n)"),
                                          trans[:, a // 4, 0:(b - a) * P])
                if rest:
                    last = nc.scalar.copy(pth[:rest, n % 2, full], trans[:rest, full // 4, 0:P])
                last.then_inc(thigh, 1)

            act.wait_ge(constants, 19)
            for what in range(3):
                high(0, 0, what)

            def body(u0, pair, last):
                for n in range(NU + 1):
                    if n >= 1:
                        turned_high(n - 1, u0)
                    if n < NU:
                        raise_(n, u0, pair)
                    s = n // TT
                    if n < NU and n % TT in (3, 4, 5) and not (last and s == 1):
                        high(pair * 2 + s + 1, 1 - s, n % TT - 3)
            pairs(act, body)

        @block.vector
        def _(dve):
            dve.sem_inc(biased, TT + 1)
            dve.sem_inc(tlow, 1)
            dve.sem_inc(scaled, 2)

            def add_bias(n, u0, pair):
                s, t = unit(n)
                wd, k0, b2 = width_of(t), key0_of(t), n % 2
                wait_apart(dve, multiplied, u0 + n + 1, passed)
                if not sparse and n % TT == 0:
                    dve.wait_ge(c_in[s], pair * 16 + 16)
                wait_apart(dve, turned, u0 + n + 1, passed)
                add = bias[t] if sparse else minus[:, s, k0:k0 + wd]
                nc.vector.tensor_tensor_reduce(out=prob[:, b2, 0:wd],
                                               in0=logits[:, b2].rearrange("p a b -> p (a b)")[:, 0:wd], in1=add,
                                               scale=1.0, scalar=-3.0e38, op0=ALU.add, op1=ALU.max,
                                               accum_out=top[:, b2:b2 + 1]).then_inc(biased, 1)
                dve.wait_ge(biased, u0 + n + TT + 2)
                if sparse:
                    nc.vector.tensor_scalar(shift[:, b2:b2 + 1], top[:, b2:b2 + 1],
                                            slope[:, bass.ds(pair * 2 + s, 1)], -1.0, ALU.mult, ALU.mult
                                            ).then_inc(shifted, 1)
                else:
                    row = ctok[:, t, bass.ds(pair * 2 + s, 1)]
                    nc.vector.tensor_scalar(row_c[:, b2:b2 + 1], top[:, b2:b2 + 1], row, None, ALU.add
                                            ).then_inc(small, 1)
                    dve.wait_ge(small, small_at(n, u0))
                    nc.vector.tensor_scalar(shift[:, b2:b2 + 1], row_c[:, b2:b2 + 1], -1.0, row, ALU.mult, ALU.add
                                            ).then_inc(shifted, 1)

            def small_at(n, u0):
                return u0 * 2 + n + 1 + max(0, n - 2)

            def turned_low(n, u0):
                s, t = unit(n)
                wd = width_of(t)
                dve.wait_ge(thigh, u0 + n + 1)
                full, rest = wd // P, wd % P
                for a in range(0, full, 4):
                    b = min(a + 4, full)
                    last = nc.vector.tensor_tensor(ptl[:, n % 2, a:b].rearrange("p a n -> p (a n)"),
                                                   trans[:, a // 4, 0:(b - a) * P],
                                                   pth[:, n % 2, a:b].rearrange("p a n -> p (a n)").bitcast(F32),
                                                   ALU.subtract)
                if rest:
                    last = nc.vector.tensor_tensor(ptl[:rest, n % 2, full], trans[:rest, full // 4, 0:P],
                                                   pth[:rest, n % 2, full].bitcast(F32), ALU.subtract)
                last.then_inc(tlow, 1)

            def normalise(n, u0, pair):
                s, t = unit(n)
                dve.wait_ge(summed, u0 + n + 3)
                nc.vector.reciprocal(inverse[:, n % 4:n % 4 + 1], total[:, n % 4:n % 4 + 1]).then_inc(small, 1)
                dve.wait_ge(small, (u0 + n + 1) if sparse else u0 * 2 + n + 1 + min(n + 3, NU))
                nc.vector.tensor_scalar(o[:, t, bass.ds((pair * 2 + s) * HD, HD)], outs[:, n % 2, 0:HD],
                                        inverse[:, n % 4:n % 4 + 1], None, ALU.mult).then_inc(scaled, 1)

            def body(u0, pair, last):
                for n in range(NU + 2):
                    if n < NU:
                        add_bias(n, u0, pair)
                    if 1 <= n <= NU:
                        turned_low(n - 1, u0)
                    if n >= 2:
                        normalise(n - 2, u0, pair)
            pairs(dve, body)


def mlp(nc, name, xh, xl, y, w_up, w_down):
    UP, LOADS, BLOCKS = 4, 8, 12
    wu = w_up.rearrange("(k p) n -> p k n", p=P)
    wd = w_down.rearrange("(k p) n -> p k n", p=P)
    with Phase(nc, name) as ph:
        raw, wh, wl, win, high, low = weight_slots(ph)
        hh, hl = (ph.sb(n, [P, UP, TOK], F32R) for n in ("hh", "hl"))
        hidden = ph.sb("hidden", [P, 2, TOK])
        acc = ph.ps("acc", [P, 2, NG, 512])
        multiplied, taken = ph.sem("multiplied"), ph.sem("taken")
        cleared, squared, split, step = (ph.sem(n) for n in ("cleared", "squared", "split", "step"))
        block = ph.block()

        def chunks(engine, body):
            with engine.Fori(0, D_FF // 512) as c:
                body(c)

        @block.sync
        def _(sp):
            def body(c):
                for n in range(LOADS):
                    sp.wait_ge(low, c * LOADS + n + 1)
                    if n < UP:
                        src, k = wu[:, :, bass.ds(c * 512 + n * P, P)], KT
                    else:
                        src, k = wd[:, bass.ds(c * 4, 4), (n - UP) * 256:(n - UP + 1) * 256], 4
                    sp.dma_start(raw[:, n % 2].rearrange("p (k n) -> p k n", k=k), src).then_inc(win[n % 2], 16)
            chunks(sp, body)

        @block.scalar
        def _(act):
            def body(c):
                for n in range(LOADS):
                    act.wait_ge(win[n % 2], c * (LOADS * 8) + n // 2 * 16 + 16)
                    done = n - 1 if 2 <= n <= 5 else UP + 2 * (n - 5) if n > 5 else (-2, 0)[n]
                    act.wait_ge(multiplied, c * BLOCKS + done + 3)
                    nc.scalar.copy(wh[:, n % 2], raw[:, n % 2]).then_inc(high, 1)
            chunks(act, body)

        @block.gpsimd
        def _(pool):
            pool.sem_inc(low, 2)

            def body(c):
                for n in range(LOADS):
                    pool.wait_ge(high, c * LOADS + n + 1)
                    nc.gpsimd.tensor_tensor(wl[:, n % 2], raw[:, n % 2], wh[:, n % 2].bitcast(F32), ALU.subtract
                                            ).then_inc(low, 1)
            chunks(pool, body)

        @block.tensor
        def _(pe):
            pe.sem_inc(multiplied, 3)

            def body(c):
                for n in range(BLOCKS):
                    up = n < UP
                    load = n if up else UP + (n - UP) // 2
                    if up or (n - UP) % 2 == 0:
                        pe.wait_ge(low, c * LOADS + load + 3)
                    pe.wait_ge(taken, c * BLOCKS + n + 1)
                    for k in range(KT if up else 4):
                        if n == UP:
                            pe.wait_ge(split, c * UP + k + 1)
                        for g in range(NG):
                            at = k * P if up else k * 256 + n % 2 * P
                            w_h, w_l = (w[:, load % 2, at:at + P] for w in (wh, wl))
                            x_h, x_l = (x[:, k, g * G:(g + 1) * G] for x in ((xh, xl) if up else (hh, hl)))
                            for part, (w, x) in enumerate(((w_h, x_h), (w_h, x_l), (w_l, x_h))):
                                mm = nc.tensor.matmul(acc[:, n % 2, g, 0:G], w, x, start=k == 0 and part == 0,
                                                      stop=k == (KT if up else 4) - 1 and part == 2)
                    mm.then_inc(multiplied, 1)
            chunks(pe, body)

        @block.vector
        def _(dve):
            dve.sem_inc(taken, 2)
            nc.vector.memset(y[:, 0:KT, :], 0.0).then_inc(cleared, 1)
            dve.wait_ge(cleared, 1)

            def body(c):
                for n in range(BLOCKS):
                    dve.wait_ge(multiplied, c * BLOCKS + n + 4)
                    banks = acc[:, n % 2, :, 0:G]
                    if n < UP:
                        h = hidden[:, n % 2]
                        nc.vector.tensor_scalar_max(h.rearrange("p (g n) -> p g n", g=NG), banks, 0.0
                                                    ).then_inc(taken, 1)
                        dve.wait_ge(taken, c * BLOCKS + n + 3)
                        nc.vector.tensor_tensor(h, h, h, ALU.mult).then_inc(squared, 1)
                        dve.wait_ge(squared, c * UP + n + 1)
                        nc.vector.tensor_copy(hh[:, n], h).then_inc(step, 1)
                        dve.wait_ge(step, c * UP + n + 1)
                        nc.vector.tensor_tensor(hl[:, n], h, hh[:, n].bitcast(F32), ALU.subtract).then_inc(split, 1)
                    else:
                        at = y[:, n - UP].rearrange("p (g n) -> p g n", g=NG)
                        nc.vector.tensor_tensor(at, banks, at, ALU.add).then_inc(taken, 1)
            chunks(dve, body)
            dve.wait_ge(taken, D_FF // 512 * BLOCKS + 2)


def trunk(nc, x_prompt, x_sample, cache_a_k, cache_a_v, cache_a_kidx, cache_b_k, cache_b_v, cache_b_logf, w_a_in,
          w_a_o, w_b_kv, b_b_f, w_b_q, w_b_o, w_up, w_down, ln_g, ln_b, y_prompt, y_sample, a_k_prompt, a_v_prompt,
          a_kidx_prompt, b_k_prompt, b_v_prompt, b_logf_prompt, a_k_sample, a_v_sample, a_kidx_sample, b_k_sample,
          b_v_sample, b_logf_sample):
    def scratch(name, shape):
        return nc.dram_tensor(name, shape, F32, kind="Internal").ap()

    fm_a = scratch("fm_a", [17 * P, KEYS])
    fm_kv = scratch("fm_kv", [17 * P, KEYS])
    fm_q = scratch("fm_q", [8 * P, KEYS])
    w_rows = scratch("w_rows", [TOK, IDX_H])
    minus_c = scratch("minus_c", [HEADS, KEYS])
    x_rows = [scratch(f"x_rows{i}", [TOK, D]) for i in range(3)]

    def row_tile(prompt, stream):
        return lambda t: stream if t == ST else prompt[t * P:(t + 1) * P]

    def scratch_tile(x):
        return lambda t: x[t * P:t * P + rows_of(t)]

    flat = lambda x: x.rearrange("s h d -> s (h d)")
    ak_p, av_p, ak_s, av_s = (flat(x[0, 0]) for x in (a_k_prompt, a_v_prompt, a_k_sample, a_v_sample))
    bk_p, bv_p, bk_s, bv_s = (flat(x[0]) for x in (b_k_prompt, b_v_prompt, b_k_sample, b_v_sample))

    def to_rows(prompt, stream, block):
        at = bass.ds(block * P, P)
        return [(prompt[:, at].rearrange("(t p) n -> p t n", p=P), lambda st: st[:, 0:ST]),
                (stream[:, at], lambda st: st[:NEW, ST])]

    def last_a(_):
        k, w = slice(0, IDX_D), slice(IDX_D, IDX_D + IDX_H)
        return [(a_kidx_prompt[0, 0].rearrange("(t p) n -> p t n", p=P), lambda st: st[:, 0:ST, k]),
                (a_kidx_sample[0, 0], lambda st: st[:NEW, ST, k]),
                (w_rows[0:SEQ].rearrange("(t p) n -> p t n", p=P), lambda st: st[:, 0:ST, w]),
                (w_rows[SEQ:TOK], lambda st: st[:NEW, ST, w])]

    with Phase(nc, "all") as ph:
        ident = ph.sb("ident", [P, P])
        rows = ph.sb("rows", [P, TT, D])
        ctok = ph.sb("ctok", [P, TT, HEADS])
        y = rows[:].rearrange("p t d -> p (t d)")[:, 0:KT * TOK].rearrange("p (k n) -> p k n", k=KT)
        make_identity(nc, ident)
        turn_caches(nc, ident, [(cache_a_k[0, 0], fm_a, A_K * P), (cache_a_kidx[0, 0:1].rearrange("a s d -> s a d"),
                                                                 fm_a, A_KI * P), (cache_b_k[0], fm_kv, 0)])

        def activations(p):
            return p.sb("xh", [P, KT, TOK], F32R), p.sb("xl", [P, KT, TOK], F32R)

        with Phase(nc, "a_in") as p:
            xh, xl = activations(p)
            refill(nc, "turn_x", ident, xh, xl, "rows", residual=row_tile(x_prompt[0], x_sample[0]))
            project(nc, "a_qkv", xh, xl, w_a_in[0], ident, blocks=17, last_cols=72, fm=fm_a,
                    turns=[(A_K, 2, lambda n: to_rows(ak_p, ak_s, n - A_K)),
                           (A_V, 2, lambda n: to_rows(av_p, av_s, n - A_V)), (A_KI, 1, last_a)])
        with Phase(nc, "a_att") as p:
            bias = [p.sb(f"bias{t}", [P, width_of(t)])[:] for t in range(TT)]
            select_keys(nc, fm_a, w_rows, bias)
            attend(nc, "a_heads", ident, rows, fm_a, A_Q * P, fm_a[A_K * P:(A_K + N_KV) * P],
                   lambda pair, s: (pair + s) // 2, av_p, flat(cache_a_v[0, 0]), av_s, bias=bias)
        clear_semaphores(nc)
        with Phase(nc, "mid") as p:
            xh, xl = activations(p)
            refill(nc, "a_turn", ident, xh, xl, "sbuf", y=rows)
            project(nc, "a_out", xh, xl, w_a_o[0], y=y)
            refill(nc, "a_norm", ident, xh, xl, "norm", residual=row_tile(x_prompt[0], x_sample[0]), y=y,
                   gain=ln_g[0, 0], shift=ln_b[0, 0], keep=scratch_tile(x_rows[0]))
            mlp(nc, "a_mlp", xh, xl, y, w_up[0], w_down[0])
            refill(nc, "a_norm2", ident, xh, xl, "norm", residual=scratch_tile(x_rows[0]), y=y,
                   gain=ln_g[0, 1], shift=ln_b[0, 1], keep=scratch_tile(x_rows[1]))
            project(nc, "b_kv", xh, xl, w_b_kv, ident, blocks=17, last_cols=HEADS, fm=fm_kv,
                    turns=[(0, 8, lambda n: to_rows(bk_p, bk_s, n)), (8, 8, lambda n: to_rows(bv_p, bv_s, n - 8))])
            project(nc, "b_q", xh, xl, w_b_q[0], ident, blocks=8, fm=fm_q)
        clear_semaphores(nc)
        forget_gates(nc, ident, fm_kv[16 * P:17 * P], b_b_f.rearrange("(h a) -> h a", a=1), cache_b_logf[0],
                     b_logf_prompt[0], b_logf_sample[0], minus_c, ctok)
        attend(nc, "b_heads", ident, rows, fm_q, 0, fm_kv, lambda pair, s: pair * 2 + s + 1, bv_p,
               flat(cache_b_v[0]), bv_s, minus_c=minus_c, ctok=ctok)
        with Phase(nc, "end") as p:
            xh, xl = activations(p)
            refill(nc, "b_turn", ident, xh, xl, "sbuf", y=rows)
            project(nc, "b_out", xh, xl, w_b_o[0], y=y)
            refill(nc, "b_norm", ident, xh, xl, "norm", residual=scratch_tile(x_rows[1]), y=y,
                   gain=ln_g[1, 0], shift=ln_b[1, 0], keep=scratch_tile(x_rows[2]))
            mlp(nc, "b_mlp", xh, xl, y, w_up[1], w_down[1])
            refill(nc, "b_norm2", ident, xh, xl, "norm", residual=scratch_tile(x_rows[2]), y=y,
                   gain=ln_g[1, 1], shift=ln_b[1, 1], keep=row_tile(y_prompt[0], y_sample[0]), last=True)


_INS = ["x_prompt", "x_sample", "cache_a_k", "cache_a_v", "cache_a_kidx", "cache_b_k", "cache_b_v", "cache_b_logf",
        "w_a_in", "w_a_o", "w_b_kv", "b_b_f", "w_b_q", "w_b_o", "w_up", "w_down", "ln_g", "ln_b"]
_OUTS = [(1, SEQ, D), (1, NEW, D),
         (1, 1, SEQ, N_KV, HD), (1, 1, SEQ, N_KV, HD), (1, 1, SEQ, IDX_D),
         (1, SEQ, HEADS, HD), (1, SEQ, HEADS, HD), (1, SEQ, HEADS),
         (1, 1, NEW, N_KV, HD), (1, 1, NEW, N_KV, HD), (1, 1, NEW, IDX_D),
         (1, NEW, HEADS, HD), (1, NEW, HEADS, HD), (1, NEW, HEADS)]


def kernel(**inputs):
    import concourse.bacc as bacc
    from concourse.bass_utils import run_bass_kernel_spmd

    nc = bacc.Bacc("TRN2", target_bir_lowering=False, num_devices=1)
    arrays, args = {}, []
    for name in _INS:
        a = np.ascontiguousarray(inputs[name])
        arrays[f"in_{name}"] = a
        args.append(nc.dram_tensor(f"in_{name}", a.shape, mybir.dt.from_np(a.dtype), kind="ExternalInput").ap())
    for i, shape in enumerate(_OUTS):
        args.append(nc.dram_tensor(f"out_{i}", shape, F32, kind="ExternalOutput").ap())
    Phase.raised.clear()
    trunk(nc, *args)
    r = run_bass_kernel_spmd(nc, [arrays], core_ids=[0])
    return tuple(r.results[0][f"out_{i}"] for i in range(len(_OUTS)))
```

```python
from contextlib import ExitStack

import numpy as np

import concourse.bass as bass
from concourse import mybir

F32 = mybir.dt.float32
F32R = mybir.dt.float32r
ALU = mybir.AluOpType
ACT = mybir.ActivationFunctionType
AX_X = mybir.AxisListType.X

P = 128
D = 1024
KT = D // P
SEQ, NEW, PAST = 1024, 32, 512
TOK = SEQ + NEW
TT = SEQ // P + 1
ST = TT - 1
HEADS, HD = 8, 128
N_KV = 2
IDX_H, IDX_D = 8, 64
CHUNK = 64
D_FF = 4 * D
KEYS = SEQ + PAST + NEW
S0 = SEQ
SN = SEQ + PAST
TOPK = 256
TOPK_STREAM = min(TOPK, (PAST + NEW) // 4)
IDX_SCALE = (IDX_H * IDX_D) ** -0.5
SCALE = HD ** -0.5
ALPHA = 4.0 ** 0.25
LN_EPS = 1e-5
BIG = 1e30
TAKEN = -3.0e38
BARRED = -3.2e38
A_Q, A_K, A_V, A_QI, A_KI = 0, 8, 10, 12, 16


def rows_of(t):
    return NEW if t == ST else P


def width_of(t):
    return PAST + NEW if t == ST else P * (t + 1)


def key0_of(t):
    return S0 if t == ST else 0


def wait_apart(engine, sem, value, passed):
    engine.wait_ge(sem, value)
    engine.sem_inc(passed, 1)


class Group:

    def __init__(self, tiles, banks):
        self.tiles, self.banks = tiles, banks
        self.start, self.cols = {}, 0
        for t in tiles:
            self.start[t] = self.cols
            self.cols += rows_of(t)
        self.g = self.cols // banks

    def at(self, t):
        return slice(self.start[t], self.start[t] + rows_of(t))


EVERY = Group(list(range(TT)), 3)
EARLY = Group([0, 1, 2, 3, 4, ST], 2)
LATE = Group([5, 6, 7], 1)


class Counted:

    def __init__(self, sem):
        self.sem, self.n = sem, 0

    def up(self, instruction):
        self.n += 1
        instruction.then_inc(self.sem, 1)
        return self.n


def in_pairs(engine, first, count, step):
    if count >= 4:
        with engine.Fori(first // 2, (first + count) // 2) as pair:
            for s in range(2):
                step(pair * 2 + s, s)
    elif count >= 2:
        for n in range(first, first + count // 2 * 2):
            step(n, n % 2)
    if count % 2:
        step(first + count - 1, 0)


class Phase:

    raised = []

    def __init__(self, nc, name):
        self.nc, self.name, self.ctx = nc, name, ExitStack()

    def __enter__(self):
        return self

    def __exit__(self, *e):
        return self.ctx.__exit__(*e)

    def sb(self, name, shape, dt=F32):
        return self.ctx.enter_context(self.nc.sbuf_tensor(f"{self.name}_{name}", shape, dt))

    def ps(self, name, shape):
        return self.ctx.enter_context(self.nc.psum_tensor(f"{self.name}_{name}", shape, F32))

    def sem(self, name):
        handle = self.nc.alloc_semaphore(f"{self.name}_{name}")
        self.raised.append(handle)
        return handle

    def block(self):
        return self.ctx.enter_context(self.nc.Block())


def clear_semaphores(nc):
    nc.clear_and_free_semaphores(list(Phase.raised))
    Phase.raised.clear()
    nc.all_engine_barrier()


def make_identity(nc, ident):
    with Phase(nc, "ident") as ph:
        zeroed = ph.sem("zeroed")
        block = ph.block()

        @block.gpsimd
        def _(pool):
            nc.gpsimd.memset(ident[:], 0.0).then_inc(zeroed, 1)
            pool.wait_ge(zeroed, 1)
            nc.gpsimd.affine_select(out=ident[:], in_=ident[:], compare_op=ALU.not_equal, fill=1.0, base=0,
                                    pattern=[[-1, P]], channel_multiplier=1).then_inc(zeroed, 1)
            pool.wait_ge(zeroed, 2)


def refill(nc, name, ident, grp, xh, xl, source, residual=None, y=None, gain=None, shift=None, keep=None, last=False):
    tiles = grp.tiles
    TN = len(tiles)
    with Phase(nc, name) as ph:
        rin = [ph.sem(f"rows_in{s}") for s in range(2)]
        kept = [ph.sem(f"rows_kept{s}") for s in range(2)]
        turned, high, low = ph.sem("turned"), ph.sem("high"), ph.sem("low")
        back = ph.ps("back", [P, 2, 2, 512])
        norm = source == "norm"
        if source != "sbuf":
            rows = ph.sb("rows", [P, 2, D])
        if norm:
            fed, centred, scaled, shifted = (ph.sem(n) for n in ("fed", "centred", "scaled", "shifted"))
            params, vec, root = ph.sem("params"), ph.sem("vec"), ph.sem("root")
            up = ph.ps("up", [P, 2, 2, 512])
            summed = ph.sb("summed", [P, 2, D])
            cent = ph.sb("cent", [P, 2, D])
            done = ph.sb("done", [P, 2, D])
            gains = ph.sb("gains", [P, D])
            shifts = ph.sb("shifts", [P, D])
            stats = ph.sb("stats", [P, 2, 2, 6])
            mv = ph.sb("mv", [P, 2, 2])
            small = ph.sb("small", [P, 2, 3])
        src = {"rows": lambda t: rows[:, t % 2], "sbuf": lambda t: y[:, tiles[t], :], "norm": lambda t: done[:, t % 2]}[source]
        block = ph.block()

        @block.sync
        def _(sp):
            if norm:
                sp.dma_start(gains[:], gain.partition_broadcast(P)).then_inc(params, 16)
                sp.dma_start(shifts[:], shift.partition_broadcast(P)).then_inc(params, 16)
            if source != "sbuf":
                for t in range(TN):
                    if t >= 2:
                        sp.wait_ge(vec if norm else turned, 1 + 6 * (t - 2) if norm else t - 1)
                    sp.dma_start(rows[:rows_of(tiles[t]), t % 2], residual(tiles[t])).then_inc(rin[t % 2], 16)

        if norm:
            @block.gpsimd
            def _(pool):
                pool.wait_ge(params, 32)
                for t in range(TN):
                    r = rows_of(tiles[t])
                    pool.wait_ge(scaled, t + 1)
                    if t >= 2:
                        pool.wait_ge(kept[t % 2], 16 * (t // 2))
                        if not last:
                            pool.wait_ge(turned, t - 1)
                    nc.gpsimd.tensor_tensor(done[:r, t % 2], summed[:r, t % 2], shifts[:r], ALU.add).then_inc(shifted, 1)
                    pool.wait_ge(shifted, t + 1)
                    pool.dma_start(keep(tiles[t]), done[:r, t % 2]).then_inc(kept[t % 2], 16)
                for s in range(2):
                    pool.wait_ge(kept[s], 16 * ((TN + 1 - s) // 2))

        @block.tensor
        def _(pe):
            def feed(t):
                r = rows_of(tiles[t])
                if t >= 2:
                    pe.wait_ge(vec, 1 + 6 * (t - 2))
                for j in range(KT):
                    mm = nc.tensor.transpose(up[:r, t % 2, j // 4, j % 4 * P:(j % 4 + 1) * P],
                                             y[:, j, grp.at(tiles[t])], ident[:])
                mm.then_inc(fed, 1)

            def turn(t):
                r = rows_of(tiles[t])
                if norm:
                    pe.wait_ge(shifted, t + 1)
                elif source == "rows":
                    pe.wait_ge(rin[t % 2], 16 * (t // 2 + 1))
                if t >= 2:
                    pe.wait_ge(low, t - 1)
                for j in range(KT):
                    mm = nc.tensor.transpose(back[:, t % 2, j // 4, j % 4 * P:j % 4 * P + r],
                                             src(t)[:r, j * P:(j + 1) * P], ident[:r, :r])
                mm.then_inc(turned, 1)

            for t in range(TN + 1):
                if norm and t < TN:
                    feed(t)
                if not last and t >= 1:
                    turn(t - 1)

        def fm(x, t):
            return x[:, :, grp.at(tiles[t])].rearrange("p (a b) n -> p a b n", a=2)

        def bank(t):
            r = rows_of(tiles[t])
            return back[:, t % 2].rearrange("p a (b n) -> p a b n", n=P)[:, :, :, :r]

        @block.scalar
        def _(act):
            for t in range(TN + 1):
                if norm and t < TN:
                    r, s = rows_of(tiles[t]), t % 2
                    act.wait_ge(centred, 2 * t + 1)
                    nc.scalar.activation(small[:r, s, 1:2], small[:r, s, 0:1], ACT.Sqrt).then_inc(root, 1)
                    act.wait_ge(centred, 2 * t + 2)
                    nc.scalar.mul(summed[:r, s], cent[:r, s], small[:r, s, 2:3]).then_inc(scaled, 1)
                if not last and t >= 1:
                    act.wait_ge(turned, t)
                    nc.scalar.copy(fm(xh, t - 1), bank(t - 1)).then_inc(high, 1)

        @block.vector
        def _(dve):
            for t in range(TN + 2):
                if norm and t < TN:
                    r, s = rows_of(tiles[t]), t % 2
                    dve.wait_ge(fed, t + 1)
                    dve.wait_ge(rin[s], 16 * (t // 2 + 1))
                    if t >= 2:
                        dve.wait_ge(shifted, t - 1)
                    nc.vector.scalar_tensor_tensor(out=summed[:r, s], in0=rows[:r, s], scalar=ALPHA,
                                                   in1=up[:r, s].rearrange("p a b -> p (a b)"), op0=ALU.mult,
                                                   op1=ALU.add).then_inc(vec, 1)
                    dve.wait_ge(vec, 6 * t + 1)
                    for c in range(2):
                        nc.vector.bn_stats(stats[:r, s, c], summed[:r, s, c * 512:(c + 1) * 512]).then_inc(vec, 1)
                    dve.wait_ge(vec, 6 * t + 3)
                    nc.vector.bn_aggr(mv[:r, s], stats[:r, s].rearrange("p a b -> p (a b)")).then_inc(vec, 1)
                    dve.wait_ge(vec, 6 * t + 4)
                    nc.vector.tensor_scalar_add(small[:r, s, 0:1], mv[:r, s, 1:2], LN_EPS).then_inc(centred, 1)
                    if t == 0:
                        dve.wait_ge(params, 32)
                    if t >= 2:
                        dve.wait_ge(scaled, t - 1)
                    nc.vector.scalar_tensor_tensor(out=cent[:r, s], in0=summed[:r, s], scalar=mv[:r, s, 0:1],
                                                   in1=gains[:r], op0=ALU.subtract, op1=ALU.mult).then_inc(vec, 1)
                    dve.wait_ge(root, t + 1)
                    nc.vector.reciprocal(small[:r, s, 2:3], small[:r, s, 1:2]).then_inc(vec, 1)
                    dve.wait_ge(vec, 6 * t + 6)
                    dve.sem_inc(centred, 1)
                if not last and t >= 2:
                    dve.wait_ge(high, t - 1)
                    nc.vector.tensor_tensor(fm(xl, t - 2), bank(t - 2), fm(xh, t - 2).bitcast(F32),
                                            ALU.subtract).then_inc(low, 1)


def weight_slots(ph):
    raw = ph.sb("raw", [P, 2, D])
    wh = ph.sb("wh", [P, 2, D], F32R)
    wl = ph.sb("wl", [P, 2, D], F32R)
    return raw, wh, wl, [ph.sem(f"weights_in{s}") for s in range(2)], ph.sem("weights_high"), ph.sem("weights_low")


def project(nc, name, grp, xh, xl, weights, ident=None, first=0, blocks=KT, last_cols=P, y=None, fm=None, turns=None,
            beside=None):
    wv = weights.rearrange("(k p) n -> p k n", p=P)
    NB, G = grp.banks, grp.g
    with Phase(nc, name) as ph:
        raw, wh, wl, win, high, low = weight_slots(ph)
        multiplied, taken = ph.sem("multiplied"), ph.sem("taken")
        acc = ph.ps("acc", [P, 2, NB, 512])
        if y is None:
            stage = ph.sb("stage", [P, 2, TOK])
            stored = [ph.sem(f"stored{s}") for s in range(2)]
            group, staged = ph.sem("group"), ph.sem("staged")
            turned, rowed, passed = ph.sem("turned"), ph.sem("rowed"), ph.sem("passed")
            tstage = ph.sb("tstage", [P, 2, TT, P])
            tstored = [ph.sem(f"tstored{s}") for s in range(2)]
            tb = beside.dots if beside else ph.ps("tb", [P, 2, 512])
        segments, at, so_far = [], 0, 0
        if beside:
            segments.append((0, beside.blocks, None, 0))
            at = beside.blocks
        for turn0, count, stores in turns or []:
            if turn0 > at:
                segments.append((at, turn0 - at, None, 0))
            segments.append((turn0, count, stores, so_far - turn0))
            at, so_far = turn0 + count, so_far + count
        if at < blocks:
            segments.append((at, blocks - at, None, 0))

        def over(engine, first, count, step):
            if beside and first < beside.blocks:
                for n in range(first, first + count):
                    step(n, n % 2)
            else:
                in_pairs(engine, first, count, step)

        block = ph.block()

        def load(sp, n, s):
            sp.wait_ge(low, n + 1)
            if isinstance(n, int) and n == blocks - 1 and last_cols < P:
                at = (first + n) * P
                sp.dma_start(raw[:, s].rearrange("p (k n) -> p k n", k=KT)[:, :, 0:last_cols],
                             wv[:, :, at:at + last_cols]).then_inc(win[s], 16)
            else:
                sp.dma_start(raw[:, s].rearrange("p (k n) -> p k n", k=KT),
                             wv[:, :, bass.ds((n + first) * P, P)]).then_inc(win[s], 16)

        @block.sync
        def _(sp):
            if y is not None:
                in_pairs(sp, 0, blocks, lambda n, s: load(sp, n, s))
                return
            load(sp, 0, 0)
            load(sp, 1, 1)
            whole = blocks - (last_cols < P)
            row_stores = [0, 0]
            for seg0, count, stores, m_less_n in segments:
                def step(n, s):
                    sp.wait_ge(taken, n + 3)
                    rows = bass.ds((n + first) * P, P)
                    sp.dma_start(fm[rows, 0:SEQ], stage[:, s, 0:SEQ]).then_inc(stored[s], 16)
                    sp.dma_start(fm[rows, SN:KEYS], stage[:, s, SEQ:TOK]).then_inc(stored[s], 16)
                    if not isinstance(n, int) or n + 2 < blocks:
                        load(sp, n + 2, s)
                    if stores:
                        m = n + m_less_n
                        ms = m % 2 if isinstance(m, int) else s
                        wait_apart(sp, rowed, m * 3 + 4, passed)
                        for out, part in stores(n):
                            row_stores[ms] += 16
                            sp.dma_start(out, part(tstage[:, ms])).then_inc(tstored[ms], 16)

                regular = min(count, max(0, whole - 2 - seg0)) // 2 * 2
                before = list(row_stores)
                in_pairs(sp, seg0, regular, step)
                if regular >= 4:
                    row_stores[:] = [b + (r - b) * (regular // 2) for b, r in zip(before, row_stores)]
                for n in range(seg0 + regular, seg0 + count):
                    step(n, n % 2)
            for s in range(2):
                sp.wait_ge(stored[s], 32 + 32 * ((blocks + 1 - s) // 2))
                if row_stores[s]:
                    sp.wait_ge(tstored[s], 32 + row_stores[s])

        @block.gpsimd
        def _(pool):
            pool.sem_inc(low, 2)

            def split_low(n, s):
                pool.wait_ge(high, n + 1)
                nc.gpsimd.tensor_tensor(wl[:, s], raw[:, s], wh[:, s].bitcast(F32), ALU.subtract).then_inc(low, 1)

            if not beside:
                in_pairs(pool, 0, blocks, split_low)
                return
            split_low(0, 0)
            for n in range(beside.blocks):
                split_low(n + 1, (n + 1) % 2)
                for u in beside.units(n):
                    beside.add(pool, u)
            for n in range(beside.blocks + 1, blocks):
                split_low(n, n % 2)

        @block.tensor
        def _(pe):
            pe.sem_inc(multiplied, 2)
            if beside:
                beside.begin(pe)

            def multiply(n, s):
                pe.wait_ge(low, n + 3)
                pe.wait_ge(taken, n + 1)
                units = list(beside.units(n)) if beside and isinstance(n, int) else []
                done, every = 0, NB * KT // max(1, len(units))
                for g in range(NB):
                    for k in range(KT):
                        for part, (w, x) in enumerate(((wh, xh), (wh, xl), (wl, xh))):
                            mm = nc.tensor.matmul(acc[:, s, g, 0:G], w[:, s, k * P:(k + 1) * P],
                                                  x[:, k, g * G:(g + 1) * G], start=k == 0 and part == 0,
                                                  stop=k == KT - 1 and part == 2)
                        if k == KT - 1:
                            if g < NB - 1 and y is None:
                                mm.then_inc(group, 1)
                            if g == NB - 1:
                                mm.then_inc(multiplied, 1)
                        done += 1
                        if units and done % every == 0:
                            beside.score(pe, units.pop(0))
                for u in units:
                    beside.score(pe, u)

            def turn(n, s, m):
                if beside and isinstance(m, int) and m == 0:
                    beside.end(pe)
                for t in range(TT):
                    if t == 0:
                        pe.wait_ge(staged, n * 2 + 2)
                        pe.wait_ge(rowed, m * 3 + 1)
                    if t == 5:
                        pe.wait_ge(taken, n + 3)
                    if t == ST:
                        pe.wait_ge(rowed, m * 3 + 2)
                    r = rows_of(t)
                    mm = nc.tensor.transpose(tb[:r, t // 4 % 2, t % 4 * P:(t % 4 + 1) * P],
                                             stage[:, s, t * P:t * P + r], ident[:])
                    if t in (3, 7, 8):
                        mm.then_inc(turned, 1)

            for seg0, count, stores, m_less_n in segments:
                if beside and stores:
                    beside.end(pe)

                def step(n, s):
                    multiply(n, s)
                    if stores:
                        turn(n, s, n + m_less_n)
                over(pe, seg0, count, step)

        def split_high(act, n, s):
            act.wait_ge(win[s], n // 2 * 16 + 16 if isinstance(n, int) else (n - s) * 8 + 16)
            act.wait_ge(multiplied, n + 1)
            nc.scalar.copy(wh[:, s], raw[:, s]).then_inc(high, 1)

        def take(engine, copy, n, s, stores, m_less_n):
            engine.wait_ge(stored[s], n // 2 * 32 + 32 if isinstance(n, int) else (n - s) * 16 + 32)
            for g in range(NB):
                if g < NB - 1:
                    engine.wait_ge(group, n * 2 + g + 1)
                else:
                    engine.wait_ge(multiplied, n + 3)
                copy(stage[:, s, g * G:(g + 1) * G], acc[:, s, g, 0:G]).then_inc(staged if g < NB - 1 else taken, 1)
            if stores:
                m = n + m_less_n
                ms = m % 2 if isinstance(m, int) else s
                engine.wait_ge(tstored[ms], m // 2 * 32 + 32 if isinstance(m, int) else (m - ms) * 16 + 32)
                for i, (a, b) in enumerate(((0, 4), (4, 8), (8, 9))):
                    engine.wait_ge(turned, m * 3 + i + 1)
                    r = rows_of(a)
                    copy(tstage[:r, ms, a:b, :], tb[:r, i % 2, 0:(b - a) * P].rearrange("p (a n) -> p a n", n=P)
                         ).then_inc(rowed, 1)

        def start_stages(engine):
            engine.sem_inc(rowed, 1)
            for s in range(2):
                engine.sem_inc(stored[s], 32)
                engine.sem_inc(tstored[s], 32)

        @block.scalar
        def _(act):
            if not beside:
                in_pairs(act, 0, blocks, lambda n, s: split_high(act, n, s))
                return
            act.sem_inc(taken, 2)
            start_stages(act)
            split_high(act, 0, 0)
            for n in range(blocks):
                stores, m_less_n = next((x[2], x[3]) for x in segments if x[0] <= n < x[0] + x[1])
                if n + 1 < blocks:
                    split_high(act, n + 1, (n + 1) % 2)
                for u in beside.units(n):
                    beside.weigh(act, u)
                take(act, nc.scalar.copy, n, n % 2, stores, m_less_n)

        @block.vector
        def _(dve):
            if beside:
                beside.choose(dve)
                return
            dve.sem_inc(taken, 2)
            if y is not None:
                def take_y(n, s):
                    dve.wait_ge(multiplied, n + 3)
                    nc.vector.tensor_copy(y[:, bass.ds(n, 1), :].rearrange("p a (g n) -> p (a g) n", g=NB),
                                          acc[:, s, :, 0:G]).then_inc(taken, 1)
                in_pairs(dve, 0, blocks, take_y)
                return
            start_stages(dve)
            for seg0, count, stores, m_less_n in segments:
                in_pairs(dve, seg0, count, lambda n, s: take(dve, nc.vector.tensor_copy, n, s, stores, m_less_n))


def turn_caches(nc, ident, jobs):
    with Phase(nc, "caches") as ph:
        cin, stored = ph.sem("rows_in"), [ph.sem(f"stored{s}") for s in range(2)]
        turned, copied = ph.sem("turned"), ph.sem("copied")
        tiles = [ph.sb(f"rows{j}", [P, PAST // P, rows.shape[1] * rows.shape[2]]) for j, (rows, _, _) in enumerate(jobs)]
        stage = ph.sb("stage", [P, 2, PAST])
        bank = ph.ps("bank", [P, 2, 512])
        heads = [(j, h, rows.shape[2], fm, row0 + h * rows.shape[2])
                 for j, (rows, fm, row0) in enumerate(jobs) for h in range(rows.shape[1])]
        block = ph.block()

        @block.sync
        def _(sp):
            for j, (rows, _, _) in enumerate(jobs):
                sp.dma_start(tiles[j][:], rows.rearrange("(t p) h d -> p t (h d)", p=P)).then_inc(cin, 16)
            for n, (j, h, w, fm, row) in enumerate(heads):
                sp.wait_ge(copied, n + 1)
                sp.dma_start(fm[row:row + w, S0:SN], stage[:w, n % 2]).then_inc(stored[n % 2], 16)
            for s in range(2):
                sp.wait_ge(stored[s], 16 * ((len(heads) + 1 - s) // 2))

        @block.tensor
        def _(pe):
            pe.wait_ge(cin, 16 * len(jobs))
            for n, (j, h, w, _, _) in enumerate(heads):
                if n >= 2:
                    pe.wait_ge(copied, n - 1)
                for t in range(PAST // P):
                    mm = nc.tensor.transpose(bank[:w, n % 2, t * P:(t + 1) * P], tiles[j][:, t, h * w:(h + 1) * w],
                                             ident[:])
                mm.then_inc(turned, 1)

        @block.scalar
        def _(act):
            for n, (j, h, w, _, _) in enumerate(heads):
                act.wait_ge(turned, n + 1)
                if n >= 2:
                    act.wait_ge(stored[n % 2], n // 2 * 16)
                nc.scalar.copy(stage[:w, n % 2], bank[:w, n % 2]).then_inc(copied, 1)


class Indexer:

    TILES = [2, ST, 3, 4, 5, 6, 7]
    LATE_FROM = 4
    Q0 = 2 * P
    QN = SEQ - Q0
    QC = QN + P
    blocks = 8

    def __init__(self, nc, keep, bias):
        self.nc, self.bias = nc, bias
        self.minus = keep.sb("minus", [P, SEQ])
        self.left = keep.sb("left", [P, SEQ])
        self.best = keep.sb("best", [P, 8])
        self.added, self.step, self.passed, self.measured, self.chosen = (
            keep.sem(n) for n in ("added", "step", "passed", "measured", "chosen"))
        self.steps = Counted(self.step)
        self.list = [(i, t, h) for i, t in enumerate(self.TILES) for h in range(IDX_H)]

    def units(self, block):
        each = len(self.list) // self.blocks
        return range(block * each, (block + 1) * each) if block < self.blocks else ()

    def q_of(self, t):
        return self.QN if t == ST else t * P - self.Q0

    def distance(self, t):
        at = (ST - 1) * P - (PAST if t == ST else t * P)
        return self.minus[:, at:at + width_of(t)]

    def prepare(self, ph, fm, wtok):
        nc, QN, QC = self.nc, self.QN, self.QC
        self.qhl = qhl = ph.sb("qhl", [P, IDX_H, QC], F32R)
        self.khh = khh = ph.sb("khh", [P, KEYS], F32R)
        self.kll = kll = ph.sb("kll", [P, KEYS], F32R)
        self.w = w = ph.sb("w", [P, TT, IDX_H])
        with Phase(nc, "ready") as p:
            qraw = p.sb("qraw", [P, IDX_H, QN + NEW])
            qtmp = p.sb("qtmp", [P, 2, QN + NEW])
            kraw = p.sb("kraw", [P, KEYS])
            wraw = p.sb("wraw", [P, TT, IDX_H])
            q_in, k_in, w_in = p.sem("q_in"), p.sem("k_in"), p.sem("w_in")
            cleared, qcopied, khigh, wscaled = (p.sem(n) for n in ("cleared", "qcopied", "khigh", "wscaled"))
            qready, kready, numbered = (p.sem(n) for n in ("qready", "kready", "numbered"))
            offset = self.left[:].bitcast(mybir.dt.int32)
            minus, left, measured = self.minus, self.left, self.measured
            block = p.block()

            @block.sync
            def _(sp):
                qrows = fm[A_QI * P:(A_QI + 4) * P].rearrange("(h d) c -> d h c", d=IDX_D)
                krows = fm[A_KI * P:A_KI * P + IDX_D]
                for half in range(2):
                    at = slice(half * 64, half * 64 + 64)
                    sp.dma_start(kraw[at], krows).then_inc(k_in, 16)
                    sp.dma_start(qraw[at, :, 0:QN], qrows[:, :, self.Q0:SEQ]).then_inc(q_in, 16)
                    sp.dma_start(qraw[at, :, QN:QN + NEW], qrows[:, :, SN:KEYS]).then_inc(q_in, 16)
                sp.wait_ge(cleared, 2)
                sp.dma_start(wraw[:, 0:ST], wtok[0:SEQ].rearrange("(t p) h -> p t h", p=P)).then_inc(w_in, 16)
                sp.dma_start(wraw[:NEW, ST], wtok[SEQ:TOK]).then_inc(w_in, 16)

            @block.gpsimd
            def _(pool):
                nc.gpsimd.memset(wraw[:, ST], 0.0).then_inc(cleared, 1)
                nc.gpsimd.memset(qhl[:, :, QN + NEW:QC].bitcast(F32), 0.0).then_inc(cleared, 1)
                nc.gpsimd.iota(offset, pattern=[[-1, SEQ]], base=(ST - 1) * P, channel_multiplier=1
                               ).then_inc(numbered, 1)
                pool.wait_ge(khigh, 1)
                nc.gpsimd.tensor_tensor(kll[:], kraw[:], khh[:].bitcast(F32), ALU.subtract).then_inc(kready, 1)
                pool.wait_ge(kready, 1)

            @block.scalar
            def _(act):
                act.wait_ge(k_in, 32)
                nc.scalar.copy(khh[:], kraw[:]).then_inc(khigh, 1)
                act.wait_ge(w_in, 32)
                nc.scalar.mul(w[:].rearrange("p a b -> p (a b)"), wraw[:].rearrange("p a b -> p (a b)"), IDX_SCALE
                              ).then_inc(wscaled, 1)
                act.wait_ge(wscaled, 1)
                act.wait_ge(q_in, 64)
                for h in range(IDX_H):
                    if h >= 2:
                        act.wait_ge(qready, h - 1)
                    nc.scalar.copy(qtmp[64:128, h % 2].bitcast(F32R), qraw[64:128, h]).then_inc(qcopied, 1)
                    nc.scalar.copy(qhl[0:64, h, 0:QN + NEW], qraw[0:64, h]).then_inc(qcopied, 1)
                act.wait_ge(qcopied, 2 * IDX_H)

            @block.vector
            def _(dve):
                dve.wait_ge(numbered, 1)
                nc.vector.tensor_copy(minus[:], offset).then_inc(measured, 1)
                dve.wait_ge(measured, 1)
                nc.vector.tensor_scalar(left[:], minus[:], -1.0, None, ALU.mult).then_inc(measured, 1)
                dve.wait_ge(measured, 2)
                nc.vector.tensor_tensor(minus[:], minus[:], left[:], ALU.min).then_inc(measured, 1)
                for h in range(IDX_H):
                    dve.wait_ge(qcopied, 2 * h + 1)
                    nc.vector.tensor_tensor(qhl[64:128, h, 0:QN + NEW], qraw[64:128, h], qtmp[64:128, h % 2],
                                            ALU.subtract).then_inc(qready, 1)
                dve.wait_ge(qready, IDX_H)
                dve.wait_ge(measured, 3)

    def mix_into(self, ph):
        self.rel = ph.sb("rel", [P, 2, SEQ])
        self.dots = ph.ps("dots", [P, 2, 512])
        self.multiplied, self.rectified, self.weighted = (ph.sem(n) for n in ("dotted", "rectified", "weighted"))

    def begin(self, pe):
        pass

    def end(self, pe):
        pe.wait_ge(self.rectified, len(self.list))

    def score(self, pe, n):
        i, t, h = self.list[n]
        wd, k0, q = width_of(t), key0_of(t), self.q_of(t)
        if n >= 1:
            pe.wait_ge(self.rectified, n)
        for a in range(0, wd, 512):
            b = min(a + 512, wd)
            for part, k in enumerate((self.khh, self.kll)):
                mm = self.nc.tensor.matmul(self.dots[:, a // 512, 0:b - a], self.qhl[:, h, q:q + P],
                                           k[:, k0 + a:k0 + b], start=part == 0, stop=part == 1)
        mm.then_inc(self.multiplied, 1)

    def weigh(self, act, n):
        i, t, h = self.list[n]
        rel = self.rel[:, n % 2, 0:width_of(t)]
        act.wait_ge(self.multiplied, n + 1)
        if n >= 2:
            act.wait_ge(self.added, n - 1)
        self.nc.scalar.activation(rel, self.dots[:].rearrange("p a b -> p (a b)")[:, 0:width_of(t)], ACT.Relu
                                  ).then_inc(self.rectified, 1)
        act.wait_ge(self.rectified, n + 1)
        self.nc.scalar.mul(rel, rel, self.w[:, t, h:h + 1]).then_inc(self.weighted, 1)

    def add(self, pool, n):
        i, t, h = self.list[n]
        rel, score = self.rel[:, n % 2, 0:width_of(t)], self.bias[t]
        pool.wait_ge(self.weighted, n + 1)
        if h == 0:
            self.nc.gpsimd.tensor_copy(score, rel).then_inc(self.added, 1)
        else:
            pool.wait_ge(self.added, n)
            self.nc.gpsimd.tensor_tensor(score, score, rel, ALU.add).then_inc(self.added, 1)

    def choose(self, dve):
        nc, steps = self.nc, self.steps
        for t in (0, 1):
            steps.up(nc.vector.tensor_copy(self.bias[t], self.distance(t)))
            dve.wait_ge(self.step, steps.n)
            steps.up(nc.vector.memset(self.bias[t][0:CHUNK, width_of(t) - CHUNK:width_of(t)], -BIG))
        for i in range(self.LATE_FROM):
            self.choose_tile(dve, i)

    def choose_late(self, dve):
        for i in range(self.LATE_FROM, len(self.TILES)):
            self.choose_tile(dve, i)

    def choose_tile(self, dve, i):
        nc, steps, step, best = self.nc, self.steps, self.step, self.best
        t = self.TILES[i]
        wd = width_of(t)
        scores, rest = self.bias[t], self.left[:, 0:wd]
        dve.wait_ge(self.added, IDX_H * (i + 1))
        if t != ST:
            steps.up(nc.vector.memset(scores[0:CHUNK, wd - CHUNK:wd], BARRED))
            dve.wait_ge(step, steps.n)
        steps.up(nc.vector.max(best[:], scores))
        dve.wait_ge(step, steps.n)
        steps.up(nc.vector.match_replace(rest, best[:], scores, TAKEN))
        rounds = (TOPK_STREAM if t == ST else TOPK) // 8 - 1
        n0 = steps.n
        with dve.Fori(0, rounds) as r:
            wait_apart(dve, step, r * 2 + n0, self.passed)
            nc.vector.max(best[:], rest).then_inc(step, 1)
            wait_apart(dve, step, r * 2 + n0 + 1, self.passed)
            nc.vector.match_replace(rest, best[:], rest, TAKEN).then_inc(step, 1)
        steps.n += 2 * rounds
        dve.wait_ge(step, steps.n)
        steps.up(nc.vector.tensor_tensor(rest, rest, scores, ALU.not_equal))
        dve.wait_ge(step, steps.n)
        steps.up(nc.vector.tensor_scalar(rest, rest, BIG, -BIG, ALU.mult, ALU.add))
        dve.wait_ge(step, steps.n)
        nc.vector.tensor_tensor(self.bias[t], rest, self.distance(t), ALU.add).then_inc(self.chosen, 1)
        dve.wait_ge(self.chosen, i + 1)


def forget_gates(nc, ident, fm, b_f, cache_logf, out_prompt, out_sample, minus_c, ctok):
    with Phase(nc, "forget") as ph:
        f = ph.sb("f", [HEADS, TOK])
        bf = ph.sb("bf", [HEADS, 1])
        z, e, u, d, lnu, r, logf = (ph.sb(n, [HEADS, TOK]) for n in ("z", "e", "u", "d", "lnu", "r", "logf"))
        stream = ph.sb("stream", [HEADS, PAST + NEW])
        ones = ph.sb("ones", [HEADS, SEQ])
        c = ph.sb("c", [HEADS, KEYS])
        mc = ph.sb("mc", [HEADS, KEYS])
        ltok = ph.sb("ltok", [P, TT, HEADS])
        bank = ph.ps("bank", [P, 2, 512])
        fin, step, turned, copied, stored = (ph.sem(n) for n in ("f_in", "step", "turned", "copied", "stored"))
        acts = ph.sem("acts")
        block = ph.block()

        @block.sync
        def _(sp):
            sp.dma_start(f[:, 0:SEQ], fm[0:HEADS, 0:SEQ]).then_inc(fin, 16)
            sp.dma_start(f[:, SEQ:TOK], fm[0:HEADS, SN:KEYS]).then_inc(fin, 16)
            sp.dma_start(bf[:], b_f).then_inc(fin, 16)
            with nc.allow_non_contiguous_dma("512 by 8 values"):
                sp.dma_start(stream[:, 0:PAST], cache_logf.rearrange("s h -> h s")).then_inc(fin, 16)
            sp.wait_ge(copied, 3)
            sp.dma_start(minus_c, mc[:]).then_inc(stored, 16)
            sp.dma_start(out_prompt.rearrange("(t p) h -> p t h", p=P), ltok[:, 0:ST]).then_inc(stored, 16)
            sp.dma_start(out_sample, ltok[:NEW, ST]).then_inc(stored, 16)
            sp.wait_ge(stored, 48)

        @block.scalar
        def _(act):
            act.wait_ge(step, 4)
            nc.scalar.activation(e[:], e[:], ACT.Exp, scale=-1.0).then_inc(acts, 1)
            act.wait_ge(step, 6)
            nc.scalar.activation(lnu[:], u[:], ACT.Ln).then_inc(acts, 1)

        @block.vector
        def _(dve):
            s = Counted(step)

            def then(instruction):
                s.up(instruction)
                dve.wait_ge(step, s.n)

            then(nc.vector.memset(ones[:], 1.0))
            nc.vector.memset(ctok[:, ST], 0.0)
            dve.wait_ge(fin, 64)
            then(nc.vector.tensor_scalar(z[:], f[:], bf[:], None, ALU.add))
            then(nc.vector.tensor_scalar(e[:], z[:], -1.0, None, ALU.mult))
            then(nc.vector.tensor_tensor(e[:], e[:], z[:], ALU.max))
            dve.wait_ge(acts, 1)
            then(nc.vector.tensor_scalar_min(z[:], z[:], 0.0))
            then(nc.vector.tensor_scalar_add(u[:], e[:], 1.0))
            then(nc.vector.tensor_scalar(d[:], u[:], -1.0, 1e-30, ALU.add, ALU.max))
            then(nc.vector.reciprocal(r[:], d[:]))
            then(nc.vector.tensor_tensor(r[:], r[:], e[:], ALU.mult))
            dve.wait_ge(acts, 2)
            then(nc.vector.tensor_scalar(d[:], u[:], 1.0, None, ALU.is_equal))
            then(nc.vector.tensor_tensor(d[:], d[:], e[:], ALU.mult))
            then(nc.vector.tensor_scalar(u[:], u[:], 1.0, None, ALU.is_gt))
            then(nc.vector.tensor_tensor(u[:], u[:], r[:], ALU.mult))
            then(nc.vector.tensor_tensor(u[:], u[:], lnu[:], ALU.mult))
            then(nc.vector.tensor_tensor(u[:], u[:], d[:], ALU.add))
            then(nc.vector.tensor_tensor(logf[:], z[:], u[:], ALU.subtract))
            then(nc.vector.tensor_copy(stream[:, PAST:], logf[:, SEQ:TOK]))
            then(nc.vector.tensor_tensor_scan(c[:, 0:SEQ], ones[:], logf[:, 0:SEQ], 0.0, ALU.mult, ALU.add))
            then(nc.vector.tensor_tensor_scan(c[:, S0:KEYS], ones[:, 0:PAST + NEW], stream[:], 0.0, ALU.mult, ALU.add))
            dve.sem_inc(turned, 1)
            nc.vector.tensor_scalar(mc[:], c[:], -1.0, None, ALU.mult).then_inc(copied, 1)
            dve.wait_ge(turned, 2)
            for n, to in enumerate((ltok, ctok)):
                nc.vector.tensor_copy(to[:, 0:ST], bank[:, n, 0:ST * HEADS].rearrange("p (t h) -> p t h", h=HEADS)
                                      ).then_inc(step, 1)
                nc.vector.tensor_copy(to[:NEW, ST], bank[:NEW, n, ST * HEADS:TT * HEADS]).then_inc(copied, 1)
            dve.wait_ge(copied, 3)

        @block.tensor
        def _(pe):
            pe.wait_ge(turned, 1)
            for n in range(2):
                for t in range(TT):
                    r_ = rows_of(t)
                    src = (logf[:, t * P:t * P + r_] if n == 0 else
                           c[:, SN:KEYS] if t == ST else c[:, t * P:(t + 1) * P])
                    mm = nc.tensor.transpose(bank[:r_, n, t * HEADS:(t + 1) * HEADS], src, ident[:HEADS, :HEADS])
            mm.then_inc(turned, 1)


def attend(nc, name, ident, grp, o, fmq, q0, fmk, v_prompt, v_past, v_new, bias=None, minus_c=None, ctok=None):
    sparse = bias is not None
    QW = (grp.cols + P - 1) // P * P
    VT = KEYS // P + 1
    order = sorted(grp.tiles, key=width_of)
    U = len(order)
    NU = 2 * U
    TS = 6
    WIDE = max(width_of(t) for t in order)
    prompt = [t for t in grp.tiles if t != ST]
    q_parts = [(slice(0, len(prompt) * P), slice(prompt[0] * P, (prompt[-1] + 1) * P))]
    if ST in grp.tiles:
        q_parts.append((grp.at(ST), slice(SN, KEYS)))
    Q, K, V = range(3)
    with Phase(nc, name) as ph:
        qraw, kraw, vraw = ph.sb("qraw", [P, grp.cols]), ph.sb("kraw", [P, KEYS]), ph.sb("vraw", [P, VT, HD])
        qh, ql = (ph.sb(n, [P, 2, QW], F32R) for n in ("qh", "ql"))
        kh, kl = (ph.sb(n, [P, 2, KEYS], F32R) for n in ("kh", "kl"))
        vh, vl = (ph.sb(n, [P, 2, VT, HD], F32R) for n in ("vh", "vl"))
        qscale, slope = ph.sb("qscale", [P, HEADS]), ph.sb("slope", [P, HEADS])
        prob = ph.sb("prob", [P, 2, WIDE])
        pth, ptl = (ph.sb(n, [P, 2, KT, P], F32R) for n in ("pth", "ptl"))
        top, shift = ph.sb("top", [P, 2]), ph.sb("shift", [P, 2])
        total, inverse = ph.sb("total", [P, TS]), ph.sb("inverse", [P, TS])
        if not sparse:
            minus = ph.sb("minus", [P, 2, KEYS])
            row_c = ph.sb("row_c", [P, 2])
            later = ph.sb("later", [P, P], F32R)
            one = ph.sb("one", [P, P], F32R)
        logits, trans, outs = ph.ps("logits", [P, 2, 2, 512]), ph.ps("trans", [P, 2, 512]), ph.ps("outs", [P, 2, 512])
        loaded, highs, lows = ([ph.sem(f"{kind}_{x}") for x in "qkv"] for kind in ("loaded", "highs", "lows"))
        c_in = [ph.sem(f"c_in{s}") for s in range(2)]
        constants, qscaled, passed = (ph.sem(n) for n in ("constants", "qscaled", "passed"))
        multiplied, biased, row_top, shifted, raised = (
            ph.sem(n) for n in ("multiplied", "biased", "row_top", "shifted", "raised"))
        turned, thigh, tlow, summed, inverted, scaled = (
            ph.sem(n) for n in ("turned", "thigh", "tlow", "summed", "inverted", "scaled"))
        CONSTANTS = 1 + 2 * (QW > grp.cols) + 2 * HEADS + 3 * (not sparse)
        loads = (16 * len(q_parts), 16, 48)

        def unit(n):
            return n % NU // U, order[n % NU % U]

        def slot(n, pair):
            if not sparse:
                return unit(n)[0]
            if isinstance(pair, int):
                return (pair + n // NU) // 2
            return 0 if n < 0 else bass.ds(pair - 1, 1)

        def part(x, at):
            return x[:, at] if isinstance(at, int) else x[:, at].rearrange("p a b -> p (a b)")

        def prepared(n, first, last):
            s, i = n // U, n % U
            if n >= NU:
                return []
            jobs = []
            if not (last and s == 1):
                if sparse and i == 1:
                    jobs = [(Q, s + 1, 1 - s)]
                elif not sparse and i in (3, 4, 5):
                    jobs = [(i - 3, s + 1, 1 - s)]
            if sparse and first and n in (4, 5):
                jobs.append((n - 3, 1, 1))
            return jobs

        def done(engine, sem, unit_no, first, u0):
            if not (first and unit_no < 0):
                engine.wait_ge(sem, u0 + unit_no + 1)

        def done_apart(engine, sem, unit_no, first, u0):
            if not (first and unit_no < 0):
                wait_apart(engine, sem, u0 + unit_no + 1, passed)

        def pairs(engine, body):
            body(0, 0, True, False)
            with engine.Fori(1, HEADS // 2 - 1) as pair:
                body(pair * NU, pair, False, False)
            body((HEADS // 2 - 1) * NU, HEADS // 2 - 1, False, True)

        block = ph.block()

        @block.sync
        def _(sp):
            def load(what, head):
                if not (isinstance(head, int) and head == 0):
                    wait_apart(sp, lows[what], head, passed)
                if what == Q:
                    for to, at in q_parts:
                        sp.dma_start(qraw[:, to], fmq[bass.ds(q0 + head * P, P), at]).then_inc(loaded[Q], 16)
                elif what == K:
                    sp.dma_start(kraw[:], fmk[bass.ds(head * P, P)]).then_inc(loaded[K], 16)
                else:
                    cols = bass.ds(head * P, P)
                    sp.dma_start(vraw[:, 0:8], v_prompt[:, cols].rearrange("(t p) d -> p t d", p=P)
                                 ).then_inc(loaded[V], 16)
                    sp.dma_start(vraw[:, 8:12], v_past[:, cols].rearrange("(t p) d -> p t d", p=P)
                                 ).then_inc(loaded[V], 16)
                    sp.dma_start(vraw[:NEW, 12], v_new[:, cols]).then_inc(loaded[V], 16)

            load(Q, 0)
            load(K, 0)
            sp.wait_ge(constants, 1)
            load(V, 0)

            def body(u0, pair, first, last):
                for s in range(2):
                    if not sparse:
                        if not first:
                            sp.wait_ge(biased, u0 + (s + 1) * U - NU)
                        sp.dma_start(minus[:, s], minus_c[bass.ds(pair * 2 + s, 1)].rearrange("a k -> (a k)")
                                     .partition_broadcast(P)).then_inc(c_in[s], 16)
                    for n in range(s * U, (s + 1) * U):
                        for what, ahead, _ in prepared(n, first, last):
                            load(what, pair * 2 + ahead)
            pairs(sp, body)

        @block.gpsimd
        def _(pool):
            nc.gpsimd.memset(vraw[:, 12], 0.0).then_inc(constants, 1)
            if QW > grp.cols:
                nc.gpsimd.memset(qh[:, :, grp.cols:QW].bitcast(F32), 0.0).then_inc(constants, 1)
                nc.gpsimd.memset(ql[:, :, grp.cols:QW].bitcast(F32), 0.0).then_inc(constants, 1)
            for h in range(HEADS):
                power = 2.0 ** (h + 1) if sparse else 1.0
                nc.gpsimd.memset(qscale[:, h:h + 1], SCALE * power).then_inc(constants, 1)
                nc.gpsimd.memset(slope[:, h:h + 1], 1.0 / power).then_inc(constants, 1)
            if not sparse:
                nc.gpsimd.memset(prob[:, 0, 0:P], 0.0).then_inc(constants, 1)
                pool.wait_ge(constants, CONSTANTS - 2)
                nc.gpsimd.affine_select(out=later[:], in_=prob[:, 0, 0:P], compare_op=ALU.is_ge, fill=-BIG, base=0,
                                        pattern=[[-1, P]], channel_multiplier=1).then_inc(constants, 1)
                nc.gpsimd.tensor_copy(one[:], ident[:]).then_inc(constants, 1)

            def low(what, head, s):
                pool.wait_ge(highs[what], head + 1)
                to, raw, high = ((ql[:, s, 0:grp.cols], qraw, qh[:, s, 0:grp.cols]), (kl[:, s], kraw, kh[:, s]),
                                 (vl[:, s], vraw, vh[:, s]))[what]
                nc.gpsimd.tensor_tensor(to, raw[:], high.bitcast(F32), ALU.subtract).then_inc(lows[what], 1)

            for what in (Q, K, V):
                low(what, 0, 0)

            def body(u0, pair, first, last):
                for n in range(NU):
                    for what, ahead, s in prepared(n, first, last):
                        low(what, pair * 2 + ahead, s)
            pairs(pool, body)

        @block.tensor
        def _(pe):
            pe.wait_ge(constants, CONSTANTS)

            def scores(n, u0, pair, first):
                s, t = unit(n)
                if n % U == 0:
                    pe.wait_ge(lows[Q], pair * 2 + s + 1)
                    if not sparse:
                        pe.wait_ge(lows[K], pair * 2 + s + 1)
                    elif n == 0:
                        pe.wait_ge(lows[K], 1 if isinstance(pair, int) and pair < 2 else
                                   2 if isinstance(pair, int) else pair)
                done(pe, biased, n - 2, first, u0)
                wd, k0, q = width_of(t), key0_of(t), slice(grp.start[t], grp.start[t] + P)
                ks = slot(n, pair)
                for a in range(0, wd, 512):
                    b = min(a + 512, wd)
                    to = logits[:, n % 2, a // 512, 0:b - a]
                    parts = ((qh, kh), (ql, kh), (qh, kl))
                    masked = not sparse and b == wd
                    for i, (x, y) in enumerate(parts):
                        mm = nc.tensor.matmul(to, x[:, s, q], part(y, ks)[:, k0 + a:k0 + b], start=i == 0,
                                              stop=i == 2 and not masked)
                    if masked:
                        m = rows_of(t)
                        mm = nc.tensor.matmul(logits[:, n % 2, a // 512, b - a - m:b - a], one[:], later[:, 0:m],
                                              start=False, stop=True)
                mm.then_inc(multiplied, 1)

            def turn(n, u0, first):
                s, t = unit(n)
                wd = width_of(t)
                done(pe, raised, n, first, u0)
                done(pe, tlow, n - 1, first, u0)
                for j, a in enumerate(range(0, wd, P)):
                    b = min(a + P, wd)
                    mm = nc.tensor.transpose(trans[:b - a, j // 4, j % 4 * P:(j % 4 + 1) * P],
                                             prob[:, n % 2, a:b], ident[:])
                mm.then_inc(turned, 1)

            def weigh(n, u0, pair, first):
                s, t = unit(n)
                wd, v0 = width_of(t), key0_of(t) // P
                if not sparse and n % U == 0:
                    pe.wait_ge(lows[V], (pair * 2 + s if n >= 0 else pair * 2 - 2 + s) + 1)
                elif sparse and n == 0:
                    pe.wait_ge(lows[V], 1 if isinstance(pair, int) and pair < 2 else
                               2 if isinstance(pair, int) else pair)
                done(pe, tlow, n, first, u0)
                done(pe, scaled, n - 2, first, u0)
                vs = slot(n, pair)
                tiles = [(j, min(P, wd - j * P)) for j in range((wd + P - 1) // P)]
                for j, m in tiles:
                    for i, (x, y) in enumerate(((pth, vh), (ptl, vh), (pth, vl))):
                        v = y[:m, vs, v0 + j]
                        if not isinstance(vs, int):
                            v = v.rearrange("p a d -> p (a d)")
                        mm = nc.tensor.matmul(outs[:, n % 2, 0:HD], x[:m, n % 2, j], v,
                                              start=j == 0 and i == 0, stop=j == len(tiles) - 1 and i == 2)
                mm.then_inc(summed, 1)

            def body(u0, pair, first, last):
                for n in range(NU + 3 if last else NU):
                    if n < NU:
                        scores(n, u0, pair, first)
                    if not (first and n < 3):
                        weigh(n - 3, u0, pair, first)
                    if n <= NU and not (first and n < 1):
                        turn(n - 1, u0, first)
            pairs(pe, body)

        @block.scalar
        def _(act):
            def high(what, head, s):
                act.wait_ge(loaded[what], head * loads[what] + loads[what])
                if what == Q:
                    nc.scalar.mul(qraw[:], qraw[:], qscale[:, bass.ds(head, 1)]).then_inc(qscaled, 1)
                    act.wait_ge(qscaled, head + 1)
                    nc.scalar.copy(qh[:, s, 0:grp.cols], qraw[:]).then_inc(highs[Q], 1)
                elif what == K:
                    nc.scalar.copy(kh[:, s], kraw[:]).then_inc(highs[K], 1)
                else:
                    nc.scalar.copy(vh[:, s], vraw[:]).then_inc(highs[V], 1)

            def raise_(n, u0, pair, first):
                s, t = unit(n)
                wd = width_of(t)
                done_apart(act, shifted, n, first, u0)
                scale = slope[:, bass.ds((pair if n >= 0 else pair - 1) * 2 + s, 1)] if sparse else 1.0
                nc.scalar.activation(prob[:, n % 2, 0:wd], prob[:, n % 2, 0:wd], ACT.Exp, scale=scale,
                                     bias=shift[:, n % 2:n % 2 + 1], accum_out=total[:, n % TS:n % TS + 1]
                                     ).then_inc(raised, 1)

            def turned_high(n, u0, first):
                s, t = unit(n)
                wd = width_of(t)
                done(act, turned, n, first, u0)
                done(act, summed, n - 2, first, u0)
                full, rest = wd // P, wd % P
                for i, a in enumerate(range(0, full, 4)):
                    b = min(a + 4, full)
                    last = nc.scalar.copy(pth[:, n % 2, a:b].rearrange("p a n -> p (a n)"),
                                          trans[:, a // 4, 0:(b - a) * P])
                if rest:
                    last = nc.scalar.copy(pth[:rest, n % 2, full], trans[:rest, full // 4, 0:P])
                last.then_inc(thigh, 1)

            act.wait_ge(constants, CONSTANTS)
            for what in (Q, K, V):
                high(what, 0, 0)

            def body(u0, pair, first, last):
                for n in range(NU + 2 if last else NU):
                    if not (first and n < 2):
                        turned_high(n - 2, u0, first)
                    if n <= NU and not (first and n < 1):
                        raise_(n - 1, u0, pair, first)
                    for what, ahead, s in prepared(n, first, last):
                        high(what, pair * 2 + ahead, s)
            pairs(act, body)

        @block.vector
        def _(dve):
            def add_bias(n, u0, pair, first):
                s, t = unit(n)
                wd, k0, b2 = width_of(t), key0_of(t), n % 2
                done_apart(dve, multiplied, n, first, u0)
                if not sparse and n % U == 0:
                    dve.wait_ge(c_in[s], pair * 16 + 16)
                done_apart(dve, turned, n - 2, first, u0)
                add = bias[t] if sparse else minus[:, s, k0:k0 + wd]
                nc.vector.tensor_tensor_reduce(out=prob[:, b2, 0:wd],
                                               in0=logits[:, b2].rearrange("p a b -> p (a b)")[:, 0:wd], in1=add,
                                               scale=1.0, scalar=-3.0e38, op0=ALU.add, op1=ALU.max,
                                               accum_out=top[:, b2:b2 + 1]).then_inc(biased, 1)
                dve.wait_ge(biased, u0 + n + 1)
                if sparse:
                    nc.vector.tensor_scalar(shift[:, b2:b2 + 1], top[:, b2:b2 + 1],
                                            slope[:, bass.ds(pair * 2 + s, 1)], -1.0, ALU.mult, ALU.mult
                                            ).then_inc(shifted, 1)
                else:
                    row = ctok[:, t, bass.ds(pair * 2 + s, 1)]
                    nc.vector.tensor_scalar(row_c[:, b2:b2 + 1], top[:, b2:b2 + 1], row, None, ALU.add
                                            ).then_inc(row_top, 1)
                    dve.wait_ge(row_top, u0 + n + 1)
                    nc.vector.tensor_scalar(shift[:, b2:b2 + 1], row_c[:, b2:b2 + 1], -1.0, row, ALU.mult, ALU.add
                                            ).then_inc(shifted, 1)

            def turned_low(n, u0, first):
                s, t = unit(n)
                wd = width_of(t)
                done(dve, thigh, n, first, u0)
                full, rest = wd // P, wd % P
                for a in range(0, full, 4):
                    b = min(a + 4, full)
                    last = nc.vector.tensor_tensor(ptl[:, n % 2, a:b].rearrange("p a n -> p (a n)"),
                                                   trans[:, a // 4, 0:(b - a) * P],
                                                   pth[:, n % 2, a:b].rearrange("p a n -> p (a n)").bitcast(F32),
                                                   ALU.subtract)
                if rest:
                    last = nc.vector.tensor_tensor(ptl[:rest, n % 2, full], trans[:rest, full // 4, 0:P],
                                                   pth[:rest, n % 2, full].bitcast(F32), ALU.subtract)
                last.then_inc(tlow, 1)

            def normalise(n, u0, pair, first):
                s, t = unit(n)
                head = (pair if n >= 0 else pair - 1) * 2 + s
                done(dve, summed, n, first, u0)
                nc.vector.reciprocal(inverse[:, n % TS:n % TS + 1], total[:, n % TS:n % TS + 1]).then_inc(inverted, 1)
                done(dve, inverted, n, first, u0)
                nc.vector.tensor_scalar(o[:, t, bass.ds(head * HD, HD)], outs[:, n % 2, 0:HD],
                                        inverse[:, n % TS:n % TS + 1], None, ALU.mult).then_inc(scaled, 1)

            def body(u0, pair, first, last):
                for n in range(NU + 4 if last else NU):
                    if n < NU + 2 and not (first and n < 2):
                        turned_low(n - 2, u0, first)
                    if not (first and n < 4):
                        normalise(n - 4, u0, pair, first)
                    if n < NU:
                        add_bias(n, u0, pair, first)
            pairs(dve, body)


def mlp(nc, name, grp, xh, xl, y, w_up, w_down, beside=None):
    UP, LOADS, BLOCKS, CHUNKS = 4, 8, 12, D_FF // 512
    NB, G = grp.banks, grp.g
    wu = w_up.rearrange("(k p) n -> p k n", p=P)
    wd = w_down.rearrange("(k p) n -> p k n", p=P)
    frees = {UP + 2 * (load - UP) + 1 if load >= UP else load: load + 2 for load in range(LOADS)}
    with Phase(nc, name) as ph:
        raw, wh, wl, win, high, low = weight_slots(ph)
        hh, hl = (ph.sb(n, [P, UP, grp.cols], F32R) for n in ("hh", "hl"))
        hidden = ph.sb("hidden", [P, 2, grp.cols])
        acc = ph.ps("acc", [P, 2, NB, 512])
        multiplied, taken = ph.sem("multiplied"), ph.sem("taken")
        cleared, squared, split, step = (ph.sem(n) for n in ("cleared", "squared", "split", "step"))
        block = ph.block()

        def chunks(engine, body):
            with engine.Fori(0, CHUNKS) as c:
                body(c)

        @block.sync
        def _(sp):
            def body(c):
                for n in range(LOADS):
                    sp.wait_ge(low, c * LOADS + n + 1)
                    if n < UP:
                        src, k = wu[:, :, bass.ds(c * 512 + n * P, P)], KT
                    else:
                        src, k = wd[:, bass.ds(c * 4, 4), (n - UP) * 256:(n - UP + 1) * 256], 4
                    sp.dma_start(raw[:, n % 2].rearrange("p (k n) -> p k n", k=k), src).then_inc(win[n % 2], 16)
            chunks(sp, body)

        def split_high(act, c, n):
            act.wait_ge(win[n % 2], c * (LOADS * 8) + n // 2 * 16 + 16)
            done = n - 1 if 2 <= n <= 5 else UP + 2 * (n - 5) if n > 5 else (-2, 0)[n]
            act.wait_ge(multiplied, c * BLOCKS + done + 3)
            nc.scalar.copy(wh[:, n % 2], raw[:, n % 2]).then_inc(high, 1)

        def split_low(pool, c, n):
            pool.wait_ge(high, c * LOADS + n + 1)
            nc.gpsimd.tensor_tensor(wl[:, n % 2], raw[:, n % 2], wh[:, n % 2].bitcast(F32), ALU.subtract
                                    ).then_inc(low, 1)

        def look_ahead(engine, split_one, after_block):
            split_one(engine, 0, 0)
            split_one(engine, 0, 1)

            def body(c, last=False):
                for n in range(BLOCKS):
                    if n in frees and not (last and frees[n] >= LOADS):
                        split_one(engine, c, frees[n])
                    after_block(c, n)
            with engine.Fori(0, CHUNKS - 1) as c:
                body(c)
            body(CHUNKS - 1, last=True)

        def per_block(h):
            return h.rearrange("p (g n) -> p g n", g=NB)

        @block.scalar
        def _(act):
            if not beside:
                def body(c):
                    for n in range(LOADS):
                        split_high(act, c, n)
                chunks(act, body)
                return
            act.sem_inc(taken, 2)

            def take(c, n):
                h, banks = hidden[:, n % 2], acc[:, n % 2, :, 0:G]
                act.wait_ge(multiplied, c * BLOCKS + n + 4)
                act.wait_ge(step, c * BLOCKS + n + 1)
                if n < UP:
                    nc.scalar.activation(per_block(h), banks, ACT.Relu).then_inc(taken, 1)
                    act.wait_ge(taken, c * BLOCKS + n + 3)
                    nc.scalar.activation(h, h, ACT.Square).then_inc(squared, 1)
                    act.wait_ge(squared, c * (UP * 2) + 2 * n + 1)
                    nc.scalar.copy(hh[:, n], h).then_inc(squared, 1)
                else:
                    nc.scalar.copy(per_block(h), banks).then_inc(taken, 1)
            look_ahead(act, split_high, take)

        @block.gpsimd
        def _(pool):
            pool.sem_inc(low, 2)
            if not beside:
                def body(c):
                    for n in range(LOADS):
                        split_low(pool, c, n)
                chunks(pool, body)
                return
            pool.sem_inc(step, 2)
            nc.gpsimd.memset(y[:, 0:KT, :], 0.0).then_inc(cleared, 1)
            pool.wait_ge(cleared, 1)

            def finish(c, n):
                h = hidden[:, n % 2]
                if n < UP:
                    pool.wait_ge(squared, c * (UP * 2) + 2 * n + 2)
                    nc.gpsimd.tensor_tensor(hl[:, n], h, hh[:, n].bitcast(F32), ALU.subtract).then_inc(split, 1)
                    pool.wait_ge(split, c * UP + n + 1)
                    pool.sem_inc(step, 1)
                else:
                    pool.wait_ge(taken, c * BLOCKS + n + 3)
                    nc.gpsimd.tensor_tensor(y[:, n - UP], y[:, n - UP], h, ALU.add).then_inc(step, 1)
            look_ahead(pool, split_low, finish)
            pool.wait_ge(step, CHUNKS * BLOCKS + 2)

        @block.tensor
        def _(pe):
            pe.sem_inc(multiplied, 3)

            def multiply(n, ks):
                up = n < UP
                load = n if up else UP + (n - UP) // 2
                last = (KT if up else 4) - 1
                for k in ks:
                    for g in range(NB):
                        at = k * P if up else k * 256 + n % 2 * P
                        w_h, w_l = (w[:, load % 2, at:at + P] for w in (wh, wl))
                        x_h, x_l = (x[:, k, g * G:(g + 1) * G] for x in ((xh, xl) if up else (hh, hl)))
                        for part, (w, x) in enumerate(((w_h, x_h), (w_h, x_l), (w_l, x_h))):
                            mm = nc.tensor.matmul(acc[:, n % 2, g, 0:G], w, x, start=k == 0 and part == 0,
                                                  stop=k == last and part == 2)
                if ks[-1] == last:
                    mm.then_inc(multiplied, 1)

            def body(c):
                for n in range(UP):
                    pe.wait_ge(low, c * LOADS + n + 3)
                    pe.wait_ge(taken, c * BLOCKS + n + 1)
                    multiply(n, range(KT))
                pe.wait_ge(low, c * LOADS + UP + 3)
                for n in (UP, UP + 1):
                    pe.wait_ge(taken, c * BLOCKS + n + 1)
                    for k in range(UP - 1):
                        if n == UP:
                            pe.wait_ge(split, c * UP + k + 1)
                        multiply(n, [k])
                pe.wait_ge(split, c * UP + UP)
                for n in (UP, UP + 1):
                    multiply(n, [UP - 1])
                for n in range(UP + 2, BLOCKS):
                    if n % 2 == 0:
                        pe.wait_ge(low, c * LOADS + UP + (n - UP) // 2 + 3)
                    pe.wait_ge(taken, c * BLOCKS + n + 1)
                    multiply(n, range(UP))
            chunks(pe, body)

        @block.vector
        def _(dve):
            if beside:
                beside(dve)
                return
            dve.sem_inc(taken, 2)
            nc.vector.memset(y[:, 0:KT, :], 0.0).then_inc(cleared, 1)
            dve.wait_ge(cleared, 1)

            def body(c):
                for n in range(BLOCKS):
                    dve.wait_ge(multiplied, c * BLOCKS + n + 4)
                    banks = acc[:, n % 2, :, 0:G]
                    if n < UP:
                        h = hidden[:, n % 2]
                        nc.vector.tensor_scalar_max(per_block(h), banks, 0.0).then_inc(taken, 1)
                        dve.wait_ge(taken, c * BLOCKS + n + 3)
                        nc.vector.tensor_tensor(h, h, h, ALU.mult).then_inc(squared, 1)
                        dve.wait_ge(squared, c * UP + n + 1)
                        nc.vector.tensor_copy(hh[:, n], h).then_inc(step, 1)
                        dve.wait_ge(step, c * UP + n + 1)
                        nc.vector.tensor_tensor(hl[:, n], h, hh[:, n].bitcast(F32), ALU.subtract).then_inc(split, 1)
                    else:
                        at = per_block(y[:, n - UP])
                        nc.vector.tensor_tensor(at, banks, at, ALU.add).then_inc(taken, 1)
            chunks(dve, body)
            dve.wait_ge(taken, CHUNKS * BLOCKS + 2)


def trunk(nc, x_prompt, x_sample, cache_a_k, cache_a_v, cache_a_kidx, cache_b_k, cache_b_v, cache_b_logf, w_a_in,
          w_a_o, w_b_kv, b_b_f, w_b_q, w_b_o, w_up, w_down, ln_g, ln_b, y_prompt, y_sample, a_k_prompt, a_v_prompt,
          a_kidx_prompt, b_k_prompt, b_v_prompt, b_logf_prompt, a_k_sample, a_v_sample, a_kidx_sample, b_k_sample,
          b_v_sample, b_logf_sample):
    def scratch(name, shape):
        return nc.dram_tensor(name, shape, F32, kind="Internal").ap()

    fm_a = scratch("fm_a", [17 * P, KEYS])
    fm_kv = scratch("fm_kv", [17 * P, KEYS])
    fm_q = scratch("fm_q", [8 * P, KEYS])
    w_rows = scratch("w_rows", [TOK, IDX_H])
    minus_c = scratch("minus_c", [HEADS, KEYS])
    x_rows = [scratch(f"x_rows{i}", [TOK, D]) for i in range(3)]

    def row_tile(prompt, stream):
        return lambda t: stream if t == ST else prompt[t * P:(t + 1) * P]

    def scratch_tile(x):
        return lambda t: x[t * P:t * P + rows_of(t)]

    flat = lambda x: x.rearrange("s h d -> s (h d)")
    ak_p, av_p, ak_s, av_s = (flat(x[0, 0]) for x in (a_k_prompt, a_v_prompt, a_k_sample, a_v_sample))
    bk_p, bv_p, bk_s, bv_s = (flat(x[0]) for x in (b_k_prompt, b_v_prompt, b_k_sample, b_v_sample))

    def to_rows(prompt, stream, block):
        at = bass.ds(block * P, P)
        return [(prompt[:, at].rearrange("(t p) n -> p t n", p=P), lambda st: st[:, 0:ST]),
                (stream[:, at], lambda st: st[:NEW, ST])]

    def last_a(_):
        k, w = slice(0, IDX_D), slice(IDX_D, IDX_D + IDX_H)
        return [(a_kidx_prompt[0, 0].rearrange("(t p) n -> p t n", p=P), lambda st: st[:, 0:ST, k]),
                (a_kidx_sample[0, 0], lambda st: st[:NEW, ST, k]),
                (w_rows[0:SEQ].rearrange("(t p) n -> p t n", p=P), lambda st: st[:, 0:ST, w]),
                (w_rows[SEQ:TOK], lambda st: st[:NEW, ST, w])]

    x_tile, y_tile = row_tile(x_prompt[0], x_sample[0]), row_tile(y_prompt[0], y_sample[0])
    k_stores = lambda n: to_rows(ak_p, ak_s, n - A_K)
    v_stores = lambda n: to_rows(av_p, av_s, n - A_V)

    def activations(p, grp):
        return p.sb("xh", [P, KT, grp.cols], F32R), p.sb("xl", [P, KT, grp.cols], F32R)

    def output_rows(p, grp):
        rows = p.sb("rows", [P, TT, D])
        y = rows[:].rearrange("p t d -> p (t d)")[:, 0:KT * grp.cols].rearrange("p (k n) -> p k n", k=KT)
        return rows, y

    def after_attention(layer, name, grp, rows, y, w_o, before, between, after, beside=None):
        with Phase(nc, f"{name}_x") as p:
            xh, xl = activations(p, grp)
            refill(nc, f"{name}_turn", ident, grp, xh, xl, "sbuf", y=rows)
            project(nc, f"{name}_out", grp, xh, xl, w_o, y=y)
            refill(nc, f"{name}_norm", ident, grp, xh, xl, "norm", residual=before, y=y, gain=ln_g[layer, 0],
                   shift=ln_b[layer, 0], keep=between)
            mlp(nc, f"{name}_mlp", grp, xh, xl, y, w_up[layer], w_down[layer], beside=beside)
            refill(nc, f"{name}_norm2", ident, grp, xh, xl, "norm", residual=between, y=y, gain=ln_g[layer, 1],
                   shift=ln_b[layer, 1], keep=after, last=True)

    with Phase(nc, "all") as ph:
        ident = ph.sb("ident", [P, P])
        ctok = ph.sb("ctok", [P, TT, HEADS])
        make_identity(nc, ident)
        turn_caches(nc, ident, [(cache_a_k[0, 0], fm_a, A_K * P), (cache_a_kidx[0, 0:1].rearrange("a s d -> s a d"),
                                                                 fm_a, A_KI * P), (cache_b_k[0], fm_kv, 0)])
        with Phase(nc, "a") as keep:
            bias = [keep.sb(f"bias{t}", [P, width_of(t)])[:] for t in range(TT)]
            indexer = Indexer(nc, keep, bias)
            with Phase(nc, "a_in") as p:
                xh, xl = activations(p, EVERY)
                refill(nc, "turn_x", ident, EVERY, xh, xl, "rows", residual=x_tile)
                project(nc, "a_index", EVERY, xh, xl, w_a_in[0], ident, first=A_QI, blocks=5, last_cols=72, fm=fm_a,
                        turns=[(4, 1, last_a)])
                indexer.prepare(p, fm_a, w_rows)
                indexer.mix_into(p)
                project(nc, "a_qkv", EVERY, xh, xl, w_a_in[0], ident, blocks=A_QI, fm=fm_a,
                        turns=[(A_K, 2, k_stores), (A_V, 2, v_stores)], beside=indexer)

            def layer_a(name, grp, beside=None):
                with Phase(nc, f"{name}_o") as p:
                    rows, y = output_rows(p, grp)
                    attend(nc, f"{name}_heads", ident, grp, rows, fm_a, A_Q * P, fm_a[A_K * P:(A_K + N_KV) * P],
                           av_p, flat(cache_a_v[0, 0]), av_s, bias=bias)
                    after_attention(0, name, grp, rows, y, w_a_o[0], x_tile, scratch_tile(x_rows[0]),
                                    scratch_tile(x_rows[1]), beside)

            layer_a("early", EARLY, indexer.choose_late)
            clear_semaphores(nc)
            layer_a("late", LATE)
        clear_semaphores(nc)
        with Phase(nc, "b_in") as p:
            xh, xl = activations(p, EVERY)
            refill(nc, "b_turn_x", ident, EVERY, xh, xl, "rows", residual=scratch_tile(x_rows[1]))
            project(nc, "b_kv", EVERY, xh, xl, w_b_kv, ident, blocks=17, last_cols=HEADS, fm=fm_kv,
                    turns=[(0, 8, lambda n: to_rows(bk_p, bk_s, n)), (8, 8, lambda n: to_rows(bv_p, bv_s, n - 8))])
            project(nc, "b_q", EVERY, xh, xl, w_b_q[0], ident, blocks=8, fm=fm_q)
        forget_gates(nc, ident, fm_kv[16 * P:17 * P], b_b_f.rearrange("(h a) -> h a", a=1), cache_b_logf[0],
                     b_logf_prompt[0], b_logf_sample[0], minus_c, ctok)
        with Phase(nc, "b_o") as p:
            rows, y = output_rows(p, EVERY)
            attend(nc, "b_heads", ident, EVERY, rows, fm_q, 0, fm_kv, bv_p, flat(cache_b_v[0]), bv_s,
                   minus_c=minus_c, ctok=ctok)
            after_attention(1, "b", EVERY, rows, y, w_b_o[0], scratch_tile(x_rows[1]), scratch_tile(x_rows[2]), y_tile)


_INS = ["x_prompt", "x_sample", "cache_a_k", "cache_a_v", "cache_a_kidx", "cache_b_k", "cache_b_v", "cache_b_logf",
        "w_a_in", "w_a_o", "w_b_kv", "b_b_f", "w_b_q", "w_b_o", "w_up", "w_down", "ln_g", "ln_b"]
_OUTS = [(1, SEQ, D), (1, NEW, D),
         (1, 1, SEQ, N_KV, HD), (1, 1, SEQ, N_KV, HD), (1, 1, SEQ, IDX_D),
         (1, SEQ, HEADS, HD), (1, SEQ, HEADS, HD), (1, SEQ, HEADS),
         (1, 1, NEW, N_KV, HD), (1, 1, NEW, N_KV, HD), (1, 1, NEW, IDX_D),
         (1, NEW, HEADS, HD), (1, NEW, HEADS, HD), (1, NEW, HEADS)]


def kernel(**inputs):
    import concourse.bacc as bacc
    from concourse.bass_utils import run_bass_kernel_spmd

    nc = bacc.Bacc("TRN2", target_bir_lowering=False, num_devices=1)
    arrays, args = {}, []
    for name in _INS:
        a = np.ascontiguousarray(inputs[name])
        arrays[f"in_{name}"] = a
        args.append(nc.dram_tensor(f"in_{name}", a.shape, mybir.dt.from_np(a.dtype), kind="ExternalInput").ap())
    for i, shape in enumerate(_OUTS):
        args.append(nc.dram_tensor(f"out_{i}", shape, F32, kind="ExternalOutput").ap())
    Phase.raised.clear()
    trunk(nc, *args)
    r = run_bass_kernel_spmd(nc, [arrays], core_ids=[0])
    return tuple(r.results[0][f"out_{i}"] for i in range(len(_OUTS)))
```

```python
from contextlib import ExitStack

import numpy as np

import concourse.bass as bass
from concourse import mybir

F32 = mybir.dt.float32
F32R = mybir.dt.float32r
ALU = mybir.AluOpType
ACT = mybir.ActivationFunctionType
AX_X = mybir.AxisListType.X

P = 128
D = 1024
KT = D // P
SEQ, NEW, PAST = 1024, 32, 512
TOK = SEQ + NEW
TT = SEQ // P + 1
ST = TT - 1
HEADS, HD = 8, 128
N_KV = 2
IDX_H, IDX_D = 8, 64
CHUNK = 64
D_FF = 4 * D
KEYS = SEQ + PAST + NEW
S0 = SEQ
SN = SEQ + PAST
TOPK = 256
TOPK_STREAM = min(TOPK, (PAST + NEW) // 4)
IDX_SCALE = (IDX_H * IDX_D) ** -0.5
SCALE = HD ** -0.5
ALPHA = 4.0 ** 0.25
LN_EPS = 1e-5
BIG = 1e30
TAKEN = -3.0e38
BARRED = -3.2e38
A_Q, A_K, A_V, A_QI, A_KI = 0, 8, 10, 12, 16


def rows_of(t):
    return NEW if t == ST else P


def width_of(t):
    return PAST + NEW if t == ST else P * (t + 1)


def key0_of(t):
    return S0 if t == ST else 0


def wait_apart(engine, sem, value, passed):
    engine.wait_ge(sem, value)
    engine.sem_inc(passed, 1)


class Group:

    def __init__(self, tiles, banks):
        self.tiles, self.banks = tiles, banks
        self.start, self.cols = {}, 0
        for t in tiles:
            self.start[t] = self.cols
            self.cols += rows_of(t)
        self.g = self.cols // banks

    def at(self, t):
        return slice(self.start[t], self.start[t] + rows_of(t))


EVERY = Group(list(range(TT)), 3)
EARLY = Group([0, 1, 2, 3, 4, ST], 2)
LATE = Group([5, 6, 7], 1)


class Counted:

    def __init__(self, sem):
        self.sem, self.n = sem, 0

    def up(self, instruction):
        self.n += 1
        instruction.then_inc(self.sem, 1)
        return self.n


def in_pairs(engine, first, count, step):
    if count >= 4:
        with engine.Fori(first // 2, (first + count) // 2) as pair:
            for s in range(2):
                step(pair * 2 + s, s)
    elif count >= 2:
        for n in range(first, first + count // 2 * 2):
            step(n, n % 2)
    if count % 2:
        step(first + count - 1, 0)


class Phase:

    raised = []

    def __init__(self, nc, name):
        self.nc, self.name, self.ctx = nc, name, ExitStack()

    def __enter__(self):
        return self

    def __exit__(self, *e):
        return self.ctx.__exit__(*e)

    def sb(self, name, shape, dt=F32):
        return self.ctx.enter_context(self.nc.sbuf_tensor(f"{self.name}_{name}", shape, dt))

    def ps(self, name, shape):
        return self.ctx.enter_context(self.nc.psum_tensor(f"{self.name}_{name}", shape, F32))

    def sem(self, name):
        handle = self.nc.alloc_semaphore(f"{self.name}_{name}")
        self.raised.append(handle)
        return handle

    def block(self):
        return self.ctx.enter_context(self.nc.Block())


def clear_semaphores(nc):
    nc.clear_and_free_semaphores(list(Phase.raised))
    Phase.raised.clear()
    nc.all_engine_barrier()


def make_identity(nc, ident):
    with Phase(nc, "ident") as ph:
        zeroed = ph.sem("zeroed")
        block = ph.block()

        @block.gpsimd
        def _(pool):
            nc.gpsimd.memset(ident[:], 0.0).then_inc(zeroed, 1)
            pool.wait_ge(zeroed, 1)
            nc.gpsimd.affine_select(out=ident[:], in_=ident[:], compare_op=ALU.not_equal, fill=1.0, base=0,
                                    pattern=[[-1, P]], channel_multiplier=1).then_inc(zeroed, 1)
            pool.wait_ge(zeroed, 2)


def refill(nc, name, ident, grp, xh, xl, source, residual=None, y=None, gain=None, shift=None, keep=None, last=False,
           ahead=None, along=None):
    tiles = grp.tiles
    TN = len(tiles)
    with Phase(nc, name) as ph:
        rin = [ph.sem(f"rows_in{s}") for s in range(2)]
        kept = [ph.sem(f"rows_kept{s}") for s in range(2)]
        turned, high, low = ph.sem("turned"), ph.sem("high"), ph.sem("low")
        back = ph.ps("back", [P, 2, 2, 512])
        norm = source == "norm"
        if source != "sbuf":
            rows = ph.sb("rows", [P, 2, D])
        if norm:
            fed, centred, scaled, shifted = (ph.sem(n) for n in ("fed", "centred", "scaled", "shifted"))
            params, vec, root = ph.sem("params"), ph.sem("vec"), ph.sem("root")
            averaged, squared, varied, inverted = (ph.sem(n) for n in ("averaged", "squared", "varied", "inverted"))
            up = ph.ps("up", [P, 2, 2, 512])
            summed = ph.sb("summed", [P, 2, D])
            cent = ph.sb("cent", [P, 2, D])
            done = ph.sb("done", [P, 2, D])
            gains = ph.sb("gains", [P, D])
            shifts = ph.sb("shifts", [P, D])
            squares = ph.sb("squares", [P, D])
            SUM, MEAN, SQUARES, VARIANCE, ROOT, INVERSE = range(6)
            small = ph.sb("small", [P, 2, 6])
        src = {"rows": lambda t: rows[:, t % 2], "sbuf": lambda t: y[:, tiles[t], :],
               "norm": lambda t: done[:, t % 2]}[source]
        ring = ahead and ahead[0]
        if ahead:
            ring.fill_from(ph, *ahead[1:])
        if along:
            along.mix_into(ph)

        def split_at(t):
            return [s for s in range(2) if ahead and t == min(2 + s, TN - 1)]

        block = ph.block()

        @block.sync
        def _(sp):
            if norm:
                sp.dma_start(gains[:], gain.partition_broadcast(P)).then_inc(params, 16)
                sp.dma_start(shifts[:], shift.partition_broadcast(P)).then_inc(params, 16)
            if ahead and source == "sbuf":
                ring.load(sp)
            if source != "sbuf":
                for t in range(TN):
                    if t >= 2:
                        sp.wait_ge(vec if norm else turned, t - 1)
                    sp.dma_start(rows[:rows_of(tiles[t]), t % 2], residual(tiles[t])).then_inc(rin[t % 2], 16)
                    if ahead and t == 1:
                        ring.load(sp)
                    if along:
                        if t == 1:
                            along.load(sp)
                        for head in along.after(t - 2):
                            along.store(sp, head)
                if along:
                    for t in (TN - 2, TN - 1):
                        for head in along.after(t):
                            along.store(sp, head)
                    along.all_stored(sp)

        if norm:
            @block.gpsimd
            def _(pool):
                pool.wait_ge(params, 32)
                for t in range(TN):
                    r = rows_of(tiles[t])
                    pool.wait_ge(scaled, t + 1)
                    if t >= 2:
                        pool.wait_ge(kept[t % 2], 16 * (t // 2))
                        if not last:
                            pool.wait_ge(turned, t - 1)
                    nc.gpsimd.tensor_tensor(done[:r, t % 2], cent[:r, t % 2], shifts[:r], ALU.add).then_inc(shifted, 1)
                    pool.wait_ge(shifted, t + 1)
                    pool.dma_start(keep(tiles[t]), done[:r, t % 2]).then_inc(kept[t % 2], 16)
                    for s in split_at(t):
                        ring.split_low(pool, s)
                for s in range(2):
                    pool.wait_ge(kept[s], 16 * ((TN + 1 - s) // 2))

        elif ahead:
            @block.gpsimd
            def _(pool):
                for s in range(2):
                    ring.split_low(pool, s)

        @block.tensor
        def _(pe):
            def feed(t):
                r = rows_of(tiles[t])
                if t >= 2:
                    pe.wait_ge(vec, t - 1)
                for j in range(KT):
                    mm = nc.tensor.transpose(up[:r, t % 2, j // 4, j % 4 * P:(j % 4 + 1) * P],
                                             y[:, j, grp.at(tiles[t])], ident[:])
                mm.then_inc(fed, 1)

            def turn(t):
                r = rows_of(tiles[t])
                if norm:
                    pe.wait_ge(shifted, t + 1)
                elif source == "rows":
                    pe.wait_ge(rin[t % 2], 16 * (t // 2 + 1))
                if t >= 2:
                    pe.wait_ge(low, t - 1)
                for j in range(KT):
                    mm = nc.tensor.transpose(back[:, t % 2, j // 4, j % 4 * P:j % 4 * P + r],
                                             src(t)[:r, j * P:(j + 1) * P], ident[:r, :r])
                mm.then_inc(turned, 1)

            if norm:
                feed(0)
            for t in range(TN + 2):
                if norm and t + 1 < TN:
                    feed(t + 1)
                if not last and 0 <= t - (2 if norm else 0) < TN:
                    turn(t - (2 if norm else 0))
                    if along:
                        for head in along.after(t):
                            along.turn(pe, head)

        def fm(x, t):
            return x[:, :, grp.at(tiles[t])].rearrange("p (a b) n -> p a b n", a=2)

        def bank(t):
            r = rows_of(tiles[t])
            return back[:, t % 2].rearrange("p a (b n) -> p a b n", n=P)[:, :, :, :r]

        LATER = 2 if norm else 0

        @block.scalar
        def _(act):
            def value(t, i):
                return small[:rows_of(tiles[t]), t % 2, i:i + 1]

            def square(t):
                r, s = rows_of(tiles[t]), t % 2
                act.wait_ge(averaged, t + 1)
                nc.scalar.activation(squares[:r], summed[:r, s], ACT.Square, bias=value(t, MEAN),
                                     accum_out=value(t, SQUARES)).then_inc(squared, 1)

            def root_of(t):
                act.wait_ge(varied, t + 1)
                nc.scalar.activation(value(t, ROOT), value(t, VARIANCE), ACT.Sqrt).then_inc(root, 1)

            def scale(t):
                r, s = rows_of(tiles[t]), t % 2
                act.wait_ge(centred, t + 1)
                act.wait_ge(inverted, t + 1)
                nc.scalar.mul(cent[:r, s], cent[:r, s], value(t, INVERSE)).then_inc(scaled, 1)

            def high_of(t):
                act.wait_ge(turned, t + 1)
                nc.scalar.copy(fm(xh, t), bank(t)).then_inc(high, 1)

            for t in range(TN + 2):
                if norm and 1 <= t <= TN:
                    root_of(t - 1)
                if norm and t < TN:
                    square(t)
                if norm and 1 <= t <= TN:
                    scale(t - 1)
                if not last and 0 <= t - LATER < TN:
                    high_of(t - LATER)
                    if along:
                        for head in along.after(t):
                            along.take(act, head)
                for s in split_at(t):
                    ring.split_high(act, s)

        @block.vector
        def _(dve):
            def low_of(t):
                dve.wait_ge(high, t + 1)
                nc.vector.tensor_tensor(fm(xl, t), bank(t), fm(xh, t).bitcast(F32), ALU.subtract).then_inc(low, 1)

            def value(t, i):
                return small[:rows_of(tiles[t]), t % 2, i:i + 1]

            for t in range(TN + 3):
                if norm and t < TN:
                    r, s = rows_of(tiles[t]), t % 2
                    dve.wait_ge(fed, t + 1)
                    dve.wait_ge(rin[s], 16 * (t // 2 + 1))
                    if t >= 2:
                        dve.wait_ge(centred, t - 1)
                    nc.vector.scalar_tensor_tensor(out=summed[:r, s], in0=rows[:r, s], scalar=ALPHA,
                                                   in1=up[:r, s].rearrange("p a b -> p (a b)"), op0=ALU.mult,
                                                   op1=ALU.add, accum_out=value(t, SUM)).then_inc(vec, 1)
                if norm and 1 <= t <= TN:
                    dve.wait_ge(squared, t)
                    nc.vector.tensor_scalar(value(t - 1, VARIANCE), value(t - 1, SQUARES), 1.0 / D, LN_EPS, ALU.mult,
                                            ALU.add).then_inc(varied, 1)
                if norm and t < TN:
                    dve.wait_ge(vec, t + 1)
                    nc.vector.tensor_scalar(value(t, MEAN), value(t, SUM), -1.0 / D, None, ALU.mult
                                            ).then_inc(averaged, 1)
                if norm and 1 <= t <= TN:
                    r1, s1 = rows_of(tiles[t - 1]), (t - 1) % 2
                    if t == 1:
                        dve.wait_ge(params, 32)
                    if t >= 3:
                        dve.wait_ge(shifted, t - 2)
                    nc.vector.scalar_tensor_tensor(out=cent[:r1, s1], in0=summed[:r1, s1], scalar=value(t - 1, MEAN),
                                                   in1=gains[:r1], op0=ALU.add, op1=ALU.mult).then_inc(centred, 1)
                    dve.wait_ge(root, t)
                    nc.vector.reciprocal(value(t - 1, INVERSE), value(t - 1, ROOT)).then_inc(inverted, 1)
                if not last and norm and t >= 3:
                    low_of(t - 3)
                if not last and not norm and 1 <= t <= TN:
                    low_of(t - 1)


class Ring:

    def __init__(self, nc, ph):
        self.nc = nc
        self.raw = ph.sb("raw", [P, 2, D])
        self.wh = ph.sb("wh", [P, 2, D], F32R)
        self.wl = ph.sb("wl", [P, 2, D], F32R)
        self.full = False

    def fill_from(self, ph, weights, first=0):
        self.first_in, self.first_high, self.first_low = (ph.sem(n) for n in ("first_in", "first_high", "first_low"))
        self.source = weights.rearrange("(k p) n -> p k n", p=P)[:, :, first * P:(first + 2) * P]

    def load(self, sp):
        for s in range(2):
            sp.dma_start(self.raw[:, s].rearrange("p (k n) -> p k n", k=KT), self.source[:, :, s * P:(s + 1) * P]
                         ).then_inc(self.first_in, 16)

    def split_high(self, act, s):
        act.wait_ge(self.first_in, 32)
        self.nc.scalar.copy(self.wh[:, s], self.raw[:, s]).then_inc(self.first_high, 1)

    def split_low(self, pool, s):
        pool.wait_ge(self.first_high, s + 1)
        self.nc.gpsimd.tensor_tensor(self.wl[:, s], self.raw[:, s], self.wh[:, s].bitcast(F32), ALU.subtract
                                     ).then_inc(self.first_low, 1)
        if s == 1:
            pool.wait_ge(self.first_low, 2)
            self.full = True

    def slots(self, ph):
        spared = 2 if self.full else 0
        self.full = False
        return (self.raw, self.wh, self.wl, [ph.sem(f"weights_in{s}") for s in range(2)], ph.sem("weights_high"),
                ph.sem("weights_low"), spared)


def project(nc, name, grp, ring, xh, xl, weights, ident=None, first=0, blocks=KT, last_cols=P, y=None, fm=None,
            turns=None, beside=None, along=None):
    wv = weights.rearrange("(k p) n -> p k n", p=P)
    NB, G = grp.banks, grp.g
    LOOK_AHEAD = 3
    with Phase(nc, name) as ph:
        raw, wh, wl, win, high, low, spared = ring.slots(ph)
        multiplied, taken = ph.sem("multiplied"), ph.sem("taken")
        acc = ph.ps("acc", [P, 2, NB, 512])
        if y is None:
            stage = ph.sb("stage", [P, 2, TOK])
            stored = [ph.sem(f"stored{s}") for s in range(2)]
            group, staged = ph.sem("group"), ph.sem("staged")
            turned, rowed, passed = ph.sem("turned"), ph.sem("rowed"), ph.sem("passed")
            tstage = ph.sb("tstage", [P, 2, TT, P])
            tstored = [ph.sem(f"tstored{s}") for s in range(2)]
            tb = beside.dots if beside else ph.ps("tb", [P, 2, 512]) if turns else None
        if along:
            along.mix_into(ph)

        def small_work(engine_name, engine, n):
            if along and (engine_name, n) in along.steps:
                along.steps[engine_name, n](engine)

        def whole_range(engine_name, engine, first, count, step):
            if not along:
                in_pairs(engine, first, count, step)
                return
            for n in range(first, first + count):
                step(n, n % 2)
                small_work(engine_name, engine, n)

        segments, at, so_far = [], 0, 0
        if beside:
            segments.append((0, beside.blocks, None, 0))
            at = beside.blocks
        for turn0, count, stores in turns or []:
            if turn0 > at:
                segments.append((at, turn0 - at, None, 0))
            segments.append((turn0, count, stores, so_far - turn0))
            at, so_far = turn0 + count, so_far + count
        if at < blocks:
            segments.append((at, blocks - at, None, 0))

        def over(engine, first, count, step):
            if along:
                whole_range("tensor", engine, 0, count, step)
            elif beside and first < beside.blocks:
                for n in range(first, first + count):
                    step(n, n % 2)
            else:
                in_pairs(engine, first, count, step)

        block = ph.block()

        def load(sp, n, s):
            sp.wait_ge(low, n + 1)
            if isinstance(n, int) and n == blocks - 1 and last_cols < P:
                at = (first + n) * P
                sp.dma_start(raw[:, s].rearrange("p (k n) -> p k n", k=KT)[:, :, 0:last_cols],
                             wv[:, :, at:at + last_cols]).then_inc(win[s], 16)
            else:
                sp.dma_start(raw[:, s].rearrange("p (k n) -> p k n", k=KT),
                             wv[:, :, bass.ds((n + first) * P, P)]).then_inc(win[s], 16)

        @block.sync
        def _(sp):
            if spared:
                for s in range(2):
                    sp.sem_inc(win[s], 16)
            if y is not None:
                in_pairs(sp, spared, blocks - spared, lambda n, s: load(sp, n, s))
                return
            for n in range(spared, 2):
                load(sp, n, n)
            small_work("sync", sp, 1)
            whole = blocks - (last_cols < P)
            row_stores = [0, 0]
            for seg0, count, stores, m_less_n in segments:
                def step(n, s):
                    sp.wait_ge(taken, n + 3)
                    rows = bass.ds((n + first) * P, P)
                    sp.dma_start(fm[rows, 0:SEQ], stage[:, s, 0:SEQ]).then_inc(stored[s], 16)
                    sp.dma_start(fm[rows, SN:KEYS], stage[:, s, SEQ:TOK]).then_inc(stored[s], 16)
                    if not isinstance(n, int) or n + 2 < blocks:
                        load(sp, n + 2, s)
                    if stores:
                        m = n + m_less_n
                        ms = m % 2 if isinstance(m, int) else s
                        wait_apart(sp, rowed, m * 3 + 4, passed)
                        for out, part in stores(n):
                            row_stores[ms] += 16
                            sp.dma_start(out, part(tstage[:, ms])).then_inc(tstored[ms], 16)

                regular = min(count, max(0, whole - 2 - seg0)) // 2 * 2
                before = list(row_stores)
                in_pairs(sp, seg0, regular, step)
                if regular >= 4:
                    row_stores[:] = [b + (r - b) * (regular // 2) for b, r in zip(before, row_stores)]
                for n in range(seg0 + regular, seg0 + count):
                    step(n, n % 2)
            for s in range(2):
                sp.wait_ge(stored[s], 32 + 32 * ((blocks + 1 - s) // 2))
                if row_stores[s]:
                    sp.wait_ge(tstored[s], 32 + row_stores[s])
            small_work("sync", sp, "end")

        @block.gpsimd
        def _(pool):
            pool.sem_inc(low, 2 + spared)

            def split_low(n, s):
                pool.wait_ge(high, n + 1)
                nc.gpsimd.tensor_tensor(wl[:, s], raw[:, s], wh[:, s].bitcast(F32), ALU.subtract).then_inc(low, 1)

            if not beside:
                in_pairs(pool, spared, blocks - spared, split_low)
                return
            if not spared:
                split_low(0, 0)
            for n in range(beside.blocks):
                for i, u in enumerate(beside.units(n)):
                    if i == LOOK_AHEAD and n + 1 >= spared:
                        split_low(n + 1, (n + 1) % 2)
                    beside.add(pool, u)
            for n in range(beside.blocks + 1, blocks):
                split_low(n, n % 2)

        @block.tensor
        def _(pe):
            pe.sem_inc(multiplied, 2)

            def multiply(n, s):
                pe.wait_ge(low, n + 3)
                pe.wait_ge(taken, n + 1)
                units = list(beside.units(n)) if beside and isinstance(n, int) else []
                done, every = 0, NB * KT // max(1, len(units))
                for g in range(NB):
                    for k in range(KT):
                        for part, (w, x) in enumerate(((wh, xh), (wh, xl), (wl, xh))):
                            mm = nc.tensor.matmul(acc[:, s, g, 0:G], w[:, s, k * P:(k + 1) * P],
                                                  x[:, k, g * G:(g + 1) * G], start=k == 0 and part == 0,
                                                  stop=k == KT - 1 and part == 2)
                        if k == KT - 1:
                            if g < NB - 1 and y is None:
                                mm.then_inc(group, 1)
                            if g == NB - 1:
                                mm.then_inc(multiplied, 1)
                        done += 1
                        if units and done % every == 0:
                            beside.score(pe, units.pop(0))
                for u in units:
                    beside.score(pe, u)

            def turn(n, s, m):
                if beside and isinstance(m, int) and m == 0:
                    beside.end(pe)
                for t in range(TT):
                    if t == 0:
                        pe.wait_ge(staged, n * 2 + 2)
                        pe.wait_ge(rowed, m * 3 + 1)
                    if t == 5:
                        pe.wait_ge(taken, n + 3)
                    if t == ST:
                        pe.wait_ge(rowed, m * 3 + 2)
                    r = rows_of(t)
                    mm = nc.tensor.transpose(tb[:r, t // 4 % 2, t % 4 * P:(t % 4 + 1) * P],
                                             stage[:, s, t * P:t * P + r], ident[:])
                    if t in (3, 7, 8):
                        mm.then_inc(turned, 1)

            for seg0, count, stores, m_less_n in segments:
                if beside and stores:
                    beside.end(pe)

                def step(n, s):
                    multiply(n, s)
                    if stores:
                        turn(n, s, n + m_less_n)
                over(pe, seg0, count, step)

        def split_high(act, n, s):
            act.wait_ge(win[s], n // 2 * 16 + 16 if isinstance(n, int) else (n - s) * 8 + 16)
            act.wait_ge(multiplied, n + 1)
            nc.scalar.copy(wh[:, s], raw[:, s]).then_inc(high, 1)

        def take(engine, copy, n, s, stores, m_less_n):
            engine.wait_ge(stored[s], n // 2 * 32 + 32 if isinstance(n, int) else (n - s) * 16 + 32)
            for g in range(NB):
                if g < NB - 1:
                    engine.wait_ge(group, n * 2 + g + 1)
                else:
                    engine.wait_ge(multiplied, n + 3)
                copy(stage[:, s, g * G:(g + 1) * G], acc[:, s, g, 0:G]).then_inc(staged if g < NB - 1 else taken, 1)
            if stores:
                m = n + m_less_n
                ms = m % 2 if isinstance(m, int) else s
                engine.wait_ge(tstored[ms], m // 2 * 32 + 32 if isinstance(m, int) else (m - ms) * 16 + 32)
                for i, (a, b) in enumerate(((0, 4), (4, 8), (8, 9))):
                    engine.wait_ge(turned, m * 3 + i + 1)
                    r = rows_of(a)
                    copy(tstage[:r, ms, a:b, :], tb[:r, i % 2, 0:(b - a) * P].rearrange("p (a n) -> p a n", n=P)
                         ).then_inc(rowed, 1)

        def start_stages(engine):
            engine.sem_inc(rowed, 1)
            for s in range(2):
                engine.sem_inc(stored[s], 32)
                engine.sem_inc(tstored[s], 32)

        @block.scalar
        def _(act):
            if not beside:
                if spared:
                    act.sem_inc(high, spared)
                whole_range("scalar", act, spared, blocks - spared, lambda n, s: split_high(act, n, s))
                return
            act.sem_inc(taken, 2)
            start_stages(act)
            if spared:
                act.sem_inc(high, spared)
            else:
                split_high(act, 0, 0)
            for n in range(blocks):
                stores, m_less_n = next((x[2], x[3]) for x in segments if x[0] <= n < x[0] + x[1])
                if n + 1 < blocks and not beside.units(n):
                    split_high(act, n + 1, (n + 1) % 2)
                for i, u in enumerate(beside.units(n)):
                    if i == LOOK_AHEAD and n + 1 >= spared:
                        split_high(act, n + 1, (n + 1) % 2)
                    beside.weigh(act, u)
                take(act, nc.scalar.copy, n, n % 2, stores, m_less_n)

        @block.vector
        def _(dve):
            if beside:
                beside.choose(dve)
                return
            dve.sem_inc(taken, 2)
            if y is not None:
                def take_y(n, s):
                    dve.wait_ge(multiplied, n + 3)
                    nc.vector.tensor_copy(y[:, bass.ds(n, 1), :].rearrange("p a (g n) -> p (a g) n", g=NB),
                                          acc[:, s, :, 0:G]).then_inc(taken, 1)
                in_pairs(dve, 0, blocks, take_y)
                return
            start_stages(dve)
            if along:
                small_work("vector", dve, -1)
                whole_range("vector", dve, 0, blocks, lambda n, s: take(dve, nc.vector.tensor_copy, n, s, None, 0))
                return
            for seg0, count, stores, m_less_n in segments:
                in_pairs(dve, seg0, count, lambda n, s: take(dve, nc.vector.tensor_copy, n, s, stores, m_less_n))


class TurnedCaches:

    FROM, EACH, SLOTS = 3, 2, 4

    def __init__(self, nc, ident, jobs):
        self.nc, self.ident, self.jobs = nc, ident, jobs
        self.heads = [(j, h, rows.shape[2], fm, row0 + h * rows.shape[2])
                      for j, (rows, fm, row0) in enumerate(jobs) for h in range(rows.shape[1])]

    def mix_into(self, ph):
        self.loaded = [ph.sem(f"cache_in{j}") for j in range(len(self.jobs))]
        self.stored = [ph.sem(f"stored{s}") for s in range(self.SLOTS)]
        self.turned, self.copied = ph.sem("heads_turned"), ph.sem("heads_copied")
        self.tiles = [ph.sb(f"cache{j}", [P, PAST // P, rows.shape[1] * rows.shape[2]])
                      for j, (rows, _, _) in enumerate(self.jobs)]
        self.stage = ph.sb("stage", [P, self.SLOTS, PAST])
        self.bank = ph.ps("bank", [P, 2, 512])

    def after(self, t):
        if t < self.FROM:
            return ()
        at = (t - self.FROM) * self.EACH
        return range(min(at, len(self.heads)), min(at + self.EACH, len(self.heads)))

    def load(self, sp):
        for j, (rows, _, _) in enumerate(self.jobs):
            sp.dma_start(self.tiles[j][:], rows.rearrange("(t p) h d -> p t (h d)", p=P)).then_inc(self.loaded[j], 16)

    def turn(self, pe, n):
        j, h, w, _, _ = self.heads[n]
        pe.wait_ge(self.loaded[j], 16)
        if n >= 2:
            pe.wait_ge(self.copied, n - 1)
        for t in range(PAST // P):
            mm = self.nc.tensor.transpose(self.bank[:w, n % 2, t * P:(t + 1) * P],
                                          self.tiles[j][:, t, h * w:(h + 1) * w], self.ident[:])
        mm.then_inc(self.turned, 1)

    def take(self, act, n):
        w = self.heads[n][2]
        act.wait_ge(self.turned, n + 1)
        if n >= self.SLOTS:
            act.wait_ge(self.stored[n % self.SLOTS], n // self.SLOTS * 16)
        self.nc.scalar.copy(self.stage[:w, n % self.SLOTS], self.bank[:w, n % 2]).then_inc(self.copied, 1)

    def store(self, sp, n):
        _, _, w, fm, row = self.heads[n]
        sp.wait_ge(self.copied, n + 1)
        sp.dma_start(fm[row:row + w, S0:SN], self.stage[:w, n % self.SLOTS]).then_inc(self.stored[n % self.SLOTS], 16)

    def all_stored(self, sp):
        for s in range(self.SLOTS):
            sp.wait_ge(self.stored[s], 16 * ((len(self.heads) + self.SLOTS - 1 - s) // self.SLOTS))


class Indexer:

    TILES = [2, ST, 3, 4, 5, 6, 7]
    Q0 = 2 * P
    QN = SEQ - Q0
    QC = QN + P
    blocks = 8

    def __init__(self, nc, keep, bias):
        self.nc, self.bias = nc, bias
        self.minus = keep.sb("minus", [P, SEQ])
        self.left = keep.sb("left", [P, 2, SEQ])
        self.best = keep.sb("best", [P, 2, 8])
        self.list = [(i, t, h) for i, t in enumerate(self.TILES) for h in range(IDX_H)]

    def units(self, block):
        each = len(self.list) // self.blocks
        return range(block * each, (block + 1) * each) if block < self.blocks else ()

    def q_of(self, t):
        return self.QN if t == ST else t * P - self.Q0

    def distance(self, t):
        at = (ST - 1) * P - (PAST if t == ST else t * P)
        return self.minus[:, at:at + width_of(t)]

    def prepare(self, ph, fm, wtok, ring, weights):
        nc, QN, QC = self.nc, self.QN, self.QC
        self.added, self.step, self.passed, self.measured = (
            ph.sem(n) for n in ("added", "step", "passed", "measured"))
        self.steps = Counted(self.step)
        self.qhl = qhl = ph.sb("qhl", [P, IDX_H, QC], F32R)
        self.khh = khh = ph.sb("khh", [P, KEYS], F32R)
        self.kll = kll = ph.sb("kll", [P, KEYS], F32R)
        self.w = w = ph.sb("w", [P, TT, IDX_H])
        SLOTS = 4
        with Phase(nc, "ready") as p:
            qraw = p.sb("qraw", [P, SLOTS, QN + NEW])
            qtmp = p.sb("qtmp", [P, 2, QN + NEW])
            kraw = p.sb("kraw", [P, KEYS])
            wraw = p.sb("wraw", [P, TT, IDX_H])
            q_in = [p.sem(f"q_in{s}") for s in range(SLOTS // 2)]
            k_in, w_in = p.sem("k_in"), p.sem("w_in")
            ring.fill_from(p, weights)
            cleared, qcopied, khigh, wscaled = (p.sem(n) for n in ("cleared", "qcopied", "khigh", "wscaled"))
            qready, kready, numbered = (p.sem(n) for n in ("qready", "kready", "numbered"))
            offset = self.left[:, 0].bitcast(mybir.dt.int32)
            minus, left, measured = self.minus, self.left[:, 0], self.measured
            block = p.block()

            @block.sync
            def _(sp):
                qrows = fm[A_QI * P:(A_QI + 4) * P].rearrange("(h d) c -> d h c", d=IDX_D)
                krows = fm[A_KI * P:A_KI * P + IDX_D]
                halves = [slice(half * 64, half * 64 + 64) for half in range(2)]
                for at in halves:
                    sp.dma_start(kraw[at], krows).then_inc(k_in, 16)
                for h in range(0, IDX_H, 2):
                    i = h % SLOTS
                    if h >= SLOTS:
                        sp.wait_ge(qcopied, 2 * (h - SLOTS) + 4)
                        sp.wait_ge(qready, h - SLOTS + 2)
                    for at in halves:
                        sp.dma_start(qraw[at, i:i + 2, 0:QN], qrows[:, h:h + 2, self.Q0:SEQ]).then_inc(q_in[i // 2], 16)
                        sp.dma_start(qraw[at, i:i + 2, QN:QN + NEW], qrows[:, h:h + 2, SN:KEYS]
                                     ).then_inc(q_in[i // 2], 16)
                    if h == 2:
                        ring.load(sp)
                sp.wait_ge(cleared, 2)
                sp.dma_start(wraw[:, 0:ST], wtok[0:SEQ].rearrange("(t p) h -> p t h", p=P)).then_inc(w_in, 16)
                sp.dma_start(wraw[:NEW, ST], wtok[SEQ:TOK]).then_inc(w_in, 16)

            @block.gpsimd
            def _(pool):
                nc.gpsimd.memset(wraw[:, ST], 0.0).then_inc(cleared, 1)
                nc.gpsimd.memset(qhl[:, :, QN + NEW:QC].bitcast(F32), 0.0).then_inc(cleared, 1)
                nc.gpsimd.iota(offset, pattern=[[-1, SEQ]], base=(ST - 1) * P, channel_multiplier=1
                               ).then_inc(numbered, 1)
                pool.wait_ge(khigh, 1)
                nc.gpsimd.tensor_tensor(kll[:], kraw[:], khh[:].bitcast(F32), ALU.subtract).then_inc(kready, 1)
                pool.wait_ge(kready, 1)
                for s in range(2):
                    ring.split_low(pool, s)

            @block.scalar
            def _(act):
                act.wait_ge(k_in, 32)
                nc.scalar.copy(khh[:], kraw[:]).then_inc(khigh, 1)
                for h in range(IDX_H):
                    act.wait_ge(q_in[h % SLOTS // 2], h // SLOTS * 64 + 64)
                    if h >= 2:
                        act.wait_ge(qready, h - 1)
                    nc.scalar.copy(qtmp[64:128, h % 2].bitcast(F32R), qraw[64:128, h % SLOTS]).then_inc(qcopied, 1)
                    nc.scalar.copy(qhl[0:64, h, 0:QN + NEW], qraw[0:64, h % SLOTS]).then_inc(qcopied, 1)
                    if h == SLOTS - 1:
                        for s in range(2):
                            ring.split_high(act, s)
                act.wait_ge(w_in, 32)
                nc.scalar.mul(w[:].rearrange("p a b -> p (a b)"), wraw[:].rearrange("p a b -> p (a b)"), IDX_SCALE
                              ).then_inc(wscaled, 1)
                act.wait_ge(wscaled, 1)
                act.wait_ge(qcopied, 2 * IDX_H)

            @block.vector
            def _(dve):
                dve.wait_ge(numbered, 1)
                nc.vector.tensor_copy(minus[:], offset).then_inc(measured, 1)
                dve.wait_ge(measured, 1)
                nc.vector.tensor_scalar(left, minus[:], -1.0, None, ALU.mult).then_inc(measured, 1)
                dve.wait_ge(measured, 2)
                nc.vector.tensor_tensor(minus[:], minus[:], left, ALU.min).then_inc(measured, 1)
                for h in range(IDX_H):
                    dve.wait_ge(qcopied, 2 * h + 1)
                    nc.vector.tensor_tensor(qhl[64:128, h, 0:QN + NEW], qraw[64:128, h % SLOTS], qtmp[64:128, h % 2],
                                            ALU.subtract).then_inc(qready, 1)
                dve.wait_ge(qready, IDX_H)
                dve.wait_ge(measured, 3)

    def mix_into(self, ph):
        self.rel = ph.sb("rel", [P, 2, SEQ])
        self.dots = ph.ps("dots", [P, 2, 512])
        self.multiplied, self.rectified, self.weighted = (ph.sem(n) for n in ("dotted", "rectified", "weighted"))

    def end(self, pe):
        pe.wait_ge(self.rectified, len(self.list))

    def score(self, pe, n):
        i, t, h = self.list[n]
        wd, k0, q = width_of(t), key0_of(t), self.q_of(t)
        if n >= 1:
            pe.wait_ge(self.rectified, n)
        for a in range(0, wd, 512):
            b = min(a + 512, wd)
            for part, k in enumerate((self.khh, self.kll)):
                mm = self.nc.tensor.matmul(self.dots[:, a // 512, 0:b - a], self.qhl[:, h, q:q + P],
                                           k[:, k0 + a:k0 + b], start=part == 0, stop=part == 1)
        mm.then_inc(self.multiplied, 1)

    def weigh(self, act, n):
        i, t, h = self.list[n]
        rel = self.rel[:, n % 2, 0:width_of(t)]
        act.wait_ge(self.multiplied, n + 1)
        if n >= 2:
            act.wait_ge(self.added, n - 1)
        self.nc.scalar.activation(rel, self.dots[:].rearrange("p a b -> p (a b)")[:, 0:width_of(t)], ACT.Relu
                                  ).then_inc(self.rectified, 1)
        act.wait_ge(self.rectified, n + 1)
        self.nc.scalar.mul(rel, rel, self.w[:, t, h:h + 1]).then_inc(self.weighted, 1)

    def add(self, pool, n):
        i, t, h = self.list[n]
        rel, score = self.rel[:, n % 2, 0:width_of(t)], self.bias[t]
        pool.wait_ge(self.weighted, n + 1)
        if h == 0:
            self.nc.gpsimd.tensor_copy(score, rel).then_inc(self.added, 1)
        else:
            pool.wait_ge(self.added, n)
            self.nc.gpsimd.tensor_tensor(score, score, rel, ALU.add).then_inc(self.added, 1)

    def choose(self, dve):
        nc, steps = self.nc, self.steps
        for t in (0, 1):
            steps.up(nc.vector.tensor_copy(self.bias[t], self.distance(t)))
            dve.wait_ge(self.step, steps.n)
            steps.up(nc.vector.memset(self.bias[t][0:CHUNK, width_of(t) - CHUNK:width_of(t)], -BIG))
        self.choose_tiles(dve, (0, 1))
        self.choose_tiles(dve, (2, 3))

    def choose_late(self, dve):
        self.choose_tiles(dve, (4, 5))
        self.choose_tiles(dve, (6,))

    def choose_tiles(self, dve, which):
        nc, steps, step = self.nc, self.steps, self.step
        tiles = [self.TILES[i] for i in which]
        best = [self.best[:, j] for j in range(len(which))]
        scores = [self.bias[t] for t in tiles]
        rest = [self.left[:, j, 0:width_of(t)] for j, t in enumerate(tiles)]
        rounds = [(TOPK_STREAM if t == ST else TOPK) // 8 - 1 for t in tiles]
        every = range(len(which))

        def each(js, instruction):
            for j in js:
                dve.wait_ge(step, seen[j])
                seen[j] = steps.up(instruction(j))

        dve.wait_ge(self.added, IDX_H * (which[-1] + 1))
        seen = [steps.n] * len(which)
        for j, t in enumerate(tiles):
            if t != ST:
                wd = width_of(t)
                seen[j] = steps.up(nc.vector.memset(scores[j][0:CHUNK, wd - CHUNK:wd], BARRED))
        each(every, lambda j: nc.vector.max(best[j], scores[j]))
        each(every, lambda j: nc.vector.match_replace(rest[j], best[j], scores[j], TAKEN))

        def loop(js, count):
            n0, width = steps.n, len(js)
            with dve.Fori(0, count) as r:
                for i, j in enumerate(js):
                    wait_apart(dve, step, r * (2 * width) + n0 + i + 1 - width, self.passed)
                    nc.vector.max(best[j], rest[j]).then_inc(step, 1)
                for i, j in enumerate(js):
                    wait_apart(dve, step, r * (2 * width) + n0 + i + 1, self.passed)
                    nc.vector.match_replace(rest[j], best[j], rest[j], TAKEN).then_inc(step, 1)
            steps.n += 2 * width * count
            for i, j in enumerate(js):
                seen[j] = steps.n - width + i + 1

        both = min(rounds)
        loop(list(every), both)
        for j in every:
            if rounds[j] > both:
                dve.wait_ge(step, steps.n)
                loop([j], rounds[j] - both)
        each(every, lambda j: nc.vector.tensor_tensor(rest[j], rest[j], scores[j], ALU.not_equal))
        each(every, lambda j: nc.vector.tensor_scalar(rest[j], rest[j], BIG, -BIG, ALU.mult, ALU.add))
        each(every, lambda j: nc.vector.tensor_tensor(scores[j], rest[j], self.distance(tiles[j]), ALU.add))
        dve.wait_ge(step, steps.n)


class ForgetGates:

    def __init__(self, nc, ident, fm, b_f, cache_logf, out_prompt, out_sample, minus_c, ctok):
        self.nc, self.ident, self.fm, self.b_f, self.cache_logf = nc, ident, fm, b_f, cache_logf
        self.out_prompt, self.out_sample, self.minus_c, self.ctok = out_prompt, out_sample, minus_c, ctok
        self.steps = {("sync", 1): self.load, ("sync", "end"): self.store,
                      ("vector", -1): self.before_exp, ("scalar", 0): self.exp, ("vector", 1): self.before_ln,
                      ("scalar", 4): self.ln, ("vector", 4): self.sum_up, ("tensor", 6): self.turn,
                      ("vector", 6): self.take_rows}

    def mix_into(self, ph):
        self.f = ph.sb("f", [HEADS, TOK])
        self.bf = ph.sb("bf", [HEADS, 1])
        self.z, self.e, self.u, self.d, self.lnu, self.r, self.logf = (
            ph.sb(n, [HEADS, TOK]) for n in ("z", "e", "u", "d", "lnu", "r", "logf"))
        self.stream = ph.sb("stream", [HEADS, PAST + NEW])
        self.ones = ph.sb("ones", [HEADS, SEQ])
        self.c, self.mc = ph.sb("c", [HEADS, KEYS]), ph.sb("mc", [HEADS, KEYS])
        self.ltok = ph.sb("ltok", [P, TT, HEADS])
        self.bank = ph.ps("bank", [P, 2, 512])
        self.fin, self.ready, self.acts, self.summed, self.turned, self.copied, self.kept = (
            ph.sem(n) for n in ("f_in", "ready", "acts", "summed", "turned_gates", "copied", "kept"))
        self.s = Counted(ph.sem("step"))

    def load(self, sp):
        nc, fm = self.nc, self.fm
        sp.dma_start(self.f[:, 0:SEQ], fm[0:HEADS, 0:SEQ]).then_inc(self.fin, 16)
        sp.dma_start(self.f[:, SEQ:TOK], fm[0:HEADS, SN:KEYS]).then_inc(self.fin, 16)
        sp.dma_start(self.bf[:], self.b_f).then_inc(self.fin, 16)
        with nc.allow_non_contiguous_dma("512 by 8 values"):
            sp.dma_start(self.stream[:, 0:PAST], self.cache_logf.rearrange("s h -> h s")).then_inc(self.fin, 16)

    def store(self, sp):
        sp.wait_ge(self.copied, 3)
        sp.dma_start(self.minus_c, self.mc[:]).then_inc(self.kept, 16)
        sp.dma_start(self.out_prompt.rearrange("(t p) h -> p t h", p=P), self.ltok[:, 0:ST]).then_inc(self.kept, 16)
        sp.dma_start(self.out_sample, self.ltok[:NEW, ST]).then_inc(self.kept, 16)
        sp.wait_ge(self.kept, 48)

    def exp(self, act):
        act.wait_ge(self.ready, 1)
        self.nc.scalar.activation(self.e[:], self.e[:], ACT.Exp, scale=-1.0).then_inc(self.acts, 1)

    def ln(self, act):
        act.wait_ge(self.ready, 2)
        self.nc.scalar.activation(self.lnu[:], self.u[:], ACT.Ln).then_inc(self.acts, 1)

    def then(self, dve, instruction, signal=None):
        self.s.up(instruction)
        dve.wait_ge(self.s.sem, self.s.n)
        if signal is not None:
            dve.sem_inc(signal, 1)

    def before_exp(self, dve):
        nc, then, z, e = self.nc, self.then, self.z, self.e
        then(dve, nc.vector.memset(self.ones[:], 1.0))
        then(dve, nc.vector.memset(self.ctok[:, ST], 0.0))
        dve.wait_ge(self.fin, 64)
        then(dve, nc.vector.tensor_scalar(z[:], self.f[:], self.bf[:], None, ALU.add))
        then(dve, nc.vector.tensor_scalar(e[:], z[:], -1.0, None, ALU.mult))
        then(dve, nc.vector.tensor_tensor(e[:], e[:], z[:], ALU.max), self.ready)

    def before_ln(self, dve):
        nc, then, z, e, u, d, r = self.nc, self.then, self.z, self.e, self.u, self.d, self.r
        dve.wait_ge(self.acts, 1)
        then(dve, nc.vector.tensor_scalar_add(u[:], e[:], 1.0), self.ready)
        then(dve, nc.vector.tensor_scalar_min(z[:], z[:], 0.0))
        then(dve, nc.vector.tensor_scalar(d[:], u[:], -1.0, 1e-30, ALU.add, ALU.max))
        then(dve, nc.vector.reciprocal(r[:], d[:]))
        then(dve, nc.vector.tensor_tensor(r[:], r[:], e[:], ALU.mult))

    def sum_up(self, dve):
        nc, then, z, e, u, d, r = self.nc, self.then, self.z, self.e, self.u, self.d, self.r
        logf, stream, c, ones = self.logf, self.stream, self.c, self.ones
        dve.wait_ge(self.acts, 2)
        then(dve, nc.vector.tensor_scalar(d[:], u[:], 1.0, None, ALU.is_equal))
        then(dve, nc.vector.tensor_tensor(d[:], d[:], e[:], ALU.mult))
        then(dve, nc.vector.tensor_scalar(u[:], u[:], 1.0, None, ALU.is_gt))
        then(dve, nc.vector.tensor_tensor(u[:], u[:], r[:], ALU.mult))
        then(dve, nc.vector.tensor_tensor(u[:], u[:], self.lnu[:], ALU.mult))
        then(dve, nc.vector.tensor_tensor(u[:], u[:], d[:], ALU.add))
        then(dve, nc.vector.tensor_tensor(logf[:], z[:], u[:], ALU.subtract))
        then(dve, nc.vector.tensor_copy(stream[:, PAST:], logf[:, SEQ:TOK]))
        then(dve, nc.vector.tensor_tensor_scan(c[:, 0:SEQ], ones[:], logf[:, 0:SEQ], 0.0, ALU.mult, ALU.add))
        then(dve, nc.vector.tensor_tensor_scan(c[:, S0:KEYS], ones[:, 0:PAST + NEW], stream[:], 0.0, ALU.mult,
                                               ALU.add), self.summed)
        nc.vector.tensor_scalar(self.mc[:], c[:], -1.0, None, ALU.mult).then_inc(self.copied, 1)

    def turn(self, pe):
        nc, bank, ident = self.nc, self.bank, self.ident
        pe.wait_ge(self.summed, 1)
        for n in range(2):
            for t in range(TT):
                r = rows_of(t)
                src = (self.logf[:, t * P:t * P + r] if n == 0 else
                       self.c[:, SN:KEYS] if t == ST else self.c[:, t * P:(t + 1) * P])
                mm = nc.tensor.transpose(bank[:r, n, t * HEADS:(t + 1) * HEADS], src, ident[:HEADS, :HEADS])
        mm.then_inc(self.turned, 1)

    def take_rows(self, dve):
        nc, bank = self.nc, self.bank
        dve.wait_ge(self.turned, 1)
        for n, to in enumerate((self.ltok, self.ctok)):
            self.s.up(nc.vector.tensor_copy(to[:, 0:ST],
                                            bank[:, n, 0:ST * HEADS].rearrange("p (t h) -> p t h", h=HEADS)))
            dve.wait_ge(self.s.sem, self.s.n)
            nc.vector.tensor_copy(to[:NEW, ST], bank[:NEW, n, ST * HEADS:TT * HEADS]).then_inc(self.copied, 1)
        dve.wait_ge(self.copied, 3)


def attend(nc, name, ident, grp, o, fmq, q0, fmk, v_prompt, v_past, v_new, bias=None, minus_c=None, ctok=None):
    sparse = bias is not None
    QW = (grp.cols + P - 1) // P * P
    VT = KEYS // P + 1
    order = sorted(grp.tiles, key=width_of)
    U = len(order)
    NU = 2 * U
    TS = 6
    WIDE = max(width_of(t) for t in order)
    wide = lambda t: width_of(t) > 512
    both_halves = wide
    prompt = [t for t in grp.tiles if t != ST]
    q_parts = [(slice(0, len(prompt) * P), slice(prompt[0] * P, (prompt[-1] + 1) * P))]
    if ST in grp.tiles:
        q_parts.append((grp.at(ST), slice(SN, KEYS)))
    Q, K, V = range(3)
    PREPARING = (5, 6, 8)
    with Phase(nc, name) as ph:
        qraw, kraw, vraw = ph.sb("qraw", [P, grp.cols]), ph.sb("kraw", [P, KEYS]), ph.sb("vraw", [P, VT, HD])
        qh, ql = (ph.sb(n, [P, 2, QW], F32R) for n in ("qh", "ql"))
        kh, kl = (ph.sb(n, [P, 2, KEYS], F32R) for n in ("kh", "kl"))
        vhl = ph.sb("vhl", [P, 2, VT, 2, HD], F32R)
        part_sum = ph.sb("part_sum", [P, 2, HD])
        qscale, slope = ph.sb("qscale", [P, HEADS]), ph.sb("slope", [P, HEADS])
        prob = ph.sb("prob", [P, 2, WIDE])
        pth, ptl = (ph.sb(n, [P, 2, KT, P], F32R) for n in ("pth", "ptl"))
        top, shift = ph.sb("top", [P, 2]), ph.sb("shift", [P, 2])
        total, inverse = ph.sb("total", [P, TS]), ph.sb("inverse", [P, TS])
        if not sparse:
            minus = ph.sb("minus", [P, 2, KEYS])
            row_c = ph.sb("row_c", [P, 2])
            later = ph.sb("later", [P, P], F32R)
            one = ph.sb("one", [P, P], F32R)
        logits, outs = ph.ps("logits", [P, 2, 2, 512]), ph.ps("outs", [P, 2, 512])
        trans = ph.ps("trans", [P, 8, P])
        loaded, highs, lows = ([ph.sem(f"{kind}_{x}") for x in "qkv"] for kind in ("loaded", "highs", "lows"))
        c_in = [ph.sem(f"c_in{s}") for s in range(2)]
        constants, qscaled, passed = (ph.sem(n) for n in ("constants", "qscaled", "passed"))
        multiplied, biased, row_top, shifted, raised = (
            ph.sem(n) for n in ("multiplied", "biased", "row_top", "shifted", "raised"))
        turned, thigh, tlow, summed, inverted, half_scaled, scaled = (
            ph.sem(n) for n in ("turned", "thigh", "tlow", "summed", "inverted", "half_scaled", "scaled"))
        CONSTANTS = 1 + 2 * (QW > grp.cols) + 2 * HEADS + 3 * (not sparse)
        loads = (16 * len(q_parts), 16, 48)

        def unit(n):
            return n % NU // U, order[n % NU % U]

        def slot(n, pair):
            if not sparse:
                return unit(n)[0]
            if isinstance(pair, int):
                return (pair + n // NU) // 2
            return 0 if n < 0 else bass.ds(pair - 1, 1)

        def part(x, at):
            return x[:, at] if isinstance(at, int) else x[:, at].rearrange("p a b -> p (a b)")

        def turned_at(n):
            return 0 if wide(unit(n)[1]) or n % 2 == 0 else 4

        def prepared(n, first, last):
            s, i = n // U, n % U
            if n >= NU:
                return []
            jobs = []
            if not (last and s == 1):
                if sparse and i == U - 2:
                    jobs = [(Q, s + 1, 1 - s)]
                elif not sparse and i in PREPARING:
                    jobs = [(PREPARING.index(i), s + 1, 1 - s)]
            if sparse and first and n in (4, 5):
                jobs.append((n - 3, 1, 1))
            return jobs

        def done(engine, sem, unit_no, first, u0):
            if not (first and unit_no < 0):
                engine.wait_ge(sem, u0 + unit_no + 1)

        def done_apart(engine, sem, unit_no, first, u0):
            if not (first and unit_no < 0):
                wait_apart(engine, sem, u0 + unit_no + 1, passed)

        def pairs(engine, body):
            body(0, 0, True, False)
            with engine.Fori(1, HEADS // 2 - 1) as pair:
                body(pair * NU, pair, False, False)
            body((HEADS // 2 - 1) * NU, HEADS // 2 - 1, False, True)

        block = ph.block()

        @block.sync
        def _(sp):
            def load(what, head):
                if not (isinstance(head, int) and head == 0):
                    wait_apart(sp, lows[what], head, passed)
                if what == Q:
                    for to, at in q_parts:
                        sp.dma_start(qraw[:, to], fmq[bass.ds(q0 + head * P, P), at]).then_inc(loaded[Q], 16)
                elif what == K:
                    sp.dma_start(kraw[:], fmk[bass.ds(head * P, P)]).then_inc(loaded[K], 16)
                else:
                    cols = bass.ds(head * P, P)
                    sp.dma_start(vraw[:, 0:8], v_prompt[:, cols].rearrange("(t p) d -> p t d", p=P)
                                 ).then_inc(loaded[V], 16)
                    sp.dma_start(vraw[:, 8:12], v_past[:, cols].rearrange("(t p) d -> p t d", p=P)
                                 ).then_inc(loaded[V], 16)
                    sp.dma_start(vraw[:NEW, 12], v_new[:, cols]).then_inc(loaded[V], 16)

            load(Q, 0)
            load(K, 0)
            sp.wait_ge(constants, 1)
            load(V, 0)

            def body(u0, pair, first, last):
                for s in range(2):
                    if not sparse:
                        if not first:
                            sp.wait_ge(biased, u0 + (s + 1) * U - NU)
                        sp.dma_start(minus[:, s], minus_c[bass.ds(pair * 2 + s, 1)].rearrange("a k -> (a k)")
                                     .partition_broadcast(P)).then_inc(c_in[s], 16)
                    for n in range(s * U, (s + 1) * U):
                        for what, ahead, _ in prepared(n, first, last):
                            load(what, pair * 2 + ahead)
            pairs(sp, body)

        @block.gpsimd
        def _(pool):
            nc.gpsimd.memset(vraw[:, 12], 0.0).then_inc(constants, 1)
            if QW > grp.cols:
                nc.gpsimd.memset(qh[:, :, grp.cols:QW].bitcast(F32), 0.0).then_inc(constants, 1)
                nc.gpsimd.memset(ql[:, :, grp.cols:QW].bitcast(F32), 0.0).then_inc(constants, 1)
            for h in range(HEADS):
                power = 2.0 ** (h + 1) if sparse else 1.0
                nc.gpsimd.memset(qscale[:, h:h + 1], SCALE * power).then_inc(constants, 1)
                nc.gpsimd.memset(slope[:, h:h + 1], 1.0 / power).then_inc(constants, 1)
            if not sparse:
                nc.gpsimd.memset(prob[:, 0, 0:P], 0.0).then_inc(constants, 1)
                pool.wait_ge(constants, CONSTANTS - 2)
                nc.gpsimd.affine_select(out=later[:], in_=prob[:, 0, 0:P], compare_op=ALU.is_ge, fill=-BIG, base=0,
                                        pattern=[[-1, P]], channel_multiplier=1).then_inc(constants, 1)
                nc.gpsimd.tensor_copy(one[:], ident[:]).then_inc(constants, 1)

            def low(what, head, s):
                pool.wait_ge(highs[what], head + 1)
                to, raw, high = ((ql[:, s, 0:grp.cols], qraw, qh[:, s, 0:grp.cols]), (kl[:, s], kraw, kh[:, s]),
                                 (vhl[:, s, :, 1], vraw, vhl[:, s, :, 0]))[what]
                nc.gpsimd.tensor_tensor(to, raw[:], high.bitcast(F32), ALU.subtract).then_inc(lows[what], 1)

            for what in (Q, K, V):
                low(what, 0, 0)

            def body(u0, pair, first, last):
                for n in range(NU):
                    for what, ahead, s in prepared(n, first, last):
                        low(what, pair * 2 + ahead, s)
            pairs(pool, body)

        @block.tensor
        def _(pe):
            pe.wait_ge(constants, CONSTANTS)

            def scores(n, u0, pair, first):
                s, t = unit(n)
                if n % U == 0:
                    pe.wait_ge(lows[Q], pair * 2 + s + 1)
                    if not sparse:
                        pe.wait_ge(lows[K], pair * 2 + s + 1)
                    elif n == 0:
                        pe.wait_ge(lows[K], 1 if isinstance(pair, int) and pair < 2 else
                                   2 if isinstance(pair, int) else pair)
                done(pe, biased, n - 2, first, u0)
                wd, k0, q = width_of(t), key0_of(t), slice(grp.start[t], grp.start[t] + P)
                ks = slot(n, pair)
                for a in range(0, wd, 512):
                    b = min(a + 512, wd)
                    to = logits[:, n % 2, a // 512, 0:b - a]
                    parts = ((qh, kh), (ql, kh), (qh, kl))
                    masked = not sparse and b == wd
                    for i, (x, y) in enumerate(parts):
                        mm = nc.tensor.matmul(to, x[:, s, q], part(y, ks)[:, k0 + a:k0 + b], start=i == 0,
                                              stop=i == 2 and not masked)
                    if masked:
                        m = rows_of(t)
                        mm = nc.tensor.matmul(logits[:, n % 2, a // 512, b - a - m:b - a], one[:], later[:, 0:m],
                                              start=False, stop=True)
                mm.then_inc(multiplied, 1)

            def turn(n, u0, first):
                s, t = unit(n)
                wd = width_of(t)
                done(pe, raised, n, first, u0)
                overlap = wide(t) or wide(unit(n - 1)[1])
                done(pe, tlow, n - 1 if overlap else n - 2, first, u0)
                for j, a in enumerate(range(0, wd, P)):
                    b = min(a + P, wd)
                    mm = nc.tensor.transpose(trans[:b - a, turned_at(n) + j],
                                             prob[:, n % 2, a:b], ident[:])
                mm.then_inc(turned, 1)

            def weigh(n, u0, pair, first):
                s, t = unit(n)
                wd, v0 = width_of(t), key0_of(t) // P
                if not sparse and n % U == 0:
                    pe.wait_ge(lows[V], (pair * 2 + s if n >= 0 else pair * 2 - 2 + s) + 1)
                elif sparse and n == 0:
                    pe.wait_ge(lows[V], 1 if isinstance(pair, int) and pair < 2 else
                               2 if isinstance(pair, int) else pair)
                done(pe, tlow, n, first, u0)
                done(pe, scaled, n - 2, first, u0)
                vs = slot(n, pair)
                tiles = [(j, min(P, wd - j * P)) for j in range((wd + P - 1) // P)]
                for j, m in tiles:
                    v, end = vhl[:m, vs, v0 + j], j == len(tiles) - 1
                    v = v.rearrange("p h d -> p (h d)" if isinstance(vs, int) else "p a h d -> p (a h d)")
                    if both_halves(t):
                        nc.tensor.matmul(outs[:, n % 2, 0:2 * HD], pth[:m, n % 2, j], v, start=j == 0, stop=False)
                    else:
                        nc.tensor.matmul(outs[:, n % 2, 0:HD], pth[:m, n % 2, j], v[:, 0:HD], start=j == 0, stop=False)
                        nc.tensor.matmul(outs[:, n % 2, 0:HD], pth[:m, n % 2, j], v[:, HD:], start=False, stop=False)
                    mm = nc.tensor.matmul(outs[:, n % 2, 0:HD], ptl[:m, n % 2, j], v[:, 0:HD], start=False, stop=end)
                mm.then_inc(summed, 1)

            def body(u0, pair, first, last):
                for n in range(NU + 3 if last else NU):
                    if n < NU:
                        scores(n, u0, pair, first)
                    if not (first and n < 3):
                        weigh(n - 3, u0, pair, first)
                    if n <= NU and not (first and n < 1):
                        turn(n - 1, u0, first)
            pairs(pe, body)

        @block.scalar
        def _(act):
            def high(what, head, s):
                act.wait_ge(loaded[what], head * loads[what] + loads[what])
                if what == Q:
                    nc.scalar.mul(qraw[:], qraw[:], qscale[:, bass.ds(head, 1)]).then_inc(qscaled, 1)
                    act.wait_ge(qscaled, head + 1)
                    nc.scalar.copy(qh[:, s, 0:grp.cols], qraw[:]).then_inc(highs[Q], 1)
                elif what == K:
                    nc.scalar.copy(kh[:, s], kraw[:]).then_inc(highs[K], 1)
                else:
                    nc.scalar.copy(vhl[:, s, :, 0], vraw[:]).then_inc(highs[V], 1)

            def raise_(n, u0, pair, first):
                s, t = unit(n)
                wd = width_of(t)
                done_apart(act, shifted, n, first, u0)
                scale = slope[:, bass.ds((pair if n >= 0 else pair - 1) * 2 + s, 1)] if sparse else 1.0
                nc.scalar.activation(prob[:, n % 2, 0:wd], prob[:, n % 2, 0:wd], ACT.Exp, scale=scale,
                                     bias=shift[:, n % 2:n % 2 + 1], accum_out=total[:, n % TS:n % TS + 1]
                                     ).then_inc(raised, 1)

            def turned_high(n, u0, first):
                s, t = unit(n)
                wd = width_of(t)
                done(act, turned, n, first, u0)
                done(act, summed, n - 2, first, u0)
                full, rest, at = wd // P, wd % P, turned_at(n)
                last = nc.scalar.copy(pth[:, n % 2, 0:full], trans[:, at:at + full])
                if rest:
                    last = nc.scalar.copy(pth[:rest, n % 2, full], trans[:rest, at + full])
                last.then_inc(thigh, 1)

            act.wait_ge(constants, CONSTANTS)
            for what in (Q, K, V):
                high(what, 0, 0)

            def body(u0, pair, first, last):
                for n in range(NU + 2 if last else NU):
                    if not (first and n < 2):
                        turned_high(n - 2, u0, first)
                    if n <= NU and not (first and n < 1):
                        raise_(n - 1, u0, pair, first)
                    for what, ahead, s in prepared(n, first, last):
                        high(what, pair * 2 + ahead, s)
            pairs(act, body)

        @block.vector
        def _(dve):
            def add_bias(n, u0, pair, first):
                s, t = unit(n)
                wd, k0, b2 = width_of(t), key0_of(t), n % 2
                done_apart(dve, multiplied, n, first, u0)
                if not sparse and n % U == 0:
                    dve.wait_ge(c_in[s], pair * 16 + 16)
                done_apart(dve, turned, n - 2, first, u0)
                add = bias[t] if sparse else minus[:, s, k0:k0 + wd]
                nc.vector.tensor_tensor_reduce(out=prob[:, b2, 0:wd],
                                               in0=logits[:, b2].rearrange("p a b -> p (a b)")[:, 0:wd], in1=add,
                                               scale=1.0, scalar=-3.0e38, op0=ALU.add, op1=ALU.max,
                                               accum_out=top[:, b2:b2 + 1]).then_inc(biased, 1)

            def negate(n, u0, pair, first):
                s, t = unit(n)
                b2 = n % 2
                dve.wait_ge(biased, u0 + n + 1)
                if sparse:
                    nc.vector.tensor_scalar(shift[:, b2:b2 + 1], top[:, b2:b2 + 1],
                                            slope[:, bass.ds(pair * 2 + s, 1)], -1.0, ALU.mult, ALU.mult
                                            ).then_inc(shifted, 1)
                else:
                    row = ctok[:, t, bass.ds(pair * 2 + s, 1)]
                    nc.vector.tensor_scalar(row_c[:, b2:b2 + 1], top[:, b2:b2 + 1], row, None, ALU.add
                                            ).then_inc(row_top, 1)

            def less_row(n, u0, pair, first):
                s, t = unit(n)
                b2 = n % 2
                row = ctok[:, t, bass.ds(pair * 2 + s, 1)]
                dve.wait_ge(row_top, u0 + n + 1)
                nc.vector.tensor_scalar(shift[:, b2:b2 + 1], row_c[:, b2:b2 + 1], -1.0, row, ALU.mult, ALU.add
                                        ).then_inc(shifted, 1)

            def turned_low(n, u0, first):
                s, t = unit(n)
                wd = width_of(t)
                done(dve, thigh, n, first, u0)
                full, rest, at = wd // P, wd % P, turned_at(n)
                last = nc.vector.tensor_tensor(ptl[:, n % 2, 0:full], trans[:, at:at + full],
                                               pth[:, n % 2, 0:full].bitcast(F32), ALU.subtract)
                if rest:
                    last = nc.vector.tensor_tensor(ptl[:rest, n % 2, full], trans[:rest, at + full],
                                                   pth[:rest, n % 2, full].bitcast(F32), ALU.subtract)
                last.then_inc(tlow, 1)

            def invert(n, u0, first):
                done(dve, raised, n, first, u0)
                nc.vector.reciprocal(inverse[:, n % TS:n % TS + 1], total[:, n % TS:n % TS + 1]).then_inc(inverted, 1)

            def normalise(n, u0, first):
                if not both_halves(unit(n)[1]):
                    dve.sem_inc(half_scaled, 1)
                    return
                done(dve, summed, n, first, u0)
                done(dve, inverted, n, first, u0)
                nc.vector.tensor_scalar(part_sum[:, n % 2], outs[:, n % 2, HD:2 * HD], inverse[:, n % TS:n % TS + 1],
                                        None, ALU.mult).then_inc(half_scaled, 1)

            def normalise_rest(n, u0, pair, first):
                s, t = unit(n)
                head = (pair if n >= 0 else pair - 1) * 2 + s
                if not both_halves(t):
                    done(dve, summed, n, first, u0)
                    done(dve, inverted, n, first, u0)
                    nc.vector.tensor_scalar(o[:, t, bass.ds(head * HD, HD)], outs[:, n % 2, 0:HD],
                                            inverse[:, n % TS:n % TS + 1], None, ALU.mult).then_inc(scaled, 1)
                    return
                done(dve, half_scaled, n, first, u0)
                nc.vector.scalar_tensor_tensor(out=o[:, t, bass.ds(head * HD, HD)], in0=outs[:, n % 2, 0:HD],
                                               scalar=inverse[:, n % TS:n % TS + 1], in1=part_sum[:, n % 2],
                                               op0=ALU.mult, op1=ALU.add).then_inc(scaled, 1)

            def body(u0, pair, first, last):
                for n in range(NU + 4 if last else NU):
                    if not (first and n < 4):
                        normalise(n - 4, u0, first)
                        normalise_rest(n - 4, u0, pair, first)
                    if n < NU + 2 and not (first and n < 2):
                        turned_low(n - 2, u0, first)
                    if n < NU:
                        add_bias(n, u0, pair, first)
                    if n < NU + 3 and not (first and n < 3):
                        invert(n - 3, u0, first)
                    if n < NU:
                        negate(n, u0, pair, first)
                    if n < NU and not sparse:
                        less_row(n, u0, pair, first)
            pairs(dve, body)


def mlp(nc, name, grp, ring, xh, xl, y, w_up, w_down, beside=None):
    UP, LOADS, BLOCKS, CHUNKS = 4, 8, 12, D_FF // 512
    NB, G = grp.banks, grp.g
    wu = w_up.rearrange("(k p) n -> p k n", p=P)
    wd = w_down.rearrange("(k p) n -> p k n", p=P)
    frees = {UP + 2 * (load - UP) + 1 if load >= UP else load: load + 2 for load in range(LOADS)}
    with Phase(nc, name) as ph:
        raw, wh, wl, win, high, low, spared = ring.slots(ph)
        hh, hl = (ph.sb(n, [P, UP, grp.cols], F32R) for n in ("hh", "hl"))
        hidden = ph.sb("hidden", [P, 2, grp.cols])
        acc = ph.ps("acc", [P, 2, NB, 512])
        multiplied, taken = ph.sem("multiplied"), ph.sem("taken")
        cleared, squared, split, step = (ph.sem(n) for n in ("cleared", "squared", "split", "step"))
        block = ph.block()

        def chunks(engine, body):
            with engine.Fori(0, CHUNKS) as c:
                body(c)

        def loads(engine, step):
            for n in range(spared, 2):
                step(0, n)
            with engine.Fori(0, CHUNKS - 1) as c:
                for n in range(2, LOADS + 2):
                    step(c, n)
            for n in range(2, LOADS):
                step(CHUNKS - 1, n)

        @block.sync
        def _(sp):
            if spared:
                for s in range(2):
                    sp.sem_inc(win[s], 16)

            def load(c, n):
                sp.wait_ge(low, c * LOADS + n + 1)
                if n % LOADS < UP:
                    src, k = wu[:, :, bass.ds((c + n // LOADS) * 512 + n % LOADS * P, P)], KT
                else:
                    src, k = wd[:, bass.ds(c * 4, 4), (n - UP) * 256:(n - UP + 1) * 256], 4
                sp.dma_start(raw[:, n % 2].rearrange("p (k n) -> p k n", k=k), src).then_inc(win[n % 2], 16)
            loads(sp, load)

        def split_high(act, c, n):
            act.wait_ge(win[n % 2], c * (LOADS * 8) + n // 2 * 16 + 16)
            done = n - 1 if 2 <= n <= 5 else UP + 2 * (n - 5) if n > 5 else (-2, 0)[n]
            act.wait_ge(multiplied, c * BLOCKS + done + 3)
            nc.scalar.copy(wh[:, n % 2], raw[:, n % 2]).then_inc(high, 1)

        def split_low(pool, c, n):
            pool.wait_ge(high, c * LOADS + n + 1)
            nc.gpsimd.tensor_tensor(wl[:, n % 2], raw[:, n % 2], wh[:, n % 2].bitcast(F32), ALU.subtract
                                    ).then_inc(low, 1)

        def look_ahead(engine, split_one, after_block):
            for n in range(spared, 2):
                split_one(engine, 0, n)

            def body(c, last=False):
                for n in range(BLOCKS):
                    if n in frees and not (last and frees[n] >= LOADS):
                        split_one(engine, c, frees[n])
                    after_block(c, n)
            with engine.Fori(0, CHUNKS - 1) as c:
                body(c)
            body(CHUNKS - 1, last=True)

        def per_block(h):
            return h.rearrange("p (g n) -> p g n", g=NB)

        @block.scalar
        def _(act):
            if spared:
                act.sem_inc(high, spared)
            if not beside:
                loads(act, lambda c, n: split_high(act, c, n))
                return
            act.sem_inc(taken, 2)

            def take(c, n):
                h, banks = hidden[:, n % 2], acc[:, n % 2, :, 0:G]
                act.wait_ge(multiplied, c * BLOCKS + n + 4)
                act.wait_ge(step, c * BLOCKS + n + 1)
                if n < UP:
                    nc.scalar.activation(per_block(h), banks, ACT.Relu).then_inc(taken, 1)
                    act.wait_ge(taken, c * BLOCKS + n + 3)
                    nc.scalar.activation(h, h, ACT.Square).then_inc(squared, 1)
                    act.wait_ge(squared, c * (UP * 2) + 2 * n + 1)
                    nc.scalar.copy(hh[:, n], h).then_inc(squared, 1)
                else:
                    nc.scalar.copy(per_block(h), banks).then_inc(taken, 1)
            look_ahead(act, split_high, take)

        @block.gpsimd
        def _(pool):
            pool.sem_inc(low, 2 + spared)
            if not beside:
                loads(pool, lambda c, n: split_low(pool, c, n))
                return
            pool.sem_inc(step, 2)
            nc.gpsimd.memset(y[:, 0:KT, :], 0.0).then_inc(cleared, 1)
            pool.wait_ge(cleared, 1)

            def finish(c, n):
                h = hidden[:, n % 2]
                if n < UP:
                    pool.wait_ge(squared, c * (UP * 2) + 2 * n + 2)
                    nc.gpsimd.tensor_tensor(hl[:, n], h, hh[:, n].bitcast(F32), ALU.subtract).then_inc(split, 1)
                    pool.wait_ge(split, c * UP + n + 1)
                    pool.sem_inc(step, 1)
                else:
                    pool.wait_ge(taken, c * BLOCKS + n + 3)
                    nc.gpsimd.tensor_tensor(y[:, n - UP], y[:, n - UP], h, ALU.add).then_inc(step, 1)
            look_ahead(pool, split_low, finish)
            pool.wait_ge(step, CHUNKS * BLOCKS + 2)

        @block.tensor
        def _(pe):
            pe.sem_inc(multiplied, 3)

            def multiply(n, ks):
                up = n < UP
                load = n if up else UP + (n - UP) // 2
                last = (KT if up else 4) - 1
                for k in ks:
                    for g in range(NB):
                        at = k * P if up else k * 256 + n % 2 * P
                        w_h, w_l = (w[:, load % 2, at:at + P] for w in (wh, wl))
                        x_h, x_l = (x[:, k, g * G:(g + 1) * G] for x in ((xh, xl) if up else (hh, hl)))
                        for part, (w, x) in enumerate(((w_h, x_h), (w_h, x_l), (w_l, x_h))):
                            mm = nc.tensor.matmul(acc[:, n % 2, g, 0:G], w, x, start=k == 0 and part == 0,
                                                  stop=k == last and part == 2)
                if ks[-1] == last:
                    mm.then_inc(multiplied, 1)

            def body(c):
                for n in range(UP):
                    pe.wait_ge(low, c * LOADS + n + 3)
                    pe.wait_ge(taken, c * BLOCKS + n + 1)
                    multiply(n, range(KT))
                pe.wait_ge(low, c * LOADS + UP + 3)
                for n in (UP, UP + 1):
                    pe.wait_ge(taken, c * BLOCKS + n + 1)
                    for k in range(UP - 1):
                        if n == UP:
                            pe.wait_ge(split, c * UP + k + 1)
                        multiply(n, [k])
                pe.wait_ge(split, c * UP + UP)
                for n in (UP, UP + 1):
                    multiply(n, [UP - 1])
                for n in range(UP + 2, BLOCKS):
                    if n % 2 == 0:
                        pe.wait_ge(low, c * LOADS + UP + (n - UP) // 2 + 3)
                    pe.wait_ge(taken, c * BLOCKS + n + 1)
                    multiply(n, range(UP))
            chunks(pe, body)

        @block.vector
        def _(dve):
            if beside:
                beside(dve)
                return
            dve.sem_inc(taken, 2)
            nc.vector.memset(y[:, 0:KT, :], 0.0).then_inc(cleared, 1)
            dve.wait_ge(cleared, 1)

            def body(c):
                for n in range(BLOCKS):
                    dve.wait_ge(multiplied, c * BLOCKS + n + 4)
                    banks = acc[:, n % 2, :, 0:G]
                    if n < UP:
                        h = hidden[:, n % 2]
                        nc.vector.tensor_scalar_max(per_block(h), banks, 0.0).then_inc(taken, 1)
                        dve.wait_ge(taken, c * BLOCKS + n + 3)
                        nc.vector.tensor_tensor(h, h, h, ALU.mult).then_inc(squared, 1)
                        dve.wait_ge(squared, c * UP + n + 1)
                        nc.vector.tensor_copy(hh[:, n], h).then_inc(step, 1)
                        dve.wait_ge(step, c * UP + n + 1)
                        nc.vector.tensor_tensor(hl[:, n], h, hh[:, n].bitcast(F32), ALU.subtract).then_inc(split, 1)
                    else:
                        at = per_block(y[:, n - UP])
                        nc.vector.tensor_tensor(at, banks, at, ALU.add).then_inc(taken, 1)
            chunks(dve, body)
            dve.wait_ge(taken, CHUNKS * BLOCKS + 2)


def trunk(nc, x_prompt, x_sample, cache_a_k, cache_a_v, cache_a_kidx, cache_b_k, cache_b_v, cache_b_logf, w_a_in,
          w_a_o, w_b_kv, b_b_f, w_b_q, w_b_o, w_up, w_down, ln_g, ln_b, y_prompt, y_sample, a_k_prompt, a_v_prompt,
          a_kidx_prompt, b_k_prompt, b_v_prompt, b_logf_prompt, a_k_sample, a_v_sample, a_kidx_sample, b_k_sample,
          b_v_sample, b_logf_sample):
    def scratch(name, shape):
        return nc.dram_tensor(name, shape, F32, kind="Internal").ap()

    fm_a = scratch("fm_a", [17 * P, KEYS])
    fm_kv = scratch("fm_kv", [17 * P, KEYS])
    fm_q = scratch("fm_q", [8 * P, KEYS])
    w_rows = scratch("w_rows", [TOK, IDX_H])
    minus_c = scratch("minus_c", [HEADS, KEYS])
    x_rows = [scratch(f"x_rows{i}", [TOK, D]) for i in range(3)]

    def row_tile(prompt, stream):
        return lambda t: stream if t == ST else prompt[t * P:(t + 1) * P]

    def scratch_tile(x):
        return lambda t: x[t * P:t * P + rows_of(t)]

    flat = lambda x: x.rearrange("s h d -> s (h d)")
    ak_p, av_p, ak_s, av_s = (flat(x[0, 0]) for x in (a_k_prompt, a_v_prompt, a_k_sample, a_v_sample))
    bk_p, bv_p, bk_s, bv_s = (flat(x[0]) for x in (b_k_prompt, b_v_prompt, b_k_sample, b_v_sample))

    def to_rows(prompt, stream, block):
        at = bass.ds(block * P, P)
        return [(prompt[:, at].rearrange("(t p) n -> p t n", p=P), lambda st: st[:, 0:ST]),
                (stream[:, at], lambda st: st[:NEW, ST])]

    def last_a(_):
        k, w = slice(0, IDX_D), slice(IDX_D, IDX_D + IDX_H)
        return [(a_kidx_prompt[0, 0].rearrange("(t p) n -> p t n", p=P), lambda st: st[:, 0:ST, k]),
                (a_kidx_sample[0, 0], lambda st: st[:NEW, ST, k]),
                (w_rows[0:SEQ].rearrange("(t p) n -> p t n", p=P), lambda st: st[:, 0:ST, w]),
                (w_rows[SEQ:TOK], lambda st: st[:NEW, ST, w])]

    x_tile, y_tile = row_tile(x_prompt[0], x_sample[0]), row_tile(y_prompt[0], y_sample[0])
    k_stores = lambda n: to_rows(ak_p, ak_s, n - A_K)
    v_stores = lambda n: to_rows(av_p, av_s, n - A_V)

    def activations(p, grp):
        return p.sb("xh", [P, KT, grp.cols], F32R), p.sb("xl", [P, KT, grp.cols], F32R)

    def output_rows(p, grp):
        rows = p.sb("rows", [P, TT, D])
        y = rows[:].rearrange("p t d -> p (t d)")[:, 0:KT * grp.cols].rearrange("p (k n) -> p k n", k=KT)
        return rows, y

    def after_attention(layer, name, grp, rows, y, w_o, before, between, after, beside=None):
        with Phase(nc, f"{name}_x") as p:
            xh, xl = activations(p, grp)
            ring = Ring(nc, p)
            refill(nc, f"{name}_turn", ident, grp, xh, xl, "sbuf", y=rows, ahead=(ring, w_o))
            project(nc, f"{name}_out", grp, ring, xh, xl, w_o, y=y)
            refill(nc, f"{name}_norm", ident, grp, xh, xl, "norm", residual=before, y=y, gain=ln_g[layer, 0],
                   shift=ln_b[layer, 0], keep=between, ahead=(ring, w_up[layer]))
            mlp(nc, f"{name}_mlp", grp, ring, xh, xl, y, w_up[layer], w_down[layer], beside=beside)
            refill(nc, f"{name}_norm2", ident, grp, xh, xl, "norm", residual=between, y=y, gain=ln_g[layer, 1],
                   shift=ln_b[layer, 1], keep=after, last=True)

    with Phase(nc, "all") as ph:
        ident = ph.sb("ident", [P, P])
        ctok = ph.sb("ctok", [P, TT, HEADS])
        make_identity(nc, ident)
        caches = TurnedCaches(nc, ident, [(cache_a_k[0, 0], fm_a, A_K * P),
                                          (cache_a_kidx[0, 0:1].rearrange("a s d -> s a d"), fm_a, A_KI * P),
                                          (cache_b_k[0], fm_kv, 0)])
        with Phase(nc, "a") as keep:
            bias = [keep.sb(f"bias{t}", [P, width_of(t)])[:] for t in range(TT)]
            indexer = Indexer(nc, keep, bias)
            with Phase(nc, "a_in") as p:
                xh, xl = activations(p, EVERY)
                with Phase(nc, "first") as q:
                    ring = Ring(nc, q)
                    refill(nc, "turn_x", ident, EVERY, xh, xl, "rows", residual=x_tile,
                           ahead=(ring, w_a_in[0], A_QI), along=caches)
                    project(nc, "a_index", EVERY, ring, xh, xl, w_a_in[0], ident, first=A_QI, blocks=5, last_cols=72,
                            fm=fm_a, turns=[(4, 1, last_a)])
                clear_semaphores(nc)
                ring = Ring(nc, p)
                indexer.prepare(p, fm_a, w_rows, ring, w_a_in[0])
                indexer.mix_into(p)
                project(nc, "a_qkv", EVERY, ring, xh, xl, w_a_in[0], ident, blocks=A_QI, fm=fm_a,
                        turns=[(A_K, 2, k_stores), (A_V, 2, v_stores)], beside=indexer)

            def layer_a(name, grp, beside=None):
                with Phase(nc, f"{name}_o") as p:
                    rows, y = output_rows(p, grp)
                    attend(nc, f"{name}_heads", ident, grp, rows, fm_a, A_Q * P, fm_a[A_K * P:(A_K + N_KV) * P],
                           av_p, flat(cache_a_v[0, 0]), av_s, bias=bias)
                    after_attention(0, name, grp, rows, y, w_a_o[0], x_tile, scratch_tile(x_rows[0]),
                                    scratch_tile(x_rows[1]), beside)

            layer_a("early", EARLY, indexer.choose_late)
            clear_semaphores(nc)
            layer_a("late", LATE)
        clear_semaphores(nc)
        with Phase(nc, "b_in") as p:
            xh, xl = activations(p, EVERY)
            ring = Ring(nc, p)
            refill(nc, "b_turn_x", ident, EVERY, xh, xl, "rows", residual=scratch_tile(x_rows[1]),
                   ahead=(ring, w_b_kv))
            project(nc, "b_kv", EVERY, ring, xh, xl, w_b_kv, ident, blocks=17, last_cols=HEADS, fm=fm_kv,
                    turns=[(0, 8, lambda n: to_rows(bk_p, bk_s, n)), (8, 8, lambda n: to_rows(bv_p, bv_s, n - 8))])
            gates = ForgetGates(nc, ident, fm_kv[16 * P:17 * P], b_b_f.rearrange("(h a) -> h a", a=1), cache_b_logf[0],
                                b_logf_prompt[0], b_logf_sample[0], minus_c, ctok)
            project(nc, "b_q", EVERY, ring, xh, xl, w_b_q[0], ident, blocks=8, fm=fm_q, along=gates)
        with Phase(nc, "b_o") as p:
            rows, y = output_rows(p, EVERY)
            attend(nc, "b_heads", ident, EVERY, rows, fm_q, 0, fm_kv, bv_p, flat(cache_b_v[0]), bv_s,
                   minus_c=minus_c, ctok=ctok)
            after_attention(1, "b", EVERY, rows, y, w_b_o[0], scratch_tile(x_rows[1]), scratch_tile(x_rows[2]), y_tile)


_INS = ["x_prompt", "x_sample", "cache_a_k", "cache_a_v", "cache_a_kidx", "cache_b_k", "cache_b_v", "cache_b_logf",
        "w_a_in", "w_a_o", "w_b_kv", "b_b_f", "w_b_q", "w_b_o", "w_up", "w_down", "ln_g", "ln_b"]
_OUTS = [(1, SEQ, D), (1, NEW, D),
         (1, 1, SEQ, N_KV, HD), (1, 1, SEQ, N_KV, HD), (1, 1, SEQ, IDX_D),
         (1, SEQ, HEADS, HD), (1, SEQ, HEADS, HD), (1, SEQ, HEADS),
         (1, 1, NEW, N_KV, HD), (1, 1, NEW, N_KV, HD), (1, 1, NEW, IDX_D),
         (1, NEW, HEADS, HD), (1, NEW, HEADS, HD), (1, NEW, HEADS)]


def kernel(**inputs):
    import concourse.bacc as bacc
    from concourse.bass_utils import run_bass_kernel_spmd

    nc = bacc.Bacc("TRN2", target_bir_lowering=False, num_devices=1)
    arrays, args = {}, []
    for name in _INS:
        a = np.ascontiguousarray(inputs[name])
        arrays[f"in_{name}"] = a
        args.append(nc.dram_tensor(f"in_{name}", a.shape, mybir.dt.from_np(a.dtype), kind="ExternalInput").ap())
    for i, shape in enumerate(_OUTS):
        args.append(nc.dram_tensor(f"out_{i}", shape, F32, kind="ExternalOutput").ap())
    Phase.raised.clear()
    trunk(nc, *args)
    r = run_bass_kernel_spmd(nc, [arrays], core_ids=[0])
    return tuple(r.results[0][f"out_{i}"] for i in range(len(_OUTS)))
```
